# Optimizing a Trainium2 kernel written in Bass

```python
import math
import jax
import jax.numpy as jnp
from jax import lax
import numpy as np

D_MODEL = 1024
BATCH = 1
SEQ = 512
DEPTH = 1

BLOCK = 128
EPS = 1e-6

MLA_HEADS = 8
MLA_NOPE = 64
MLA_ROPE = 32
MLA_V = 64
MLA_KV_RANK = 256
ROPE_THETA = 10000.0

DIL_PATTERNS = ((128, 1), (512, 4), (2048, 16))
N_DIL_GROUPS = 3
DIL_HEADS = 8
DIL_HEAD_DIM = 64

N_EXPERT_GROUPS = 4
EXPERTS_PER_GROUP = 8
N_EXPERTS = N_EXPERT_GROUPS * EXPERTS_PER_GROUP
TOP_K_EXPERT = 2
D_FF_EXPERT = 256

MLA_Q_COLS = MLA_HEADS * (MLA_NOPE + MLA_ROPE)
DIL_COLS = 3 * N_DIL_GROUPS * DIL_HEADS * DIL_HEAD_DIM
GATE_COLS = 2 * D_MODEL
IN_COLS = MLA_Q_COLS + MLA_KV_RANK + MLA_ROPE + DIL_COLS + GATE_COLS


def rms_norm(x, g):
    xf = x.astype(jnp.float32)
    y = xf * lax.rsqrt(jnp.mean(xf * xf, axis=-1, keepdims=True) + EPS)
    return (y * g.astype(jnp.float32)).astype(x.dtype)

def alibi_slopes(n):
    return jnp.exp2(-8.0 * (jnp.arange(n, dtype=jnp.float32) + 1.0) / n)

def rope(t, positions):
    half = t.shape[-1] // 2
    freqs = ROPE_THETA ** (-jnp.arange(half, dtype=jnp.float32) / half)
    ang = positions.astype(jnp.float32)[:, :, None] * freqs
    cos = jnp.cos(ang)[:, :, None, :]
    sin = jnp.sin(ang)[:, :, None, :]
    t1 = t[..., :half].astype(jnp.float32)
    t2 = t[..., half:].astype(jnp.float32)
    return jnp.concatenate([t1 * cos - t2 * sin, t2 * cos + t1 * sin], axis=-1).astype(t.dtype)

def causal_block_attention(q, k, v, scale):
    B, S, H, dq = q.shape
    nb = S // BLOCK
    q_blocks = jnp.moveaxis(q.reshape(B, nb, BLOCK, H, dq), 1, 0)
    kpos = jnp.arange(S)

    def one_block(args):
        qb, bi = args
        s = jnp.einsum('bqhd,bkhd->bhqk', qb, k).astype(jnp.float32) * scale
        qpos = bi * BLOCK + jnp.arange(BLOCK)
        s = jnp.where(kpos[None, :] <= qpos[:, None], s, -jnp.inf)
        p = jax.nn.softmax(s, axis=-1)
        return jnp.einsum('bhqk,bkhd->bqhd', p.astype(v.dtype), v)

    o = lax.map(one_block, (q_blocks, jnp.arange(nb)))
    return jnp.moveaxis(o, 0, 1).reshape(B, S, H, v.shape[-1])

def banded_attention(q, k, v, n_back, stride, slopes, scale):
    assert n_back <= BLOCK
    N, L, H, dh = q.shape
    nb = -(-L // BLOCK)
    Lp = nb * BLOCK
    qb = jnp.pad(q, ((0, 0), (0, Lp - L), (0, 0), (0, 0))).reshape(N, nb, BLOCK, H, dh)

    def key_blocks(t):
        tp = jnp.pad(t, ((0, 0), (BLOCK, Lp - L), (0, 0), (0, 0)))
        prev = tp[:, :Lp].reshape(N, nb, BLOCK, H, dh)
        cur = tp[:, BLOCK:].reshape(N, nb, BLOCK, H, dh)
        return jnp.concatenate([prev, cur], axis=2)

    kb = key_blocks(k)
    vb = key_blocks(v)
    s = jnp.einsum('nbqhd,nbkhd->nbhqk', qb, kb).astype(jnp.float32) * scale
    i = jnp.arange(BLOCK)[:, None]
    j = jnp.arange(2 * BLOCK)[None, :]
    delta = i + BLOCK - j
    kpos = jnp.arange(nb)[:, None, None] * BLOCK - BLOCK + j[None]
    valid = (delta >= 0) & (delta <= n_back) & (kpos >= 0)
    bias = -slopes[:, None, None] * (delta * stride).astype(jnp.float32)
    s = jnp.where(valid[None, :, None], s + bias, -jnp.inf)
    m = jnp.max(s, axis=-1, keepdims=True)
    p = jnp.exp(s - m)
    den = jnp.sum(p, axis=-1, keepdims=True)
    o = jnp.einsum('nbhqk,nbkhd->nbqhd', (p / den).astype(v.dtype), vb)
    o = o.reshape(N, Lp, H, dh)[:, :L]
    lse = jnp.transpose((m + jnp.log(den))[..., 0], (0, 1, 3, 2)).reshape(N, Lp, H)[:, :L]
    return o, lse

def mla_branch(q_cols, ckv, k_rope, positions, norm_ckv, w_ukv, q_norm, k_norm):
    B, S, _ = q_cols.shape
    q = q_cols.reshape(B, S, MLA_HEADS, MLA_NOPE + MLA_ROPE)
    kv = (rms_norm(ckv, norm_ckv) @ w_ukv).reshape(B, S, MLA_HEADS, MLA_NOPE + MLA_V)
    k_nope, v = kv[..., :MLA_NOPE], kv[..., MLA_NOPE:]
    k = jnp.concatenate([k_nope, jnp.broadcast_to(k_rope[:, :, None, :], (B, S, MLA_HEADS, MLA_ROPE))], axis=-1)
    q = rms_norm(q, q_norm)
    k = rms_norm(k, k_norm)
    q = jnp.concatenate([q[..., :MLA_NOPE], rope(q[..., MLA_NOPE:], positions)], axis=-1)
    k = jnp.concatenate([k[..., :MLA_NOPE], rope(k[..., MLA_NOPE:], positions)], axis=-1)
    o = causal_block_attention(q, k, v, (MLA_NOPE + MLA_ROPE) ** -0.5)
    return o.reshape(B, S, MLA_HEADS * MLA_V)

def dilated_branch(qkv_cols, q_norm, k_norm):
    B, S, _ = qkv_cols.shape
    H, dh = DIL_HEADS, DIL_HEAD_DIM
    qkv = qkv_cols.reshape(B, S, 3, N_DIL_GROUPS, H, dh)
    q = rms_norm(qkv[:, :, 0], q_norm[:, None, :])
    k = rms_norm(qkv[:, :, 1], k_norm[:, None, :])
    v = qkv[:, :, 2]
    slopes = alibi_slopes(H)
    outs, lses = [], []
    for g, (window, dil) in enumerate(DIL_PATTERNS):
        L = S // dil
        def fold(t):
            return t[:, :, g].reshape(B, L, dil, H, dh).transpose(0, 2, 1, 3, 4).reshape(B * dil, L, H, dh)
        o, lse = banded_attention(fold(q), fold(k), fold(v), window // dil, dil, slopes, dh ** -0.5)
        outs.append(o.reshape(B, dil, L, H, dh).transpose(0, 2, 1, 3, 4).reshape(B, S, H, dh))
        lses.append(lse.reshape(B, dil, L, H).transpose(0, 2, 1, 3).reshape(B, S, H))
    w = jax.nn.softmax(jnp.stack(lses, axis=0), axis=0)
    o = jnp.sum(w[..., None] * jnp.stack(outs, axis=0).astype(jnp.float32), axis=0)
    return o.astype(qkv_cols.dtype).reshape(B, S, H * dh)

def hier_moe(h, w_rg, b_rg, w_re, b_re, w_gate, w_up, w_down):
    B, S, D = h.shape
    T = B * S
    hf = h.reshape(T, D)
    gp = jax.nn.softmax((hf @ w_rg + b_rg).astype(jnp.float32), axis=-1)
    g_p, g_i = lax.top_k(gp, 1)
    g_p, g_i = g_p[:, 0], g_i[:, 0]
    el = (hf @ w_re + b_re).astype(jnp.float32).reshape(T, N_EXPERT_GROUPS, EXPERTS_PER_GROUP)
    el_sel = el[jnp.arange(T), g_i]
    ep = jax.nn.softmax(el_sel, axis=-1)
    e_p, e_i = lax.top_k(ep, TOP_K_EXPERT)
    e_p = e_p / jnp.sum(e_p, axis=-1, keepdims=True)
    weights = g_p[:, None] * e_p
    expert_idx = g_i[:, None] * EXPERTS_PER_GROUP + e_i
    combine = jnp.sum(jax.nn.one_hot(expert_idx, N_EXPERTS, dtype=jnp.float32) * weights[..., None], axis=1)
    combine = combine.astype(hf.dtype)
    y = jnp.zeros_like(hf)
    for e in range(N_EXPERTS):
        he = jax.nn.silu(hf @ w_gate[e]) * (hf @ w_up[e])
        y = y + combine[:, e:e + 1] * (he @ w_down[e])
    return y.reshape(B, S, D)

def first_inputs(seed: int = 0) -> dict:
    key = jax.random.key(seed)
    ks = jax.random.split(key, 24)

    def nrm(k, shape, fan_in):
        return jax.random.normal(k, shape, jnp.float32) * (fan_in ** -0.5)

    def gain(k, shape):
        return 1.0 + 0.02 * jax.random.normal(k, shape, jnp.float32)

    def bias(k, shape, scale):
        return scale * jax.random.normal(k, shape, jnp.float32)

    Ld = DEPTH
    return {
        'x': jax.random.normal(ks[0], (BATCH, SEQ, D_MODEL), jnp.float32),
        'positions': jnp.broadcast_to(jnp.arange(SEQ, dtype=jnp.int32), (BATCH, SEQ)),
        'norm_attn': gain(ks[1], (Ld, D_MODEL)),
        'w_in': nrm(ks[2], (Ld, D_MODEL, IN_COLS), D_MODEL),
        'b_gate': bias(ks[3], (Ld, 2, D_MODEL), 0.02),
        'norm_ckv': gain(ks[4], (Ld, MLA_KV_RANK)),
        'w_ukv': nrm(ks[5], (Ld, MLA_KV_RANK, MLA_HEADS * (MLA_NOPE + MLA_V)), MLA_KV_RANK),
        'q_norm_mla': gain(ks[6], (Ld, MLA_NOPE + MLA_ROPE)),
        'k_norm_mla': gain(ks[7], (Ld, MLA_NOPE + MLA_ROPE)),
        'q_norm_dil': gain(ks[8], (Ld, N_DIL_GROUPS, DIL_HEAD_DIM)),
        'k_norm_dil': gain(ks[9], (Ld, N_DIL_GROUPS, DIL_HEAD_DIM)),
        'w_o_mla': nrm(ks[10], (Ld, MLA_HEADS * MLA_V, D_MODEL), MLA_HEADS * MLA_V),
        'w_o_dil': nrm(ks[11], (Ld, DIL_HEADS * DIL_HEAD_DIM, D_MODEL), DIL_HEADS * DIL_HEAD_DIM),
        'w_out': nrm(ks[12], (Ld, D_MODEL, D_MODEL), D_MODEL),
        'norm_ffn': gain(ks[13], (Ld, D_MODEL)),
        'w_router_group': nrm(ks[14], (Ld, D_MODEL, N_EXPERT_GROUPS), D_MODEL),
        'b_router_group': bias(ks[15], (Ld, N_EXPERT_GROUPS), 0.01),
        'w_router_expert': nrm(ks[16], (Ld, D_MODEL, N_EXPERTS), D_MODEL),
        'b_router_expert': bias(ks[17], (Ld, N_EXPERTS), 0.01),
        'w_gate': nrm(ks[18], (Ld, N_EXPERTS, D_MODEL, D_FF_EXPERT), D_MODEL),
        'w_up': nrm(ks[19], (Ld, N_EXPERTS, D_MODEL, D_FF_EXPERT), D_MODEL),
        'w_down': nrm(ks[20], (Ld, N_EXPERTS, D_FF_EXPERT, D_MODEL), D_FF_EXPERT),
    }

def first_block(x, positions, norm_attn, w_in, b_gate, norm_ckv, w_ukv, q_norm_mla, k_norm_mla,
              q_norm_dil, k_norm_dil, w_o_mla, w_o_dil, w_out, norm_ffn, w_router_group,
              b_router_group, w_router_expert, b_router_expert, w_gate, w_up, w_down):
    B, S, D = x.shape
    splits = [MLA_Q_COLS, MLA_Q_COLS + MLA_KV_RANK, MLA_Q_COLS + MLA_KV_RANK + MLA_ROPE,
              MLA_Q_COLS + MLA_KV_RANK + MLA_ROPE + DIL_COLS]
    for l in range(DEPTH):
        h = rms_norm(x, norm_attn[l])
        proj = h @ w_in[l]
        q_mla, ckv, k_rope, qkv_dil, gate_pre = jnp.split(proj, splits, axis=-1)
        o_mla = mla_branch(q_mla, ckv, k_rope, positions, norm_ckv[l], w_ukv[l],
                           q_norm_mla[l], k_norm_mla[l])
        o_dil = dilated_branch(qkv_dil, q_norm_dil[l], k_norm_dil[l])
        gates = jax.nn.sigmoid(gate_pre.reshape(B, S, 2, D) + b_gate[l])
        merged = gates[:, :, 0] * (o_mla @ w_o_mla[l]) + gates[:, :, 1] * (o_dil @ w_o_dil[l])
        x = x + merged @ w_out[l]
        h2 = rms_norm(x, norm_ffn[l])
        x = x + hier_moe(h2, w_router_group[l], b_router_group[l], w_router_expert[l],
                         b_router_expert[l], w_gate[l], w_up[l], w_down[l])
    return x


DEPTH_2 = 2

HEAD_DIM = 64
MOBA_HEADS = 8
SB_HEADS = 8
MOBA_WIDTH = MOBA_HEADS * HEAD_DIM
SB_WIDTH = SB_HEADS * HEAD_DIM
ATTN_IN = 3 * (MOBA_WIDTH + SB_WIDTH)
ATTN_OUT = MOBA_WIDTH + SB_WIDTH
MOBA_BLOCK = 256
MOBA_TOPK = 3
MOBA_Q_CHUNK = 32
SB_Q_BLOCK = 128
ROPE_THETA_2 = 500000.0
ROPE_DIMS = HEAD_DIM // 4
GDN_HEADS = 8
GDN_HEAD_DIM = 128
GDN_WIDTH = GDN_HEADS * GDN_HEAD_DIM
GDN_IN = 4 * GDN_WIDTH + 2 * GDN_HEADS
GDN_CONV = 4
GDN_CHUNK = 64
FFN_HIDDEN = -(-8 * D_MODEL // (3 * 256)) * 256
N_EVEN = (DEPTH_2 + 1) // 2
N_ODD = DEPTH_2 // 2


def rmsnorm(x, g):
    xf = x.astype(jnp.float32)
    y = xf * lax.rsqrt(jnp.mean(xf * xf, axis=-1, keepdims=True) + EPS)
    return (y * g.astype(jnp.float32)).astype(x.dtype)

def l2norm(x):
    xf = x.astype(jnp.float32)
    return xf * lax.rsqrt(jnp.sum(xf * xf, axis=-1, keepdims=True) + EPS)

def partial_rope(x, positions):
    half = ROPE_DIMS // 2
    inv_freq = ROPE_THETA_2 ** (-jnp.arange(half, dtype=jnp.float32) * 2.0 / ROPE_DIMS)
    ang = positions.astype(jnp.float32)[:, :, None] * inv_freq
    cos = jnp.cos(ang)[:, :, None, :].astype(x.dtype)
    sin = jnp.sin(ang)[:, :, None, :].astype(x.dtype)
    x1 = x[..., :half]
    x2 = x[..., half:ROPE_DIMS]
    return jnp.concatenate([x1 * cos - x2 * sin, x2 * cos + x1 * sin, x[..., ROPE_DIMS:]], axis=-1)

def moba_attention(q, k, v):
    B, H, T, dh = q.shape
    scale = dh ** -0.5
    n_blk = -(-T // MOBA_BLOCK)
    pad = n_blk * MOBA_BLOCK - T
    kp = jnp.pad(k, ((0, 0), (0, 0), (0, pad), (0, 0)))
    vp = jnp.pad(v, ((0, 0), (0, 0), (0, pad), (0, 0)))
    k_blocks = kp.reshape(B, H, n_blk, MOBA_BLOCK, dh)
    v_blocks = vp.reshape(B, H, n_blk, MOBA_BLOCK, dh)
    k_mean = jnp.mean(k_blocks.astype(jnp.float32), axis=3)
    q_blk = jnp.arange(T) // MOBA_BLOCK
    past = jnp.arange(n_blk)[None, :] < q_blk[:, None]
    gate = jnp.einsum('bhtd,bhnd->bhtn', q.astype(jnp.float32), k_mean)
    gate = jnp.where(past, gate, -jnp.inf)
    n_sel = min(MOBA_TOPK, max(n_blk - 1, 1))
    _, sel = lax.top_k(gate, n_sel)
    sel_valid = sel < q_blk[:, None]

    n_qc = T // MOBA_Q_CHUNK
    def to_chunks(t):
        return jnp.moveaxis(t.reshape((B, H, n_qc, MOBA_Q_CHUNK) + t.shape[3:]), 2, 0)
    b_idx = jnp.arange(B)[:, None, None, None]
    h_idx = jnp.arange(H)[None, :, None, None]
    q_offs = jnp.arange(MOBA_Q_CHUNK)
    k_offs = jnp.arange(MOBA_BLOCK)

    def chunk(args):
        ci, q_c, sel_c, valid_c = args
        t0 = ci * MOBA_Q_CHUNK
        k_sel = k_blocks[b_idx, h_idx, sel_c]
        v_sel = v_blocks[b_idx, h_idx, sel_c]
        s_sel = jnp.einsum('bhqd,bhqnkd->bhqnk', q_c, k_sel).astype(jnp.float32) * scale
        s_sel = jnp.where(valid_c[..., None], s_sel, -jnp.inf)
        s_sel = s_sel.reshape(B, H, MOBA_Q_CHUNK, n_sel * MOBA_BLOCK)
        blk_start = (t0 // MOBA_BLOCK) * MOBA_BLOCK
        k_own = lax.dynamic_slice_in_dim(kp, blk_start, MOBA_BLOCK, axis=2)
        v_own = lax.dynamic_slice_in_dim(vp, blk_start, MOBA_BLOCK, axis=2)
        s_own = jnp.einsum('bhqd,bhkd->bhqk', q_c, k_own).astype(jnp.float32) * scale
        causal = (blk_start + k_offs)[None, :] <= (t0 + q_offs)[:, None]
        s_own = jnp.where(causal, s_own, -jnp.inf)
        p = jax.nn.softmax(jnp.concatenate([s_sel, s_own], axis=-1), axis=-1).astype(v.dtype)
        p_sel = p[..., :n_sel * MOBA_BLOCK].reshape(B, H, MOBA_Q_CHUNK, n_sel, MOBA_BLOCK)
        p_own = p[..., n_sel * MOBA_BLOCK:]
        return (jnp.einsum('bhqnk,bhqnkd->bhqd', p_sel, v_sel)
                + jnp.einsum('bhqk,bhkd->bhqd', p_own, v_own))

    out = lax.map(chunk, (jnp.arange(n_qc), to_chunks(q), to_chunks(sel), to_chunks(sel_valid)))
    return jnp.moveaxis(out, 0, 2).reshape(B, H, T, dh)

def stick_breaking_attention(q, k, v):
    B, H, T, dh = q.shape
    scale = dh ** -0.5
    outs = []
    for t0 in range(0, T, SB_Q_BLOCK):
        t1 = t0 + SB_Q_BLOCK
        z = jnp.einsum('bhqd,bhkd->bhqk', q[:, :, t0:t1], k[:, :, :t1]).astype(jnp.float32) * scale
        causal = jnp.arange(t1)[None, :] < jnp.arange(t0, t1)[:, None]
        log_1m = jnp.where(causal, jax.nn.log_sigmoid(-z), 0.0)
        log_after = lax.cumsum(log_1m, axis=3, reverse=True) - log_1m
        w = jnp.where(causal, jnp.exp(jax.nn.log_sigmoid(z) + log_after), 0.0)
        outs.append(jnp.einsum('bhqk,bhkd->bhqd', w.astype(v.dtype), v[:, :, :t1]))
    return jnp.concatenate(outs, axis=2)

def attention_head_groups(h, positions, w_in, w_out):
    B, T, _ = h.shape
    proj = h @ w_in
    cuts = [MOBA_WIDTH, 2 * MOBA_WIDTH, 3 * MOBA_WIDTH,
            3 * MOBA_WIDTH + SB_WIDTH, 3 * MOBA_WIDTH + 2 * SB_WIDTH]
    qa, ka, va, qb, kb, vb = (t.reshape(B, T, -1, HEAD_DIM) for t in jnp.split(proj, cuts, axis=-1))
    qa = partial_rope(qa, positions)
    ka = partial_rope(ka, positions)
    def bhtd(t):
        return t.transpose(0, 2, 1, 3)
    oa = moba_attention(bhtd(qa), bhtd(ka), bhtd(va))
    ob = stick_breaking_attention(bhtd(qb), bhtd(kb), bhtd(vb))
    o = jnp.concatenate([oa, ob], axis=1).transpose(0, 2, 1, 3).reshape(B, T, ATTN_OUT)
    return o @ w_out

def causal_depthwise_conv(x, w):
    ch = x.shape[-1]
    return lax.conv_general_dilated(
        x, w[:, None, :].astype(x.dtype), window_strides=(1,), padding=[(GDN_CONV - 1, 0)],
        dimension_numbers=('NWC', 'WIO', 'NWC'), feature_group_count=ch)

def chunk_gated_delta_rule(q, k, v, g, beta):
    B, T, H, dk = q.shape
    dv = v.shape[-1]
    C = GDN_CHUNK
    N = T // C
    def chunks(t):
        t = t.astype(jnp.float32).reshape((B, N, C, H) + t.shape[3:])
        return t.transpose((0, 3, 1, 2) + tuple(range(4, t.ndim)))
    q, k, v, g, beta = (chunks(t) for t in (q, k, v, g, beta))
    g = jnp.cumsum(g, axis=-1)
    idx = jnp.arange(C)
    incl = idx[:, None] >= idx[None, :]
    strict = idx[:, None] > idx[None, :]
    decay = jnp.exp(jnp.where(incl, g[..., :, None] - g[..., None, :], -jnp.inf))
    k_beta = k * beta[..., None]
    lower = jnp.where(strict, jnp.einsum('bhncd,bhnsd->bhncs', k_beta, k) * decay, 0.0)
    eye = jnp.eye(C, dtype=jnp.float32)
    rhs = jnp.concatenate([v * beta[..., None], k_beta * jnp.exp(g)[..., None]], axis=-1)
    sol = lax.linalg.triangular_solve(lower + eye, rhs, left_side=True, lower=True, unit_diagonal=True)
    u, w = sol[..., :dv], sol[..., dv:]
    attn = jnp.einsum('bhncd,bhnsd->bhncs', q, k) * decay

    def step(state, xs):
        q_c, k_c, u_c, w_c, g_c, a_c = xs
        v_new = u_c - jnp.einsum('bhcd,bhde->bhce', w_c, state)
        o = (jnp.einsum('bhcd,bhde->bhce', q_c * jnp.exp(g_c)[..., None], state)
             + jnp.einsum('bhcs,bhse->bhce', a_c, v_new))
        g_last = g_c[..., -1]
        k_dec = k_c * jnp.exp(g_last[..., None] - g_c)[..., None]
        state = state * jnp.exp(g_last)[..., None, None] + jnp.einsum('bhcd,bhce->bhde', k_dec, v_new)
        return state, o

    xs = tuple(jnp.moveaxis(t, 2, 0) for t in (q, k, u, w, g, attn))
    state0 = jnp.zeros((B, H, dk, dv), jnp.float32)
    _, o = lax.scan(step, state0, xs)
    return o.transpose(1, 0, 3, 2, 4).reshape(B, T, H, dv)

def gated_deltanet(h, w_in, conv_w, a_log, dt_bias, norm_g, w_out):
    B, T, _ = h.shape
    proj = h @ w_in
    qkv = jax.nn.silu(causal_depthwise_conv(proj[..., :3 * GDN_WIDTH], conv_w))
    z = proj[..., 3 * GDN_WIDTH:4 * GDN_WIDTH].reshape(B, T, GDN_HEADS, GDN_HEAD_DIM)
    a = proj[..., 4 * GDN_WIDTH:4 * GDN_WIDTH + GDN_HEADS].astype(jnp.float32)
    b = proj[..., 4 * GDN_WIDTH + GDN_HEADS:].astype(jnp.float32)
    q, k, v = (t.reshape(B, T, GDN_HEADS, GDN_HEAD_DIM) for t in jnp.split(qkv, 3, axis=-1))
    q = l2norm(q) * GDN_HEAD_DIM ** -0.5
    k = l2norm(k)
    beta = jax.nn.sigmoid(b)
    g = -jnp.exp(a_log.astype(jnp.float32)) * jax.nn.softplus(a + dt_bias.astype(jnp.float32))
    o = chunk_gated_delta_rule(q, k, v, g, beta)
    o = rmsnorm(o, norm_g) * jax.nn.silu(z.astype(jnp.float32))
    return o.reshape(B, T, GDN_WIDTH).astype(h.dtype) @ w_out

def swiglu(h, w_in, w_out):
    gate, up = jnp.split(h @ w_in, 2, axis=-1)
    return (jax.nn.silu(gate) * up) @ w_out

def second_inputs(seed: int = 0) -> dict:
    key = jax.random.key(seed)
    ks = jax.random.split(key, 18)
    f32 = jnp.float32
    def dense(k, shape, fan_in, s=1.0):
        return jax.random.normal(k, shape, f32) * (s * fan_in ** -0.5)
    def gain(k, shape):
        return 1.0 + 0.05 * jax.random.normal(k, shape, f32)
    x = jax.random.normal(ks[0], (BATCH, SEQ, D_MODEL), f32)
    c = jax.random.normal(ks[1], (BATCH, D_MODEL), f32)
    offset = jax.random.randint(ks[2], (BATCH, 1), 0, 1024, dtype=jnp.int32)
    positions = offset + jnp.arange(SEQ, dtype=jnp.int32)[None, :]
    ada_w = dense(ks[3], (DEPTH_2, D_MODEL, 6 * D_MODEL), D_MODEL, 0.5)
    ada_b = 0.02 * jax.random.normal(ks[4], (DEPTH_2, 6 * D_MODEL), f32)
    norm_mix_g = gain(ks[5], (DEPTH_2, D_MODEL))
    norm_ffn_g = gain(ks[6], (DEPTH_2, D_MODEL))
    attn_w_in = dense(ks[7], (N_EVEN, D_MODEL, ATTN_IN), D_MODEL)
    attn_w_out = dense(ks[8], (N_EVEN, ATTN_OUT, D_MODEL), ATTN_OUT)
    gdn_w_in = dense(ks[9], (N_ODD, D_MODEL, GDN_IN), D_MODEL)
    gdn_conv_w = dense(ks[10], (N_ODD, GDN_CONV, 3 * GDN_WIDTH), GDN_CONV)
    gdn_a_log = jnp.log(jax.random.uniform(ks[11], (N_ODD, GDN_HEADS), f32, 1.0, 16.0))
    dt = jnp.exp(jax.random.uniform(ks[12], (N_ODD, GDN_HEADS), f32, math.log(1e-3), math.log(1e-1)))
    gdn_dt_bias = dt + jnp.log(-jnp.expm1(-dt))
    gdn_norm_g = gain(ks[13], (N_ODD, GDN_HEAD_DIM))
    gdn_w_out = dense(ks[14], (N_ODD, GDN_WIDTH, D_MODEL), GDN_WIDTH)
    ffn_w_in = dense(ks[15], (DEPTH_2, D_MODEL, 2 * FFN_HIDDEN), D_MODEL)
    ffn_w_out = dense(ks[16], (DEPTH_2, FFN_HIDDEN, D_MODEL), FFN_HIDDEN)
    final_norm_g = gain(ks[17], (D_MODEL,))
    return {'x': x, 'c': c, 'positions': positions, 'ada_w': ada_w, 'ada_b': ada_b,
            'norm_mix_g': norm_mix_g, 'norm_ffn_g': norm_ffn_g,
            'attn_w_in': attn_w_in, 'attn_w_out': attn_w_out,
            'gdn_w_in': gdn_w_in, 'gdn_conv_w': gdn_conv_w, 'gdn_a_log': gdn_a_log,
            'gdn_dt_bias': gdn_dt_bias, 'gdn_norm_g': gdn_norm_g, 'gdn_w_out': gdn_w_out,
            'ffn_w_in': ffn_w_in, 'ffn_w_out': ffn_w_out, 'final_norm_g': final_norm_g}

def second_block(x, c, positions, ada_w, ada_b, norm_mix_g, norm_ffn_g, attn_w_in, attn_w_out,
              gdn_w_in, gdn_conv_w, gdn_a_log, gdn_dt_bias, gdn_norm_g, gdn_w_out,
              ffn_w_in, ffn_w_out, final_norm_g):
    cond = jax.nn.silu(c)
    for layer in range(DEPTH_2):
        mod = (cond @ ada_w[layer] + ada_b[layer])[:, None, :]
        shift_m, scale_m, gate_m, shift_f, scale_f, gate_f = jnp.split(mod, 6, axis=-1)
        h = rmsnorm(x, norm_mix_g[layer]) * (1.0 + scale_m) + shift_m
        i = layer // 2
        if layer % 2 == 0:
            mixed = attention_head_groups(h, positions, attn_w_in[i], attn_w_out[i])
        else:
            mixed = gated_deltanet(h, gdn_w_in[i], gdn_conv_w[i], gdn_a_log[i], gdn_dt_bias[i],
                                   gdn_norm_g[i], gdn_w_out[i])
        x = x + gate_m * mixed
        h = rmsnorm(x, norm_ffn_g[layer]) * (1.0 + scale_f) + shift_f
        x = x + gate_f * swiglu(h, ffn_w_in[layer], ffn_w_out[layer])
    return rmsnorm(x, final_norm_g)


def setup_inputs(seed=0):
    out = dict(first_inputs(seed))
    for name, value in second_inputs(seed + 1).items():
        if name != "x":
            out[name + "_2"] = value
    return out


def reference(
    x, positions, norm_attn, w_in, b_gate, norm_ckv, w_ukv, q_norm_mla, k_norm_mla, q_norm_dil,
    k_norm_dil, w_o_mla, w_o_dil, w_out, norm_ffn, w_router_group, b_router_group,
    w_router_expert, b_router_expert, w_gate, w_up, w_down, c_2, positions_2, ada_w_2, ada_b_2,
    norm_mix_g_2, norm_ffn_g_2, attn_w_in_2, attn_w_out_2, gdn_w_in_2, gdn_conv_w_2,
    gdn_a_log_2, gdn_dt_bias_2, gdn_norm_g_2, gdn_w_out_2, ffn_w_in_2, ffn_w_out_2,
    final_norm_g_2,
):
    x = first_block(
        x, positions, norm_attn, w_in, b_gate, norm_ckv, w_ukv, q_norm_mla, k_norm_mla,
        q_norm_dil, k_norm_dil, w_o_mla, w_o_dil, w_out, norm_ffn, w_router_group,
        b_router_group, w_router_expert, b_router_expert, w_gate, w_up, w_down,
    )
    return second_block(
        x, c_2, positions_2, ada_w_2, ada_b_2, norm_mix_g_2, norm_ffn_g_2, attn_w_in_2,
        attn_w_out_2, gdn_w_in_2, gdn_conv_w_2, gdn_a_log_2, gdn_dt_bias_2, gdn_norm_g_2,
        gdn_w_out_2, ffn_w_in_2, ffn_w_out_2, final_norm_g_2,
    )


_drawn_inputs = setup_inputs


def setup_inputs(seed=0):
    import zlib

    import numpy as np

    out = dict(_drawn_inputs(seed))
    spreads = {}
    factors = {'norm_attn': 4.388,
     'b_gate': 8.0,
     'norm_ckv': 5.895,
     'q_norm_mla': 8.0,
     'k_norm_mla': 8.0,
     'q_norm_dil': 8.0,
     'k_norm_dil': 5.146,
     'b_router_group': 59.16,
     'b_router_expert': 21.522,
     'norm_mix_g_2': 3.19,
     'norm_ffn_g_2': 13.592,
     'gdn_norm_g_2': 26.694,
     'norm_ffn': 5.57}
    for name, (base, spread) in spreads.items():
        noise = np.random.default_rng([zlib.crc32(name.encode()), seed]).standard_normal(out[name].shape)
        drawn = base * np.exp(spread * noise) if base else spread * noise
        out[name] = jnp.asarray(drawn.astype(out[name].dtype))
    for name, factor in factors.items():
        out[name] = (out[name] * factor).astype(out[name].dtype)
    return out
```

```python
from contextlib import ExitStack

import numpy as np
import concourse.bass as bass
from concourse import mybir

F32 = mybir.dt.float32
I32 = mybir.dt.int32
U32 = mybir.dt.uint32
ALU = mybir.AluOpType
ACT = mybir.ActivationFunctionType
AX = mybir.AxisListType

P = 128
S = 512
NT = S // P
D = 1024
KD = D // P
EPS = 1e-6
NEG = -1e30

MLA_H, NOPE, ROPE, MLA_V, KV_RANK = 8, 64, 32, 64, 256
MLA_D = NOPE + ROPE
GROUPS, DIL_H, HD = 3, 8, 64
DIL = (1, 4, 16)
STRIDE = S // P
N_GRP, PER_GRP = 4, 8
NE = N_GRP * PER_GRP
FF = 256
NBLK = 2 * S // P + NE - 1
H = 8
ROPE2 = HD // 4
GD = 128
CONV = 4
CHUNK = 64
LEVELS = 6
HID = -(-8 * D // (3 * 256)) * 256
KH = HID // P

C_MLAQ = 0
C_CKV = MLA_H * MLA_D
C_DIL = C_CKV + KV_RANK + ROPE
C_GATE = C_DIL + 3 * GROUPS * DIL_H * HD


def constants():
    r = np.arange(P)
    part, col = r[:, None], r[None, :]
    chunk = part // CHUNK == col // CHUNK
    strip = np.zeros((P, 31), np.float32)
    strip[:, 15] = 1
    i, j = r[:, None], np.arange(2 * P)[None, :]
    delta = i + P - j
    far = -NEG
    dist0 = np.where((delta >= 0) & (delta <= P), delta, far)
    dist1 = np.where(col <= part, (part - col) * DIL[1], far)
    same = (part - col) % (DIL[2] // STRIDE) == 0
    dist2 = np.where(same & (col <= part), (part - col) * STRIDE, far)
    slopes = 2.0 ** (-8.0 * (np.arange(DIL_H) + 1.0) / DIL_H)
    levels = [((col >> l) % 2 == 1) & ((part >> l) % 2 == 0) & (col >> (l + 1) == part >> (l + 1))
              for l in range(LEVELS)]
    half, half2 = ROPE // 2, ROPE2 // 2
    f1 = np.float32(10000.0) ** (-np.arange(half, dtype=np.float32) / np.float32(half))
    f2 = np.float32(500000.0) ** (-np.arange(half2, dtype=np.float32) * np.float32(2.0) / np.float32(ROPE2))
    parts = {
        "ident": np.eye(P), "ones": np.ones((P, P)),
        "before": part < col,
        "chunk_upto": chunk & (part <= col),
        "chunk_all": chunk,
        "neg_from": -(part >= col).astype(np.float32),
        "neg_ones": -np.ones((P, P)),
        "sb_keep": part < col,
        "sb_mask": np.where(part < col, 0.0, NEG),
        "causal": np.where(col <= part, 0.0, NEG),
        "levels": np.concatenate(levels, 1),
        "strip": strip,
        "freq1": np.tile(f1, (P, 1)), "freq2": np.tile(f2, (P, 1)),
        "expert": np.tile(np.arange(NE), (P, 1)), "group": np.tile(np.arange(8), (P, 1)),
        "block": np.tile(np.arange(NBLK), (P, 1)),
        "thresholds": np.tile(P * np.arange(NT), (P, 1)),
        "token": r[:, None] + P * np.arange(NT)[None, :],
        "dist0": dist0, "dist1": dist1, "dist2": dist2,
        "slope": np.concatenate([-s * np.eye(P) for s in slopes], 1),
    }
    at, n, out = {}, 0, []
    for name, a in parts.items():
        a = np.asarray(a, np.float32)
        at[name] = (n, a.shape[1])
        n += a.shape[1]
        out.append(a)
    return np.ascontiguousarray(np.concatenate(out, 1)), at


class Queue:

    def __init__(self, engine, sem):
        self.engine, self.sem, self.count, self.waited = engine, sem, 0, {}

    def after(self, *marks):
        for sem, value in marks:
            if self.waited.get(sem.name, 0) < value:
                self.engine.wait_ge(sem, value)
                self.waited[sem.name] = value
        return self

    def run(self, instruction):
        instruction.then_inc(self.sem, 1)
        self.count += 1
        return self.sem, self.count

    def last(self):
        return (self.sem, self.count) if self.count else None


class Slot:

    def __init__(self, buf):
        self.buf, self.free = buf, []


class Ring:

    def __init__(self, bufs):
        self.slots = [Slot(b) for b in bufs]

    def take(self):
        return self.slots.pop(0)

    def give(self, slot, *marks):
        slot.free = list(marks)
        self.slots.append(slot)


class Loads:

    def __init__(self, queue, bufs, sems):
        self.queue = queue
        self.ring = Ring(bufs)
        self.sems = dict(zip([id(s) for s in self.ring.slots], sems))
        self.counts = {id(s): 0 for s in self.ring.slots}

    def load(self, view, source, *marks):
        slot = self.ring.take()
        self.queue.after(*slot.free, *marks)
        self.queue.engine.dma_start(view(slot.buf), source).then_inc(self.sems[id(slot)], 16)
        self.counts[id(slot)] += 16
        slot.ready = (self.sems[id(slot)], self.counts[id(slot)])
        return slot

    def give(self, slot, *marks):
        self.ring.give(slot, *marks)


def pipelined(jobs, depth):
    jobs, live = iter(jobs), []
    more = True
    while more or live:
        if more and len(live) < depth:
            job = next(jobs, None)
            more = job is not None
            if more:
                live.append(job)
        live = [j for j in live if next(j, "done") != "done"]


class Core:

    def __init__(self, nc, ctx, io, at):
        self.nc, self.ctx, self.io, self.at = nc, ctx, io, at
        self.nsem = 0
        self.PE = Queue(nc.tensor, self.sem("pe_done"))
        self.ACT = Queue(nc.scalar, self.sem("act_done"))
        self.DVE = Queue(nc.vector, self.sem("dve_done"))
        self.POOL = Queue(nc.gpsimd, self.sem("pool_done"))
        self.SP = Queue(nc.sync, self.sem("sp_done"))
        self.banks = Ring([ctx.enter_context(nc.psum_tensor(f"bank{i}", [P, 512], F32)) for i in range(8)])
        nw = 8
        self.weights = Loads(self.SP, [self.sb(f"weights{i}", [P, 2048]) for i in range(nw)],
                             [self.sem(f"weights{i}_in") for i in range(nw)])
        self.scratch = Ring([self.sb(f"scratch{i}", [P, 512]) for i in range(13)])
        self.small = Ring([self.sb(f"small{i}", [P, 32]) for i in range(12)])
        self.xT = self.sb("xT", [P, KD, S])
        self.hT = self.sb("hT", [P, KD, S])
        self.arena = self.sb("arena", [P, 24 * S])
        self.mixed = self.sb("mixed", [P, KD, S])
        self.mod = self.sb("mod", [P, 2, 6, KD])
        self.cols = self.sb("cols", [P, 256])
        self.x_ready = [[] for _ in range(KD)]
        self.h_ready = []
        self.h_free = []
        self.stores = []

    def sem(self, name):
        return self.ctx.enter_context(self.nc.semaphore(name))

    def sb(self, name, shape, dt=F32):
        return self.ctx.enter_context(self.nc.sbuf_tensor("sb_" + name, shape, dt))

    def const(self, name, rows=P):
        a, n = self.at[name]
        if a >= self.at["dist0"][0]:
            a -= self.at["dist0"][0]
            return self.mixed[:, 0:3, :].rearrange("p a t -> p (a t)")[0:rows, a:a + n]
        return self.consts[0:rows, a:a + n]

    def barrier(self):
        marks = [q.last() for q in (self.PE, self.ACT, self.DVE, self.POOL) if q.last()]
        for q in (self.PE, self.ACT, self.DVE, self.POOL):
            q.after(*marks)

    def load_once(self, queue, dst, src, name):
        sem = self.sem(name)
        queue.engine.dma_start(dst, src).then_inc(sem, 16)
        return sem, 16

    def weight_chunk(self, w, c0, n, kt=KD, k0=0):
        src = w[k0 * P:(k0 + kt) * P, c0:c0 + n].rearrange("(k p) n -> p k n", p=P)
        slot = self.weights.load(lambda b: b[:, 0:kt * n].rearrange("p (k n) -> p k n", k=kt), src)
        slot.w = slot.buf[:, 0:kt * n].rearrange("p (k n) -> p k n", k=kt)
        return slot

    def feature_product(self, slot, m, actT, kt, marks, bank=None, first=True, last=True):
        nc, PE = self.nc, self.PE
        if bank is None:
            bank = self.banks.take()
            PE.after(*bank.free)
        PE.after(slot.ready, *marks)
        for k in range(kt):
            mm = nc.tensor.matmul(bank.buf[:], slot.w[:, k, m * P:(m + 1) * P], actT[:, k, :],
                                  start=first and k == 0, stop=last and k == kt - 1)
        return bank, PE.run(mm)

    def token_product(self, slot, n, toks, kt, marks, c0=0, bank=None, at=0):
        nc, PE = self.nc, self.PE
        if bank is None:
            bank = self.banks.take()
            PE.after(*bank.free)
        PE.after(slot.ready, *marks)
        for k in range(kt):
            mm = nc.tensor.matmul(bank.buf[:, at:at + n], toks(k), slot.w[:, k, c0:c0 + n],
                                  start=k == 0, stop=k == kt - 1)
        return bank, PE.run(mm)

    def inv_rms_rows(self, squares, n, width):
        nc, PE, A, V = self.nc, self.PE, self.ACT, self.DVE
        bank = self.banks.take()
        PE.after(*bank.free)
        for k in range(n):
            sq, mark = squares(k)
            PE.after(mark)
            mm = PE.run(nc.tensor.matmul(bank.buf[:], self.const("ones"), sq.buf[:],
                                         start=k == 0, stop=k == n - 1))
            self.scratch.give(sq, mm)
        rms = self.scratch.take()
        A.after(mm, *rms.free)
        got = A.run(nc.scalar.activation(rms.buf[:], bank.buf[:], ACT.Sqrt, bias=self.eps[:, 0:1], scale=1.0 / width))
        self.banks.give(bank, got)
        V.after(got)
        return rms, V.run(nc.vector.reciprocal(rms.buf[:], rms.buf[:]))

    def square_tile(self, src, marks):
        sq = self.scratch.take()
        self.ACT.after(*marks, *sq.free)
        return sq, self.ACT.run(self.nc.scalar.activation(sq.buf[:], src, ACT.Square))

    def norm_residual(self, gain, shift=None, out=None):
        nc, V, A = self.nc, self.DVE, self.ACT
        out = self.hT if out is None else out
        inv, ready = self.inv_rms_rows(lambda k: self.square_tile(self.xT[:, k, :], self.x_ready[k]), KD, D)
        V.after(ready, *self.h_free)
        self.h_ready = []
        for k in range(KD):
            done = V.run(nc.vector.scalar_tensor_tensor(out=out[:, k, :], in0=self.xT[:, k, :], scalar=gain(k),
                                                        in1=inv.buf[:], op0=ALU.mult, op1=ALU.mult))
            if shift is not None:
                A.after(done)
                done = A.run(nc.scalar.activation(out[:, k, :], out[:, k, :], ACT.Identity, bias=shift(k)))
            self.h_ready.append(done)
        self.scratch.give(inv, V.last())

    def inv_rms_small(self, sums, width, mark, eps=True):
        nc, A, V = self.nc, self.ACT, self.DVE
        A.after(mark)
        got = A.run(nc.scalar.activation(sums, sums, ACT.Sqrt, bias=self.eps[:, 0:1], scale=1.0 / width))
        V.after(got)
        return V.run(nc.vector.reciprocal(sums, sums))

    def head_norm(self, src, heads, width, out, marks):
        nc, A, V = self.nc, self.ACT, self.DVE
        sq, ss = self.scratch.take(), self.small.take()
        A.after(*marks, *sq.free)
        sq3 = sq.buf[:, 0:heads * width].rearrange("p (h d) -> p h d", h=heads)
        m = A.run(nc.scalar.activation(sq3, src, ACT.Square))
        V.after(m, *ss.free)
        m = V.run(nc.vector.tensor_reduce(ss.buf[:, 0:heads], sq3, AX.X, ALU.add))
        self.scratch.give(sq, m)
        m = self.inv_rms_small(ss.buf[:, 0:heads], width, m)
        V.after(m)
        scale = ss.buf[:, 0:heads].unsqueeze(2).to_broadcast([P, heads, width])
        m = V.run(nc.vector.tensor_tensor(out, src, scale, ALU.mult))
        self.small.give(ss, m)
        return m

    def rope(self, t1, t2, cos, sin, heads, half, marks):
        nc, G = self.nc, self.POOL
        tmp = self.scratch.take()
        n = heads * half
        view = lambda i: tmp.buf[:, i * n:(i + 1) * n].rearrange("p (h d) -> p h d", h=heads)
        cosb = cos.unsqueeze(1).to_broadcast([P, heads, half])
        sinb = sin.unsqueeze(1).to_broadcast([P, heads, half])
        G.after(*marks, *tmp.free)
        for i, (t, f) in enumerate(((t1, cosb), (t2, sinb), (t2, cosb), (t1, sinb))):
            m = G.run(nc.gpsimd.tensor_tensor(view(i), t, f, ALU.mult))
        G.after(m)
        G.run(nc.gpsimd.tensor_tensor(t1, view(0), view(1), ALU.subtract))
        m = G.run(nc.gpsimd.tensor_tensor(t2, view(2), view(3), ALU.add))
        self.scratch.give(tmp, m)
        return m

    def transpose_blocks(self, blocks, rows, marks):
        nc, PE = self.nc, self.PE
        bank = self.banks.take()
        PE.after(*bank.free, *marks)
        for i, b in enumerate(blocks):
            mm = nc.tensor.transpose(bank.buf[0:rows, i * P:(i + 1) * P], b, self.const("ident"))
        return bank, PE.run(mm)

    def copy(self, out, src, marks, on=None):
        self.turn = not self.turn
        if on == "act" or (on is None and self.turn):
            self.ACT.after(*marks)
            return self.ACT.run(self.nc.scalar.copy(out, src))
        self.DVE.after(*marks)
        return self.DVE.run(self.nc.vector.tensor_copy(out, src))

    turn = False

    def add_residual(self, bank, m, j, gate=None):
        nc, V = self.nc, self.DVE
        V.after(m, *self.x_ready[j])
        x = self.xT[:, j, :]
        if gate is None:
            done = V.run(nc.vector.tensor_tensor(x, bank.buf[:], x, ALU.add))
        else:
            done = V.run(nc.vector.scalar_tensor_tensor(out=x, in0=bank.buf[:], scalar=gate, in1=x,
                                                        op0=ALU.mult, op1=ALU.add))
        self.banks.give(bank, done)
        self.x_ready[j] = [done]

    def softmax_item(self, q, k, blocks, bias, scale, values, out, negmax, den, marks, done):
        nc, PE, A, V = self.nc, self.PE, self.ACT, self.DVE
        n = blocks * P
        bank = self.banks.take()
        PE.after(*bank.free, *marks)
        nc.tensor.matmul(bank.buf[:, 0:n], q, k, start=True, stop=False)
        for i, (left, right, c) in enumerate(bias):
            w = right.shape[-1]
            mm = nc.tensor.matmul(bank.buf[:, c:c + w], left, right, start=False, stop=i == len(bias) - 1)
        m = PE.run(mm)
        V.after(m)
        m = V.run(nc.vector.tensor_reduce(negmax, bank.buf[:, 0:n], AX.X, ALU.max, negate=True))
        if scale != 1.0:
            V.after(m)
            m = V.run(nc.vector.tensor_scalar(negmax, negmax, scale, None, ALU.mult))
        p = self.scratch.take()
        A.after(m, *p.free)
        m = A.run(nc.scalar.activation(p.buf[:, 0:n], bank.buf[:, 0:n], ACT.Exp, bias=negmax, scale=scale,
                                       accum_out=den))
        self.banks.give(bank, m)
        yield
        tbank, m = self.transpose_blocks([p.buf[:, b * P:(b + 1) * P] for b in range(blocks)], P, [m])
        self.scratch.give(p, m)
        pT = self.scratch.take()
        m = self.copy(pT.buf[:, 0:n], tbank.buf[:, 0:n], [m, *pT.free])
        self.banks.give(tbank, m)
        yield
        PE.after(m)
        for b in range(blocks):
            mm = nc.tensor.matmul(out, pT.buf[:, b * P:(b + 1) * P], values(b), start=b == 0, stop=b == blocks - 1)
        m = PE.run(mm)
        self.scratch.give(pT, m)
        done(m)

    def angles(self, pos, freq, n, cos, sin):
        nc, V, A = self.nc, self.DVE, self.ACT
        PI = float(np.float32(3.1415925))
        TWO_PI, ROUND = 6.283185307179586, 12582912.0
        parts = [6.28125, 0.0019350051879882812, TWO_PI - 6.28125 - 0.0019350051879882812]
        a, t, r = self.scratch.take(), self.scratch.take(), self.scratch.take()
        V.after(*a.free, *t.free, *r.free)
        w = NT * n
        for i in range(NT):
            m = V.run(nc.vector.tensor_scalar(a.buf[:, i * n:(i + 1) * n], freq, pos[:, i:i + 1], None, ALU.mult))
        for out, turn, add in ((sin, 0.0, 0.0), (cos, 0.25, TWO_PI / 4)):
            V.after(m)
            m = V.run(nc.vector.tensor_scalar(t.buf[:, 0:w], a.buf[:, 0:w], 1 / TWO_PI, turn, ALU.mult, ALU.add))
            V.after(m)
            m = V.run(nc.vector.tensor_scalar(t.buf[:, 0:w], t.buf[:, 0:w], ROUND, None, ALU.add))
            V.after(m)
            m = V.run(nc.vector.tensor_scalar(t.buf[:, 0:w], t.buf[:, 0:w], -ROUND, None, ALU.add))
            src = a
            for c in parts:
                V.after(m)
                m = V.run(nc.vector.scalar_tensor_tensor(out=r.buf[:, 0:w], in0=t.buf[:, 0:w], scalar=-c,
                                                         in1=src.buf[:, 0:w], op0=ALU.mult, op1=ALU.add))
                src = r
            V.after(m)
            m = V.run(nc.vector.tensor_scalar(r.buf[:, 0:w], r.buf[:, 0:w], float(add), PI, ALU.add, ALU.min))
            V.after(m)
            m = V.run(nc.vector.tensor_scalar(r.buf[:, 0:w], r.buf[:, 0:w], -PI, None, ALU.max))
            A.after(m)
            m = A.run(nc.scalar.activation(out.rearrange("p t f -> p (t f)"), r.buf[:, 0:w], ACT.Sin))
        for s in (a, t, r):
            self.scratch.give(s, m)
        return m

    def modulation(self, layer):
        nc, PE, V = self.nc, self.PE, self.DVE
        bank = self.banks.take()
        PE.after(*bank.free, self.cond_ready)
        W, parts = 256, 6 * D // P
        for c in range(6 * D // W):
            slot = self.weight_chunk(self.io["ada_w_2"][layer], c * W, W)
            PE.after(slot.ready)
            for m in range(W // P):
                j = c * (W // P) + m
                for k in range(KD):
                    mm = nc.tensor.matmul(bank.buf[:, j:j + 1], slot.w[:, k, m * P:(m + 1) * P],
                                          self.cond[:, k:k + 1], start=k == 0, stop=k == KD - 1)
            done = PE.run(mm)
            self.weights.give(slot, done)
        V.after(done, self.small_in)
        out = self.mod[:, layer, :, :].rearrange("p s k -> p (s k)")
        m = V.run(nc.vector.tensor_tensor(out, bank.buf[:, 0:parts], self.ada_b[:, layer, :], ALU.add))
        self.banks.give(bank, m)
        for s, g in ((1, self.col["norm_mix"]), (4, self.col["norm_ffn2"])):
            V.after(m)
            gain = g[:, layer * KD:(layer + 1) * KD]
            m = V.run(nc.vector.scalar_tensor_tensor(out=self.mod[:, layer, s, :], in0=self.mod[:, layer, s, :],
                                                     scalar=1.0, in1=gain, op0=ALU.add, op1=ALU.mult))
        self.mod_ready = m


def setup(c):
    nc, io = c.nc, c.io
    ncst = c.at["dist0"][0]
    c.consts = c.sb("consts", [P, ncst])
    c.consts_in = c.load_once(c.SP, c.consts[:], io["consts"][:, 0:ncst], "consts_in")
    c.PE.after(c.load_once(c.SP, c.mixed[:, 0:3, :].rearrange("p a t -> p (a t)"), io["consts"][:, ncst:],
                           "dilated_consts_in"))
    x_in = [c.load_once(c.SP, c.xT[:, k, :], io["xT"][k * P:(k + 1) * P, :], f"x{k}_in") for k in range(KD)]
    c.x_ready = [[m] for m in x_in]
    cols = [("norm_attn", KD), ("norm_ffn", KD), ("b_gate", 2 * KD), ("norm_ckv", KV_RANK // P),
            ("norm_mix", 2 * KD), ("norm_ffn2", 2 * KD), ("final", KD), ("c", KD), ("gdn_norm", 1),
            ("qdil", GROUPS), ("kdil", GROUPS)]
    c.col, n = {}, 0
    sem = c.sem("columns_in")
    count = 0
    for name, w in cols:
        c.col[name] = c.cols[:, n:n + w]
        nc.gpsimd.dma_start(c.cols[:, n:n + w], io["col_" + name]).then_inc(sem, 16)
        n, count = n + w, count + 16
    c.ada_b = c.sb("ada_b", [P, 2, 6 * KD])
    c.conv_w = c.sb("conv_w", [P, CONV, 3 * H])
    c.rows = c.sb("rows", [P, 2 * MLA_D + N_GRP + NE + 2 * H])
    c.row, at = {}, 0
    for name, w in (("qmla", MLA_D), ("kmla", MLA_D), ("b_rg", N_GRP), ("b_re", NE), ("a_log", H), ("dt_bias", H)):
        c.row[name] = c.rows[:, at:at + w]
        nc.gpsimd.dma_start(c.rows[:, at:at + w], io["row_" + name].partition_broadcast(P)).then_inc(sem, 16)
        at, count = at + w, count + 16
    pos = c.sb("pos", [P, 2 * NT], I32)
    for dst, src in ((c.ada_b[:], io["col_ada_b"]), (c.conv_w[:], io["col_conv"]), (pos[:], io["col_pos"])):
        nc.gpsimd.dma_start(dst, src).then_inc(sem, 16)
        count += 16
    c.small_in = (sem, count)
    c.eps = c.sb("eps", [P, 1])
    c.posf = c.sb("posf", [P, 2 * NT])
    c.cos1, c.sin1 = c.sb("cos1", [P, NT, ROPE // 2]), c.sb("sin1", [P, NT, ROPE // 2])
    c.cos2, c.sin2 = c.sb("cos2", [P, NT, ROPE2 // 2]), c.sb("sin2", [P, NT, ROPE2 // 2])
    c.DVE.run(nc.vector.memset(c.eps[:], EPS))
    c.DVE.after(c.small_in)
    m = c.DVE.run(nc.vector.tensor_copy(c.posf[:], pos[:]))
    m = c.DVE.run(nc.vector.tensor_scalar(c.col["qdil"], c.col["qdil"], HD ** -0.5, None, ALU.mult))
    c.PE.after(c.consts_in)
    c.DVE.after(c.consts_in, m)
    c.ACT.after(c.small_in, m)
    c.POOL.after(c.small_in, m, c.consts_in)
    c.cond = c.sb("cond", [P, KD])
    c.cond_ready = c.ACT.run(nc.scalar.activation(c.cond[:], c.col["c"], ACT.Silu))
    c.angles(c.posf[:, 0:NT], c.const("freq1"), ROPE // 2, c.cos1[:], c.sin1[:])
    c.rope_ready = c.angles(c.posf[:, NT:2 * NT], c.const("freq2"), ROPE2 // 2, c.cos2[:], c.sin2[:])


def columns(table, j):
    return table[:, j:j + 1]


def folded(g, i):
    return slice(i * P, (i + 1) * P) if g == 0 else slice(i, S, STRIDE)


def fold(c, g, i):
    return lambda k: c.hT[:, k, folded(g, i)]


def dilated(c):
    nc, PE, A, V, G = c.nc, c.PE, c.ACT, c.DVE, c.POOL
    w_in = c.io["w_in"]
    WD = DIL_H * HD
    q, k, v = (c.arena[:, j * 4 * S:(j + 1) * 4 * S].rearrange("p (a t) -> p a t", a=4) for j in range(3))
    outs = [c.arena[:, (3 + g) * 4 * S:(4 + g) * 4 * S].rearrange("p (a t) -> p a t", a=4) for g in range(GROUPS)]
    negmax, den = c.negmax, c.den
    free = []
    for g in range(GROUPS):
        ready = []
        for part, dst in ((0, q), (1, k), (2, v)):
            for half in range(2):
                heads = DIL_H // 2
                slot = c.weight_chunk(w_in, C_DIL + (part * GROUPS + g) * WD + half * 256, 256)

                def tile(i, slot=slot, half=half, dst=dst, part=part, heads=heads):
                    bank, m = c.token_product(slot, 256, fold(c, g, i), KD, c.h_ready)
                    slot.used = m
                    yield
                    if part == 2:
                        m = c.copy(v[:, i, half * 256:(half + 1) * 256], bank.buf[:, 0:256], [m, *free])
                        c.banks.give(bank, m)
                        ready.append(m)
                        return
                    n = c.scratch.take()
                    V.after(*n.free)
                    src = bank.buf[:, 0:256].rearrange("p (h d) -> p h d", h=heads)
                    m = c.head_norm(src, heads, HD, n.buf[:, 0:256].rearrange("p (h d) -> p h d", h=heads), [m])
                    c.banks.give(bank, m)
                    yield
                    tb, m = c.transpose_blocks([n.buf[:, j * P:(j + 1) * P] for j in range(2)], P, [m])
                    c.scratch.give(n, m)
                    gain = columns(c.col["qdil" if part == 0 else "kdil"], g)
                    A.after(m, *free)
                    m = A.run(nc.scalar.activation(dst[:, 2 * half:2 * half + 2, i * P:(i + 1) * P],
                                                   tb.buf[:, 0:256].rearrange("p (a t) -> p a t", a=2),
                                                   ACT.Identity, scale=gain))
                    c.banks.give(tb, m)
                    ready.append(m)
                pipelined((tile(i) for i in range(NT)), 3)
                c.weights.give(slot, slot.used)

        last = []
        for i in range(NT):
            ob = c.banks.take()
            PE.after(*ob.free)
            lo = i - 1 if g == 0 and i > 0 else i
            blocks = i - lo + 1
            dist = c.const(f"dist{g}")
            moving = dist[:, (2 - blocks) * P:] if g == 0 else dist
            pv = []

            def head(h, i=i, lo=lo, blocks=blocks, moving=moving, ob=ob, pv=pv):
                rows = slice(HD * (h % 2), HD * (h % 2) + HD)
                bias = [(c.const("slope")[:, h * P:(h + 1) * P], moving, 0)]
                return c.softmax_item(
                    q[rows, h // 2, i * P:(i + 1) * P], k[rows, h // 2, lo * P:(i + 1) * P], blocks, bias, 1.0,
                    lambda b: v[:, lo + b, h * HD:(h + 1) * HD], ob.buf[:, h * HD:(h + 1) * HD],
                    negmax[:, g, i, h:h + 1], den[:, g, i, h:h + 1], ready, pv.append)
            pipelined((head(h) for h in range(DIL_H)), 3)
            m = c.copy(outs[g][:, i, :], ob.buf[:], [pv[-1]])
            c.banks.give(ob, m)
            last += [m, pv[-1]]
        free = last
    t8 = c.arena[0:DIL_H, 0:7 * S].rearrange("p (a t) -> p a t", a=7)
    c.barrier()
    for n, src in enumerate((negmax, den)):
        for g in range(GROUPS):
            bank = c.banks.take()
            PE.after(*bank.free)
            for i in range(NT):
                mm = nc.tensor.transpose(bank.buf[0:DIL_H, i * P:(i + 1) * P], src[:, g, i, :], c.const("ident"))
            m = PE.run(mm)
            for i in range(NT):
                V.after(m)
                m = V.run(nc.vector.tensor_copy(t8[:, n * GROUPS + g, folded(g, i)],
                                             bank.buf[0:DIL_H, i * P:(i + 1) * P]))
            c.banks.give(bank, m)
    low = t8[:, 6, :]
    V.after(m)
    m = V.run(nc.vector.tensor_tensor(low, t8[:, 0, :], t8[:, 1, :], ALU.min))
    V.after(m)
    m = V.run(nc.vector.tensor_tensor(low, low, t8[:, 2, :], ALU.min))
    for g in range(GROUPS):
        V.after(m)
        m = V.run(nc.vector.tensor_tensor(t8[:, g, :], low, t8[:, g, :], ALU.subtract))
    A.after(m)
    m = A.run(nc.scalar.activation(t8[:, 0:3, :], t8[:, 0:3, :], ACT.Exp))
    V.after(m)
    m = V.run(nc.vector.tensor_tensor(t8[:, 3:6, :], t8[:, 0:3, :], t8[:, 3:6, :], ALU.mult))
    V.after(m)
    m = V.run(nc.vector.tensor_tensor(low, t8[:, 3, :], t8[:, 4, :], ALU.add))
    V.after(m)
    m = V.run(nc.vector.tensor_tensor(low, low, t8[:, 5, :], ALU.add))
    V.after(m)
    m = V.run(nc.vector.reciprocal(low, low))
    V.after(m)
    m = V.run(nc.vector.tensor_tensor(t8[:, 0:3, :], t8[:, 0:3, :],
                                      low.unsqueeze(1).to_broadcast([DIL_H, 3, S]), ALU.mult))
    bank = c.banks.take()
    PE.after(m, *bank.free)
    for g in range(GROUPS):
        for i in range(NT):
            at = (g * NT + i) * DIL_H
            mm = nc.tensor.matmul(bank.buf[:, at:at + DIL_H], t8[:, g, folded(g, i)], c.const("ident", DIL_H)[:, 0:DIL_H],
                                  start=True, stop=True)
    m = PE.run(mm)
    coef = c.scratch.take()
    ncf = GROUPS * NT * DIL_H
    ready = c.copy(coef.buf[:, 0:ncf], bank.buf[:, 0:ncf], [m, *coef.free], "dve")
    c.banks.give(bank, ready)
    written = {}

    def spread(g, i):
        o3 = outs[g][:, i, :].rearrange("p (h d) -> p h d", h=DIL_H)
        at = (g * NT + i) * DIL_H
        cb = coef.buf[:, at:at + DIL_H].unsqueeze(2).to_broadcast([P, DIL_H, HD])
        V.after(ready)
        m = V.run(nc.vector.tensor_tensor(o3, o3, cb, ALU.mult))
        yield
        tb, m = c.transpose_blocks([outs[g][:, i, j * P:(j + 1) * P] for j in range(4)], P, [m])
        yield
        for j in range(4):
            dst, src = c.mixed[:, 4 + j, folded(g, i)], tb.buf[:, j * P:(j + 1) * P]
            if g == 0:
                V.after(m)
                written[j] = V.run(nc.vector.tensor_copy(dst, src))
            else:
                V.after(m, written[j])
                written[j] = V.run(nc.vector.tensor_tensor(dst, src, dst, ALU.add))
        c.banks.give(tb, written[3])
    pipelined((spread(g, i) for g in range(GROUPS) for i in range(NT)), 3)
    c.scratch.give(coef, *written.values())
    c.barrier()


def mla(c):
    nc, PE, A, V, G = c.nc, c.PE, c.ACT, c.DVE, c.POOL
    w_in, w_ukv = c.io["w_in"], c.io["w_ukv"]
    q, k = (c.arena[:, j * 8 * S:(j + 1) * 8 * S].rearrange("p (a t) -> p a t", a=8) for j in range(2))
    v = c.arena[:, 16 * S:20 * S].rearrange("p (a n) -> p a n", a=NT)
    ckvT = c.arena[:, 20 * S:22 * S].rearrange("p (a t) -> p a t", a=2)
    krope = c.arena[:, 22 * S:22 * S + NT * ROPE].rearrange("p (a n) -> p a n", a=NT)
    ready = []

    def finish_heads(n, heads, h0, i, gain, dst, m):
        n3 = n.buf[:, 0:heads * MLA_D].rearrange("p (h d) -> p h d", h=heads)
        G.after(m)
        m = G.run(nc.gpsimd.tensor_tensor(n3, n3, gain.unsqueeze(1).to_broadcast([P, heads, MLA_D]), ALU.mult))
        half = ROPE // 2
        m = c.rope(n3[:, :, NOPE:NOPE + half], n3[:, :, NOPE + half:], c.cos1[:, i, :], c.sin1[:, i, :],
                   heads, half, [m, c.rope_ready])
        yield
        tb, m = c.transpose_blocks([n.buf[:, j * MLA_D:(j + 1) * MLA_D] for j in range(heads)], MLA_D, [m])
        c.scratch.give(n, m)
        m = c.copy(dst[0:MLA_D, h0:h0 + heads, i * P:(i + 1) * P],
                   tb.buf[0:MLA_D, 0:heads * P].rearrange("p (a t) -> p a t", a=heads), [m])
        c.banks.give(tb, m)
        ready.append(m)

    for part in range(4):
        heads = 2
        w = heads * MLA_D
        slot = c.weight_chunk(w_in, C_MLAQ + part * w, w)

        def qtile(i, slot=slot, part=part):
            bank, m = c.token_product(slot, w, fold(c, 0, i), KD, c.h_ready)
            slot.used = m
            yield
            n = c.scratch.take()
            V.after(*n.free)
            m = c.head_norm(bank.buf[:, 0:w].rearrange("p (h d) -> p h d", h=heads), heads, MLA_D,
                            n.buf[:, 0:w].rearrange("p (h d) -> p h d", h=heads), [m])
            c.banks.give(bank, m)
            yield from finish_heads(n, heads, part * heads, i, c.row["qmla"], q, m)
        pipelined((qtile(i) for i in range(NT)), 3)
        c.weights.give(slot, slot.used)

    slot = c.weight_chunk(w_in, C_CKV, KV_RANK)
    slot2 = c.weight_chunk(w_in, C_CKV + KV_RANK, ROPE)

    def ckv(i):
        bank, m = c.token_product(slot, KV_RANK, fold(c, 0, i), KD, c.h_ready)
        bank, m = c.token_product(slot2, ROPE, fold(c, 0, i), KD, c.h_ready, bank=bank, at=KV_RANK)
        slot.used = m
        yield
        n = c.scratch.take()
        V.after(*n.free)
        m0 = c.copy(krope[:, i, :], bank.buf[:, KV_RANK:KV_RANK + ROPE], [m], "act")
        m = c.head_norm(bank.buf[:, 0:KV_RANK].unsqueeze(1), 1, KV_RANK, n.buf[:, 0:KV_RANK].unsqueeze(1), [m, m0])
        c.banks.give(bank, m)
        yield
        tb, m = c.transpose_blocks([n.buf[:, j * P:(j + 1) * P] for j in range(2)], P, [m])
        c.scratch.give(n, m)
        for j in range(2):
            A.after(m)
            m = A.run(nc.scalar.activation(ckvT[:, j, i * P:(i + 1) * P], tb.buf[:, j * P:(j + 1) * P],
                                           ACT.Identity, scale=columns(c.col["norm_ckv"], j)))
        c.banks.give(tb, m)
        ckv_ready.append(m)
    ckv_ready = []
    pipelined((ckv(i) for i in range(NT)), 3)
    c.weights.give(slot, slot.used)
    c.weights.give(slot2, slot.used)

    slot = c.weight_chunk(w_ukv, 0, MLA_H * (NOPE + MLA_V), kt=KV_RANK // P)

    def kvtile(i, half):
        heads = 4
        bank, m = c.token_product(slot, 512, lambda kk: ckvT[:, kk, i * P:(i + 1) * P], 2, ckv_ready, c0=512 * half)
        slot.used = m
        yield
        b3 = bank.buf[:, :].rearrange("p (h d) -> p h d", h=heads)
        n = c.scratch.take()
        n3 = n.buf[:, 0:heads * MLA_D].rearrange("p (h d) -> p h d", h=heads)
        vd = v[:, i, half * 256:(half + 1) * 256].rearrange("p (h d) -> p h d", h=heads)
        m = c.copy(vd, b3[:, :, NOPE:], [m], "act")
        ready.append(m)
        m = c.copy(n3[:, :, 0:NOPE], b3[:, :, 0:NOPE], [m, *n.free], "act")
        c.banks.give(bank, m)
        G.after(*n.free, *ckv_ready)
        m2 = G.run(nc.gpsimd.tensor_copy(n3[:, :, NOPE:], krope[:, i, :].unsqueeze(1).to_broadcast([P, heads, ROPE])))
        m = c.head_norm(n3, heads, MLA_D, n3, [m, m2])
        yield from finish_heads(n, heads, half * heads, i, c.row["kmla"], k, m)
    pipelined((kvtile(i, half) for half in range(2) for i in range(NT)), 3)
    c.weights.give(slot, slot.used)
    causal_softmax(c, lambda h: (slice(0, MLA_D), h), q, k, v, MLA_D ** -0.5, ready, 0)


def causal_softmax(c, place, q, k, v, scale, ready, out0):
    nc, PE, V = c.nc, c.PE, c.DVE
    for i in range(NT):
        ob = c.banks.take()
        PE.after(*ob.free)
        sums, nm = c.small.take(), c.small.take()
        V.after(*sums.free, *nm.free)
        c.ACT.after(*sums.free)
        pv = []

        def head(h, i=i, ob=ob, sums=sums, nm=nm, pv=pv):
            rows, t = place(h)
            return c.softmax_item(
                q[rows, t, i * P:(i + 1) * P], k[rows, t, 0:(i + 1) * P], i + 1,
                [(c.const("ident"), c.const("causal"), i * P)], scale,
                lambda b: v[:, b, h * HD:(h + 1) * HD], ob.buf[:, h * HD:(h + 1) * HD],
                nm.buf[:, h:h + 1], sums.buf[:, h:h + 1], ready, pv.append)
        pipelined((head(h) for h in range(H)), 3)
        V.after(pv[-1])
        m = V.run(nc.vector.reciprocal(sums.buf[:, 0:H], sums.buf[:, 0:H]))
        V.after(m)
        o = c.scratch.take()
        V.after(*o.free)
        m = V.run(nc.vector.tensor_tensor(o.buf[:].rearrange("p (h d) -> p h d", h=H),
                                          ob.buf[:].rearrange("p (h d) -> p h d", h=H),
                                          sums.buf[:, 0:H].unsqueeze(2).to_broadcast([P, H, HD]), ALU.mult))
        c.banks.give(ob, m)
        c.small.give(sums, m)
        c.small.give(nm, m)
        tb, m = c.transpose_blocks([o.buf[:, j * P:(j + 1) * P] for j in range(4)], P, [m])
        c.scratch.give(o, m)
        m = c.copy(c.mixed[:, out0:out0 + 4, i * P:(i + 1) * P],
                   tb.buf[:].rearrange("p (a t) -> p a t", a=4), [m])
        c.banks.give(tb, m)
        c.mixed_ready.append(m)


def merge(c):
    nc, PE, A, V = c.nc, c.PE, c.ACT, c.DVE
    merged = c.arena[:, 0:KD * S].rearrange("p (a t) -> p a t", a=KD)
    c.barrier()
    ready = []
    for jj in range(KD // 2):
        gates = [c.weight_chunk(c.io["w_in"], C_GATE + n * D + jj * 256, 256) for n in range(2)]
        projs = [c.weight_chunk(c.io[w], jj * 256, 256, kt=4) for w in ("w_o_mla", "w_o_dil")]

        def column(m_, jj=jj, gates=gates, projs=projs):
            j = 2 * jj + m_
            got = []
            for n in range(2):
                gb, m = c.feature_product(gates[n], m_, c.hT, KD, c.h_ready)
                gates[n].used = m
                gs = c.scratch.take()
                A.after(m, *gs.free)
                m = A.run(nc.scalar.activation(gs.buf[:], gb.buf[:], ACT.Sigmoid,
                                               bias=columns(c.col["b_gate"], n * KD + j)))
                c.banks.give(gb, m)
                pb, m2 = c.feature_product(projs[n], m_, c.mixed[:, 4 * n:4 * n + 4, :], 4, c.mixed_ready)
                projs[n].used = m2
                got.append((gs, m, pb, m2))
            yield
            for gs, m, pb, m2 in got:
                V.after(m, m2)
                m = V.run(nc.vector.tensor_tensor(gs.buf[:], gs.buf[:], pb.buf[:], ALU.mult))
                c.banks.give(pb, m)
            V.after(m)
            m = V.run(nc.vector.tensor_tensor(merged[:, j, :], got[0][0].buf[:], got[1][0].buf[:], ALU.add))
            ready.append(m)
            for g in got:
                c.scratch.give(g[0], m)
        pipelined((column(m_) for m_ in range(2)), 2)
        for s in gates + projs:
            c.weights.give(s, s.used)
    c.h_free = [PE.last()]
    project_out(c, c.io["w_out"], merged, KD, ready)


def project_out(c, w, actT, kt, ready, gate=None):
    per = 16 // 2
    for jj in range(KD // 2):
        banks = [None, None]
        for k0 in range(0, kt, per):
            n = min(per, kt - k0)
            slot = c.weight_chunk(w, jj * 256, 256, kt=n, k0=k0)
            for m_ in range(2):
                banks[m_], m = c.feature_product(slot, m_, actT[:, k0:k0 + n, :], n, ready, bank=banks[m_],
                                                 first=k0 == 0, last=k0 + n == kt)
            c.weights.give(slot, m)
        for m_ in range(2):
            j = 2 * jj + m_
            c.add_residual(banks[m_], m, j, None if gate is None else gate(j))


def moe(c):
    nc, io, PE, A, V, G = c.nc, c.io, c.PE, c.ACT, c.DVE, c.POOL
    c.barrier()
    L = c.arena
    at = [0]

    def take(n, dt=None):
        a = L[:, at[0]:at[0] + n]
        at[0] += n
        return a if dt is None else a.bitcast(dt)
    NL = N_GRP + NE
    logits = take(NT * NL).rearrange("p (t n) -> p t n", t=NT)
    g8 = take(NT * 8).rearrange("p (t n) -> p t n", t=NT)
    top = take(NT * 8).rearrange("p (t n) -> p t n", t=NT)
    idx = take(NT * 8, U32).rearrange("p (t n) -> p t n", t=NT)
    pick = take(2 * NT).rearrange("p (n t) -> p n t", n=2)
    onehot = take(2 * NT * NE).rearrange("p (n t e) -> p n t e", n=2, t=NT)
    both = take(NT * NE).rearrange("p (t e) -> p t e", t=NT)
    place = take(NT * NE).rearrange("p (t e) -> p t e", t=NT)
    tmp = take(NT * NE).rearrange("p (t e) -> p t e", t=NT)
    stat = take(8 * NT).rearrange("p (n t) -> p n t", n=8)
    slotf = take(2 * NT)
    sloti = take(2 * NT, I32)
    blocks = take(8 + NBLK)
    block_e = take(NBLK, I32)
    tokens = take(NBLK, I32)
    table = take(P)
    xb = [take(D) for _ in range(3)]
    xbT = [take(D) for _ in range(2)]
    yb = [take(D) for _ in range(3)]

    stored = []
    h2_sem = c.sem("h2_out")
    n_stored = 0
    for i in range(NT):
        for half in range(2):
            tb, m = c.transpose_blocks([c.hT[:, 4 * half + j, i * P:(i + 1) * P] for j in range(4)], P, c.h_ready)
            s = c.scratch.take()
            m = c.copy(s.buf[:], tb.buf[:], [m, *s.free])
            c.banks.give(tb, m)
            G.after(m)
            nc.gpsimd.dma_start(c.h2_dram[i * P:(i + 1) * P, half * 512:(half + 1) * 512], s.buf[:]).then_inc(h2_sem, 16)
            n_stored += 16
            c.scratch.give(s, (h2_sem, n_stored))
    h2_stored = (h2_sem, n_stored)

    wg = c.weight_chunk(io["w_router_group"], 0, N_GRP)
    we = c.weight_chunk(io["w_router_expert"], 0, NE)
    bank = c.banks.take()
    PE.after(*bank.free)
    for i in range(NT):
        c.token_product(wg, N_GRP, fold(c, 0, i), KD, c.h_ready, bank=bank, at=i * NL)
        _, m = c.token_product(we, NE, fold(c, 0, i), KD, c.h_ready, bank=bank, at=i * NL + N_GRP)
    c.weights.give(wg, m)
    c.weights.give(we, m)
    c.h_free = [m]
    bias = c.rows[:, 2 * MLA_D:2 * MLA_D + NL].unsqueeze(1).to_broadcast([P, NT, NL])

    def v(ins):
        return V.run(ins)
    V.after(m)
    m = v(nc.vector.tensor_tensor(logits, bank.buf[:, 0:NT * NL].rearrange("p (t n) -> p t n", t=NT), bias, ALU.add))
    c.banks.give(bank, m)
    m2 = v(nc.vector.memset(g8, NEG))
    V.after(m, m2)
    m = v(nc.vector.tensor_copy(g8[:, :, 0:N_GRP], logits[:, :, 0:N_GRP]))
    for i in range(NT):
        V.after(m)
        m = v(nc.vector.max(top[:, i, :], g8[:, i, :]))
        V.after(m)
        m = v(nc.vector.max_index(idx[:, i, :], top[:, i, :], g8[:, i, :]))
    V.after(m)
    m = v(nc.vector.tensor_copy(stat[:, 0, :], idx[:, :, 0]))
    m = v(nc.vector.tensor_tensor(g8[:, :, 0:N_GRP], g8[:, :, 0:N_GRP],
                                  top[:, :, 0:1].to_broadcast([P, NT, N_GRP]), ALU.subtract))
    A.after(m)
    m = A.run(nc.scalar.activation(g8[:, :, 0:N_GRP], g8[:, :, 0:N_GRP], ACT.Exp))
    V.after(m)
    m = v(nc.vector.tensor_reduce(stat[:, 1, :], g8[:, :, 0:N_GRP], AX.X, ALU.add))
    V.after(m)
    m = v(nc.vector.reciprocal(stat[:, 1, :], stat[:, 1, :]))
    chosen = g8[:, :, N_GRP:2 * N_GRP]
    m = v(nc.vector.tensor_tensor(chosen, c.const("group")[:, 0:N_GRP].unsqueeze(1).to_broadcast([P, NT, N_GRP]),
                                  stat[:, 0, :].unsqueeze(2).to_broadcast([P, NT, N_GRP]), ALU.is_equal))
    V.after(m)
    m = v(nc.vector.tensor_scalar(chosen, chosen, -1.0, -NEG, ALU.add, ALU.mult))
    V.after(m)
    for i in range(NT):
        m = v(nc.vector.tensor_tensor(tmp[:, i, :].rearrange("p (g e) -> p g e", g=N_GRP),
                                      logits[:, i, N_GRP:].rearrange("p (g e) -> p g e", g=N_GRP),
                                      chosen[:, i, :].unsqueeze(2).to_broadcast([P, N_GRP, PER_GRP]), ALU.add))
    for i in range(NT):
        V.after(m)
        m = v(nc.vector.max(top[:, i, :], tmp[:, i, :]))
        V.after(m)
        m = v(nc.vector.max_index(idx[:, i, :], top[:, i, :], tmp[:, i, :]))
    V.after(m)
    m = v(nc.vector.tensor_tensor(stat[:, 2, :], top[:, :, 1], top[:, :, 0], ALU.subtract))
    A.after(m)
    m = A.run(nc.scalar.activation(stat[:, 2, :], stat[:, 2, :], ACT.Exp))
    for n in range(2):
        m3 = v(nc.vector.tensor_copy(pick[:, n, :], idx[:, :, n]))
    V.after(m, m3)
    m = v(nc.vector.tensor_scalar(stat[:, 3, :], stat[:, 2, :], 1.0, None, ALU.add))
    V.after(m)
    m = v(nc.vector.reciprocal(stat[:, 3, :], stat[:, 3, :]))
    V.after(m)
    m = v(nc.vector.tensor_tensor(stat[:, 4, :], stat[:, 1, :], stat[:, 3, :], ALU.mult))
    V.after(m)
    share = v(nc.vector.tensor_tensor(stat[:, 5, :], stat[:, 4, :], stat[:, 2, :], ALU.mult))
    V.after(share)
    for n in range(2):
        m = v(nc.vector.tensor_tensor(onehot[:, n, :, :], c.const("expert").unsqueeze(1).to_broadcast([P, NT, NE]),
                                      pick[:, n, :].unsqueeze(2).to_broadcast([P, NT, NE]), ALU.is_equal))
    V.after(m)
    m = v(nc.vector.tensor_tensor(both, onehot[:, 0, :, :], onehot[:, 1, :, :], ALU.add))
    rank, count = c.banks.take(), c.banks.take()
    PE.after(m, *rank.free, *count.free)
    for i in range(NT):
        for j in range(i + 1):
            mm = nc.tensor.matmul(rank.buf[:, i * NE:(i + 1) * NE], c.const("before" if j == i else "ones"),
                                  both[:, j, :], start=j == 0, stop=j == i)
        nc.tensor.matmul(count.buf[0:NE, 0:1], both[:, i, :], c.const("ones")[:, 0:1], start=i == 0, stop=i == NT - 1)
    m = PE.run(nc.tensor.matmul(rank.buf[:, NT * NE:NT * NE + 1], c.const("ones"), c.const("ones")[:, 0:1],
                                start=True, stop=True))
    cnt, nblk, end, per = blocks[0:NE, 0:1], blocks[0:NE, 1:2], blocks[0:NE, 2:3], blocks[0:NE, 4:8]
    V.after(m)
    m = v(nc.vector.tensor_copy(cnt, count.buf[0:NE, 0:1]))
    V.after(m)
    m = v(nc.vector.tensor_scalar(per, c.const("thresholds", NE), cnt, None, ALU.is_lt))
    V.after(m)
    m = v(nc.vector.tensor_reduce(nblk, per, AX.X, ALU.add))
    PE.after(m)
    before = c.const("before", NE)[:, 0:NE]
    nc.tensor.matmul(count.buf[0:NE, 1:2], before, nblk, start=True, stop=False)
    nc.tensor.matmul(count.buf[0:NE, 1:2], c.const("ident", NE)[:, 0:NE], nblk, start=False, stop=True)
    m = PE.run(nc.tensor.matmul(count.buf[:, 2:2 + NE], nblk.to_broadcast([NE, P]), before, start=True, stop=True))
    V.after(m)
    m = v(nc.vector.tensor_copy(end, count.buf[0:NE, 1:2]))
    V.after(m)
    m = v(nc.vector.tensor_scalar(blocks[0:NE, 8:8 + NBLK], c.const("block", NE), end, None, ALU.is_ge))
    PE.after(m)
    m2 = PE.run(nc.tensor.matmul(rank.buf[0:1, 256:256 + NBLK], c.const("ones", NE)[:, 0:1],
                                 blocks[0:NE, 8:8 + NBLK], start=True, stop=True))
    V.after(m2)
    expert_ready = v(nc.vector.tensor_scalar(block_e[0:1, :], rank.buf[0:1, 256:256 + NBLK], float(NE - 1), None, ALU.min))
    V.after(m)
    m = v(nc.vector.tensor_scalar(tmp[:, 0, :], count.buf[:, 2:2 + NE], float(P), None, ALU.mult))
    c.banks.give(count, m)
    V.after(m)
    m = v(nc.vector.tensor_tensor(place, rank.buf[:, 0:NT * NE].rearrange("p (t e) -> p t e", t=NT),
                                  tmp[:, 0, :].unsqueeze(1).to_broadcast([P, NT, NE]), ALU.add))
    c.banks.give(rank, m)
    for n in range(2):
        V.after(m)
        m = v(nc.vector.tensor_tensor(tmp, onehot[:, n, :, :], place, ALU.mult))
        V.after(m)
        m = v(nc.vector.tensor_reduce(slotf[:, n * NT:(n + 1) * NT], tmp, AX.X, ALU.add))
    V.after(m)
    slots_ready = v(nc.vector.tensor_copy(sloti, slotf))
    m = G.run(nc.gpsimd.memset(table[0:NBLK, :], 0.0))
    G.after(m)
    tsem = c.sem("token_table")
    nc.gpsimd.dma_start(c.table_dram.rearrange("(b p) o -> b (p o)", p=P), table[0:NBLK, :]).then_inc(tsem, 16)
    G.after((tsem, 16), slots_ready)
    for n in range(2):
        for i in range(NT):
            nc.gpsimd.indirect_dma_start(
                out=c.table_dram, out_offset=bass.IndirectOffsetOnAxis(ap=sloti[:, n * NT + i:n * NT + i + 1], axis=0),
                in_=c.const("token")[:, i:i + 1], in_offset=None).then_inc(tsem, 16)
    G.after((tsem, 16 * (1 + 2 * NT)))
    nc.gpsimd.dma_start(table[0:NBLK, :], c.table_dram.rearrange("(b p) o -> b (p o)", p=P)).then_inc(tsem, 16)
    bank = c.banks.take()
    PE.after(*bank.free, (tsem, 16 * (2 + 2 * NT)))
    m = PE.run(nc.tensor.transpose(bank.buf[:, 0:NBLK], table[0:NBLK, :], c.const("ident", NBLK)[:, 0:NBLK]))
    V.after(m)
    tokens_ready = v(nc.vector.tensor_copy(tokens, bank.buf[:, 0:NBLK]))
    c.banks.give(bank, tokens_ready)

    gathers = [c.sem(f"gather{j}") for j in range(3)]
    outs = [c.sem(f"tile_out{j}") for j in range(3)]
    x_free = [[] for _ in range(3)]
    xT_free = [[] for _ in range(2)]
    c.SP.after(expert_ready)
    G.after(tokens_ready, h2_stored)

    def tile(b):
        j = b % 3
        G.after(*x_free[j])
        nc.gpsimd.indirect_dma_start(out=xb[j], out_offset=None, in_=c.h2_dram,
                                     in_offset=bass.IndirectOffsetOnAxis(ap=tokens[:, b:b + 1], axis=0)
                                     ).then_inc(gathers[j], 16)
        e = nc.sync.value_load(block_e[0:1, b:b + 1], min_val=0, max_val=NE - 1)
        w = []
        for name, kt, n in (("w_gate", KD, FF), ("w_up", KD, FF), ("w_down", FF // P, D)):
            view = lambda buf, kt=kt: buf.rearrange("p (k n) -> p k n", k=kt)
            src = io[name][bass.ds(e, 1), :, :].rearrange("e (k p) n -> p (e k) n", p=P)
            s = c.weights.load(view, src)
            s.w = view(s.buf)
            w.append(s)
        yield
        xt = xbT[b % 2]
        marks = []
        for half in range(2):
            tb, m = c.transpose_blocks([xb[j][:, (4 * half + q) * P:(4 * half + q + 1) * P] for q in range(4)], P,
                                       [(gathers[j], 16 * (b // 3 + 1))])
            x_free[j] = [m]
            m = c.copy(xt[:, half * 512:(half + 1) * 512], tb.buf[:], [m, *xT_free[b % 2]])
            marks.append(m)
            c.banks.give(tb, m)
        yield
        toks = lambda k: xt[:, k * P:(k + 1) * P]
        gb, m1 = c.token_product(w[0], FF, toks, KD, marks)
        ub, m2 = c.token_product(w[1], FF, toks, KD, marks)
        xT_free[b % 2] = [m2]
        c.weights.give(w[0], m1)
        c.weights.give(w[1], m2)
        he = c.scratch.take()
        A.after(m1, *he.free)
        m = A.run(nc.scalar.activation(he.buf[:, 0:FF], gb.buf[:, 0:FF], ACT.Silu))
        c.banks.give(gb, m)
        V.after(m, m2)
        m = V.run(nc.vector.tensor_tensor(he.buf[:, 0:FF], he.buf[:, 0:FF], ub.buf[:, 0:FF], ALU.mult))
        c.banks.give(ub, m)
        yield
        tb, m = c.transpose_blocks([he.buf[:, q * P:(q + 1) * P] for q in range(2)], P, [m])
        m = c.copy(he.buf[:, FF:2 * FF], tb.buf[:, 0:FF], [m])
        c.banks.give(tb, m)
        yield
        PE.after(m, w[2].ready)
        done = []
        for half in range(2):
            bk = c.banks.take()
            PE.after(*bk.free)
            for q in range(2):
                mm = nc.tensor.matmul(bk.buf[:], he.buf[:, FF + q * P:FF + (q + 1) * P],
                                      w[2].w[:, q, half * 512:(half + 1) * 512], start=q == 0, stop=q == 1)
            m = PE.run(mm)
            out_free = [(outs[j], 16 * (b // 3))] if b >= 3 else []
            mc = c.copy(yb[j][:, half * 512:(half + 1) * 512], bk.buf[:], [m, *out_free])
            c.banks.give(bk, mc)
            done.append(mc)
        c.scratch.give(he, m)
        c.weights.give(w[2], m)
        G.after(*done)
        nc.gpsimd.dma_start(c.y_dram[b * P:(b + 1) * P, :], yb[j]).then_inc(outs[j], 16)
    pipelined((tile(b) for b in range(NBLK)), 2)

    for j in range(3):
        G.after((outs[j], 16 * len(range(j, NBLK, 3))))
    c.barrier()
    tail = [c.sem(f"combine{i}") for i in range(NT)]
    both_y = xb + yb
    tail_free = [[] for _ in range(3)]
    for i in range(NT):
        pair = (both_y[2 * (i % 3)], both_y[2 * (i % 3) + 1])
        G.after(*tail_free[i % 3])
        for n in range(2):
            nc.gpsimd.indirect_dma_start(out=pair[n], out_offset=None, in_=c.y_dram,
                                         in_offset=bass.IndirectOffsetOnAxis(ap=sloti[:, n * NT + i:n * NT + i + 1], axis=0)
                                         ).then_inc(tail[i], 16)
        V.after((tail[i], 32))
        m = V.run(nc.vector.tensor_scalar(pair[1], pair[1], stat[:, 5, i:i + 1], None, ALU.mult))
        V.after(m)
        m = V.run(nc.vector.scalar_tensor_tensor(out=pair[0], in0=pair[0], scalar=stat[:, 4, i:i + 1], in1=pair[1],
                                                 op0=ALU.mult, op1=ALU.add))
        for half in range(2):
            tb, mt = c.transpose_blocks([pair[0][:, (4 * half + q) * P:(4 * half + q + 1) * P] for q in range(4)],
                                        P, [m])
            x = c.xT[:, 4 * half:4 * half + 4, i * P:(i + 1) * P]
            V.after(mt, *[mk for k in range(4) for mk in c.x_ready[4 * half + k]])
            mv = V.run(nc.vector.tensor_tensor(x, x, tb.buf[:].rearrange("p (a t) -> p a t", a=4), ALU.add))
            c.banks.give(tb, mv)
            tail_free[i % 3] = [mv]
    c.x_ready = [[V.last()] for _ in range(KD)]


def head_groups(c):
    nc, PE, A, V, G = c.nc, c.PE, c.ACT, c.DVE, c.POOL
    w_in = c.io["attn_w_in_2"]
    qa, ka, va, qb, kb, vb = (c.arena[:, j * 4 * S:(j + 1) * 4 * S].rearrange("p (a t) -> p a t", a=4)
                              for j in range(6))
    c.barrier()
    c.mixed_ready = []
    ready = []
    heads, half = 4, ROPE2 // 2
    for part, dst in ((0, qa), (1, ka), (2, va), (5, vb)):
        for hf in range(2):
            slot = c.weight_chunk(w_in, part * 512 + hf * 256, 256)

            def tile(i, slot=slot, part=part, dst=dst, hf=hf):
                bank, m = c.token_product(slot, 256, fold(c, 0, i), KD, c.h_ready)
                slot.used = m
                yield
                if part in (2, 5):
                    m = c.copy(dst[:, i, hf * 256:(hf + 1) * 256], bank.buf[:, 0:256], [m])
                    c.banks.give(bank, m)
                    ready.append(m)
                    return
                n = c.scratch.take()
                m = c.copy(n.buf[:, 0:256], bank.buf[:, 0:256], [m, *n.free])
                c.banks.give(bank, m)
                n3 = n.buf[:, 0:256].rearrange("p (h d) -> p h d", h=heads)
                m = c.rope(n3[:, :, 0:half], n3[:, :, half:2 * half], c.cos2[:, i, :], c.sin2[:, i, :], heads, half,
                           [m, c.rope_ready])
                yield
                tb, m = c.transpose_blocks([n.buf[:, j * P:(j + 1) * P] for j in range(2)], P, [m])
                c.scratch.give(n, m)
                m = c.copy(dst[:, 2 * hf:2 * hf + 2, i * P:(i + 1) * P],
                           tb.buf[:, 0:256].rearrange("p (a t) -> p a t", a=2), [m])
                c.banks.give(tb, m)
                ready.append(m)
            pipelined((tile(i) for i in range(NT)), 3)
            c.weights.give(slot, slot.used)
    for part, dst in ((3, qb), (4, kb)):
        for hf in range(2):
            slot = c.weight_chunk(w_in, part * 512 + hf * 256, 256)
            for m_ in range(2):
                bank, m = c.feature_product(slot, m_, c.hT, KD, c.h_ready)
                A.after(m)
                mc = A.run(nc.scalar.activation(dst[:, 2 * hf + m_, :], bank.buf[:], ACT.Copy,
                                                scale=1.0 if part == 3 else HD ** -0.5))
                c.banks.give(bank, mc)
                ready.append(mc)
            c.weights.give(slot, m)
    c.h_free = [PE.last()]
    causal_softmax(c, lambda h: (slice(HD * (h % 2), HD * (h % 2) + HD), h // 2), qa, ka, va, HD ** -0.5, ready, 0)
    c.barrier()

    o = qa

    def head(h):
        rows, t = slice(HD * (h % 2), HD * (h % 2) + HD), h // 2
        sp = []
        for j in range(NT):
            n = S - j * P
            zb = c.banks.take()
            PE.after(*zb.free)
            m = PE.run(nc.tensor.matmul(zb.buf[:, 0:n], kb[rows, t, j * P:(j + 1) * P], qb[rows, t, j * P:S],
                                        start=True, stop=True))
            s = c.scratch.take()
            A.after(m, *s.free)
            m = A.run(nc.scalar.activation(s.buf[:, 0:n], zb.buf[:, 0:n], ACT.Abs))
            A.after(m)
            m = A.run(nc.scalar.activation(s.buf[:, 0:n], s.buf[:, 0:n], ACT.Exp, scale=-1.0))
            A.after(m)
            m = A.run(nc.scalar.activation(s.buf[:, 0:n], s.buf[:, 0:n], ACT.Ln, bias=1.0))
            V.after(m)
            m = V.run(nc.vector.scalar_tensor_tensor(out=s.buf[:, 0:n], in0=zb.buf[:, 0:n], scalar=0.0,
                                                     in1=s.buf[:, 0:n], op0=ALU.max, op1=ALU.add))
            c.banks.give(zb, m)
            V.after(m)
            m = V.run(nc.vector.tensor_tensor(s.buf[:, 0:P], s.buf[:, 0:P], c.const("sb_keep"), ALU.mult))
            sp.append((s, m))
            yield
        ws = []
        for i in range(NT):
            n = S - i * P
            cb = c.banks.take()
            PE.after(*cb.free)
            nc.tensor.matmul(cb.buf[:, 0:n], kb[rows, t, i * P:(i + 1) * P], qb[rows, t, i * P:S], start=True, stop=False)
            nc.tensor.matmul(cb.buf[:, 0:P], c.const("ident"), c.const("sb_mask"), start=False, stop=False)
            for j in range(i, NT):
                PE.after(sp[j][1])
                mm = nc.tensor.matmul(cb.buf[:, (j - i) * P:n], c.const("neg_from" if j == i else "neg_ones"),
                                      sp[j][0].buf[:, 0:S - j * P], start=False, stop=j == NT - 1)
            m = PE.run(mm)
            w = sp[i][0]
            A.after(m)
            m = A.run(nc.scalar.activation(w.buf[:, 0:n], cb.buf[:, 0:n], ACT.Exp))
            c.banks.give(cb, m)
            ws.append((w, m))
        yield
        ob = c.banks.take()
        PE.after(*ob.free, *[m for _, m in ws])
        for q in range(NT):
            for i in range(q + 1):
                mm = nc.tensor.matmul(ob.buf[:, q * HD:(q + 1) * HD], ws[i][0].buf[:, (q - i) * P:(q - i + 1) * P],
                                      vb[:, i, h * HD:(h + 1) * HD], start=i == 0, stop=i == q)
        m = PE.run(mm)
        for w, _ in ws:
            c.scratch.give(w, m)
        m = c.copy(o[:, :, h * HD:(h + 1) * HD], ob.buf[:, 0:NT * HD].rearrange("p (q d) -> p q d", q=NT), [m])
        c.banks.give(ob, m)
        done.append(m)
    done = []
    pipelined((head(h) for h in range(H)), 2)
    for i in range(NT):
        tb, m = c.transpose_blocks([o[:, i, j * P:(j + 1) * P] for j in range(4)], P, done)
        m = c.copy(c.mixed[:, 4:8, i * P:(i + 1) * P], tb.buf[:].rearrange("p (a t) -> p a t", a=4), [m])
        c.banks.give(tb, m)
        c.mixed_ready.append(m)


def swiglu(c, layer):
    nc, A, V = c.nc, c.ACT, c.DVE
    w_in, w_out = c.io["ffn_w_in_2"][layer], c.io["ffn_w_out_2"][layer]
    hid = c.arena[:, 0:KH * S].rearrange("p (a t) -> p a t", a=KH)
    c.barrier()
    ready = []
    for jj in range(KH // 2):
        gs, us = c.weight_chunk(w_in, jj * 256, 256), c.weight_chunk(w_in, HID + jj * 256, 256)
        for m_ in range(2):
            gb, m1 = c.feature_product(gs, m_, c.hT, KD, c.h_ready)
            ub, m2 = c.feature_product(us, m_, c.hT, KD, c.h_ready)
            dst = hid[:, 2 * jj + m_, :]
            A.after(m1)
            m = A.run(nc.scalar.activation(dst, gb.buf[:], ACT.Silu))
            c.banks.give(gb, m)
            V.after(m, m2)
            m = V.run(nc.vector.tensor_tensor(dst, dst, ub.buf[:], ALU.mult))
            c.banks.give(ub, m)
            ready.append(m)
        c.weights.give(gs, m1)
        c.weights.give(us, m2)
    c.h_free = [c.PE.last()]
    project_out(c, w_out, hid, KH, ready[-1:], gate=lambda j: c.mod[:, layer, 5, j:j + 1])


def delta_net(c):
    nc, PE, A, V, G = c.nc, c.PE, c.ACT, c.DVE, c.POOL
    w_in = c.io["gdn_w_in_2"]
    HG = 4
    c.barrier()
    qT, kT, ktok, vtok = (c.arena[:, j * HG * S:(j + 1) * HG * S].rearrange("p (a t) -> p a t", a=HG)
                          for j in range(4))
    for j in range(8):
        c.scratch.give(Slot(c.arena[:, (16 + j) * S:(17 + j) * S]))
    g4 = lambda a: a.rearrange("p (h t) -> p h t", h=HG)

    slot = c.weight_chunk(w_in, 4 * H * GD, 2 * H)
    bank = c.banks.take()
    PE.after(*bank.free)
    for i in range(NT):
        _, m = c.token_product(slot, 2 * H, fold(c, 0, i), KD, c.h_ready, bank=bank, at=i * 2 * H)
    c.weights.give(slot, m)
    col = c.gate_cols
    x, t, g, beta, gcum, gtot, bexp, kdec = (col[:, j, :, :] for j in range(8))
    b3 = bank.buf[:, 0:NT * 2 * H].rearrange("p (t n) -> p t n", t=NT)
    over = lambda r: r.unsqueeze(1).to_broadcast([P, NT, H])
    V.after(m)
    m = V.run(nc.vector.tensor_tensor(x, b3[:, :, 0:H], over(c.row["dt_bias"]), ALU.add))
    A.after(m)
    m1 = A.run(nc.scalar.activation(beta, b3[:, :, H:], ACT.Sigmoid))
    c.banks.give(bank, m1)
    m = A.run(nc.scalar.activation(t, x, ACT.Abs))
    A.after(m)
    m = A.run(nc.scalar.activation(t, t, ACT.Exp, scale=-1.0))
    A.after(m)
    m = A.run(nc.scalar.activation(t, t, ACT.Ln, bias=1.0))
    m = A.run(nc.scalar.activation(c.row["a_log"], c.row["a_log"], ACT.Exp))
    V.after(m)
    m = V.run(nc.vector.scalar_tensor_tensor(out=g, in0=x, scalar=0.0, in1=t, op0=ALU.max, op1=ALU.add))
    V.after(m)
    m = V.run(nc.vector.scalar_tensor_tensor(out=g, in0=g, scalar=-1.0, in1=over(c.row["a_log"]),
                                             op0=ALU.mult, op1=ALU.mult))
    bank = c.banks.take()
    PE.after(m, *bank.free)
    flat = lambda a: a.rearrange("p t h -> p (t h)")
    nc.tensor.matmul(bank.buf[:, 0:NT * H], c.const("chunk_upto"), flat(g), start=True, stop=True)
    m = PE.run(nc.tensor.matmul(bank.buf[:, NT * H:2 * NT * H], c.const("chunk_all"), flat(g), start=True, stop=True))
    V.after(m)
    m = V.run(nc.vector.tensor_copy(flat(gcum), bank.buf[:, 0:NT * H]))
    V.after(m)
    m = V.run(nc.vector.tensor_tensor(flat(kdec), bank.buf[:, NT * H:2 * NT * H], flat(gcum), ALU.subtract))
    c.banks.give(bank, m)
    A.after(m)
    A.run(nc.scalar.activation(kdec, kdec, ACT.Exp))
    m = A.run(nc.scalar.activation(bexp, gcum, ACT.Exp))
    V.after(m, m1)
    cols_ready = V.run(nc.vector.tensor_tensor(bexp, bexp, beta, ALU.mult))

    state = c.state
    c.mixed_ready = []
    for hg in range(H // HG):
        sums = c.banks.take()
        PE.after(*sums.free)
        vfree, staged, tail = [], [], []
        for part, dst in ((0, qT), (1, kT), (2, None)):
            for hf in range(2):
                slot = c.weight_chunk(w_in, part * H * GD + hg * HG * GD + hf * 256, 256)

                def tile(m_, slot=slot, part=part, dst=dst, hf=hf):
                    hh = 2 * hf + m_
                    ct = part * H + hg * HG + hh
                    bank, m = c.feature_product(slot, m_, c.hT, KD, c.h_ready)
                    slot.used = m
                    yield
                    acc = c.scratch.take()
                    V.after(m, *acc.free)
                    tap = lambda d: c.conv_w[:, CONV - 1 - d, ct:ct + 1]
                    m = V.run(nc.vector.tensor_scalar(acc.buf[:], bank.buf[:], tap(0), None, ALU.mult))
                    for d in range(1, CONV):
                        V.after(m)
                        m = V.run(nc.vector.scalar_tensor_tensor(
                            out=acc.buf[:, d:S], in0=bank.buf[:, 0:S - d], scalar=tap(d), in1=acc.buf[:, d:S],
                            op0=ALU.mult, op1=ALU.add))
                    c.banks.give(bank, m)
                    yield
                    if part < 2:
                        A.after(m)
                        m = A.run(nc.scalar.activation(dst[:, hh, :], acc.buf[:], ACT.Silu))
                        A.after(m)
                        m = A.run(nc.scalar.activation(acc.buf[:], dst[:, hh, :], ACT.Square))
                        row = part * HG + hh
                        PE.after(m)
                        m = PE.run(nc.tensor.matmul(sums.buf[0:8, :], c.const("strip")[:, 15 - row:23 - row],
                                                    acc.buf[:], start=row == 0, stop=row == 7))
                        c.scratch.give(acc, m)
                        staged.append(m)
                    else:
                        A.after(m)
                        m = A.run(nc.scalar.activation(acc.buf[:], acc.buf[:], ACT.Silu))
                        yield
                        tb, m = c.transpose_blocks([acc.buf[:, i * P:(i + 1) * P] for i in range(NT)], P, [m])
                        c.scratch.give(acc, m)
                        m = c.copy(vtok[:, :, hh * P:(hh + 1) * P], tb.buf[:].rearrange("p (i d) -> p i d", i=NT), [m])
                        c.banks.give(tb, m)
                        tail.append(m)
                pipelined((tile(m_) for m_ in range(2)), 2)
                c.weights.give(slot, slot.used)
        rows = c.scratch.take()
        A.after(*staged, *rows.free)
        m = A.run(nc.scalar.activation(rows.buf[0:8, :], sums.buf[0:8, :], ACT.Sqrt, bias=c.eps[0:8, 0:1]))
        c.banks.give(sums, m)
        V.after(m)
        mr = V.run(nc.vector.reciprocal(rows.buf[0:8, :], rows.buf[0:8, :]))
        for row in range(8):
            dst = (qT if row < HG else kT)[:, row % HG, :]
            bank = c.banks.take()
            PE.after(mr, *bank.free)
            m = PE.run(nc.tensor.matmul(bank.buf[:], c.const("ident", 8)[:, row:row + 1].to_broadcast([8, P]),
                                        rows.buf[0:8, :], start=True, stop=True))
            V.after(m)
            m = V.run(nc.vector.scalar_tensor_tensor(out=dst, in0=dst, scalar=GD ** -0.5 if row < HG else 1.0,
                                                     in1=bank.buf[:], op0=ALU.mult, op1=ALU.mult))
            c.banks.give(bank, m)
            tail.append(m)
        c.scratch.give(rows, PE.last())
        for hh in range(HG):
            tb, m = c.transpose_blocks([kT[:, hh, i * P:(i + 1) * P] for i in range(NT)], P, tail)
            m = c.copy(ktok[:, :, hh * P:(hh + 1) * P], tb.buf[:].rearrange("p (i d) -> p i d", i=NT), [m])
            c.banks.give(tb, m)
            tail.append(m)
        V.after(*tail)
        state_ready = [V.run(nc.vector.memset(state[:], 0.0))]
        st = {"ready": state_ready}

        def product(left, right, width=P, marks=()):
            bank = c.banks.take()
            PE.after(*bank.free, *marks)
            for hh in range(HG):
                mm = nc.tensor.matmul(bank.buf[:, hh * width:(hh + 1) * width], left(hh), right(hh),
                                      start=True, stop=True)
            return bank, PE.run(mm)

        def block(s, hh):
            return s.buf[:, hh * P:(hh + 1) * P]

        def tile(i, hg=hg, tail=tail, st=st):
            tok = slice(i * P, (i + 1) * P)
            hs = slice(hg * HG, (hg + 1) * HG)
            per_head = lambda a: a[:, i, hs].unsqueeze(2).to_broadcast([P, HG, P])
            over_heads = lambda a: a.unsqueeze(1).to_broadcast([P, HG, P])
            rb, m = product(lambda hh: g[:, i, hg * HG + hh:hg * HG + hh + 1].to_broadcast([P, P]),
                            lambda hh: c.const("chunk_upto"), marks=[cols_ready, *tail])
            dec, erow = c.scratch.take(), c.scratch.take()
            V.after(m, *dec.free)
            for hh in range(HG):
                m = V.run(nc.vector.tensor_scalar(block(dec, hh), rb.buf[:, hh * P:(hh + 1) * P],
                                                  gcum[:, i, hg * HG + hh:hg * HG + hh + 1], 0.0,
                                                  ALU.subtract, ALU.min))
            A.after(m, *erow.free)
            m_e = A.run(nc.scalar.activation(erow.buf[:], rb.buf[:], ACT.Exp))
            c.banks.give(rb, m_e)
            m = A.run(nc.scalar.activation(dec.buf[:], dec.buf[:], ACT.Exp))
            G.after(m)
            m_dec = G.run(nc.gpsimd.tensor_tensor(g4(dec.buf[:]), g4(dec.buf[:]), over_heads(c.const("chunk_upto")), ALU.mult))
            yield
            gb, m1 = product(lambda hh: kT[:, hh, tok], lambda hh: kT[:, hh, tok], marks=tail)
            bb, m2 = product(lambda hh: beta[:, i, hg * HG + hh:hg * HG + hh + 1].to_broadcast([P, P]),
                             lambda hh: c.const("ident"))
            at_ = c.scratch.take()
            V.after(m1, m_dec, *at_.free)
            m = V.run(nc.vector.tensor_tensor(at_.buf[:], gb.buf[:], dec.buf[:], ALU.mult))
            c.banks.give(gb, m)
            V.after(m, m2)
            m_at = V.run(nc.vector.tensor_tensor(at_.buf[:], at_.buf[:], bb.buf[:], ALU.mult))
            c.banks.give(bb, m_at)
            qb, m3 = product(lambda hh: kT[:, hh, tok], lambda hh: qT[:, hh, tok])
            V.after(m3)
            m_attn = V.run(nc.vector.tensor_tensor(dec.buf[:], qb.buf[:], dec.buf[:], ALU.mult))
            attn = dec
            c.banks.give(qb, m_attn)
            G.after(m_e, *tail)
            qe, kb, vb, kd = (c.scratch.take() for _ in range(4))
            G.after(*qe.free, *kb.free, *vb.free, *kd.free, cols_ready)
            m_qe = G.run(nc.gpsimd.tensor_tensor(g4(qe.buf[:]), qT[:, :, tok], g4(erow.buf[:]), ALU.mult))
            G.run(nc.gpsimd.tensor_tensor(g4(kb.buf[:]), g4(ktok[:, i, :]), per_head(bexp), ALU.mult))
            G.run(nc.gpsimd.tensor_tensor(g4(vb.buf[:]), g4(vtok[:, i, :]), per_head(beta), ALU.mult))
            m_kd = G.run(nc.gpsimd.tensor_tensor(g4(kd.buf[:]), g4(ktok[:, i, :]), per_head(kdec), ALU.mult))
            yield
            level = lambda l: over_heads(c.const("levels")[:, l * P:(l + 1) * P])
            xt, xn, am = c.scratch.take(), c.scratch.take(), c.scratch.take()
            V.after(m_at, *xt.free, *xn.free, *am.free)
            m = V.run(nc.vector.tensor_tensor(g4(am.buf[:]), g4(at_.buf[:]), level(0), ALU.mult))
            V.after(m)
            m = V.run(nc.vector.tensor_tensor(g4(xt.buf[:]), over_heads(c.const("ident")), g4(am.buf[:]), ALU.subtract))
            tb, mt = c.transpose_blocks([block(xt, hh) for hh in range(HG)], P, [m])
            m_x = c.copy(xn.buf[:], tb.buf[:], [mt], "act")
            c.banks.give(tb, m_x)
            m_xt, m_b = m, m
            yield
            for l in range(1, LEVELS):
                V.after(m_b)
                m = V.run(nc.vector.tensor_tensor(g4(am.buf[:]), g4(at_.buf[:]), level(l), ALU.mult))
                bk, m = product(lambda hh: block(am, hh), lambda hh: block(xn, hh), marks=[m, m_x])
                m = c.copy(am.buf[:], bk.buf[:], [m], "act")
                c.banks.give(bk, m)
                yield
                if l < LEVELS - 1:
                    b1, ma = product(lambda hh: block(xt, hh), lambda hh: block(am, hh), marks=[m, m_xt])
                b2, mb = product(lambda hh: block(am, hh), lambda hh: block(xt, hh), marks=[m, m_xt])
                m_b = mb
                if l < LEVELS - 1:
                    V.after(ma)
                    m_x = V.run(nc.vector.tensor_tensor(xn.buf[:], xn.buf[:], b1.buf[:], ALU.subtract))
                    c.banks.give(b1, m_x)
                V.after(mb)
                m_xt = V.run(nc.vector.tensor_tensor(xt.buf[:], xt.buf[:], b2.buf[:], ALU.subtract))
                c.banks.give(b2, m_xt)
                yield
            ub, m1 = product(lambda hh: block(xt, hh), lambda hh: block(vb, hh), marks=[m_xt, m_kd])
            wb, m2 = product(lambda hh: block(kb, hh), lambda hh: block(xt, hh))
            u, w = xn, am
            m_u = c.copy(u.buf[:], ub.buf[:], [m1, m_b], "act")
            m_w = c.copy(w.buf[:], wb.buf[:], [m2, m_b], "act")
            c.banks.give(ub, m_u)
            c.banks.give(wb, m_w)
            c.scratch.give(xt, m2)
            c.scratch.give(kb, m2)
            c.scratch.give(at_, m_xt)
            yield
            for cc in range(P // CHUNK):
                rows_ = slice(cc * CHUNK, (cc + 1) * CHUNK)
                nb = c.banks.take()
                PE.after(*nb.free, m_w, m_qe, *st["ready"])
                for hh in range(HG):
                    mm = nc.tensor.matmul(nb.buf[rows_, hh * P:(hh + 1) * P],
                                          w.buf[:, hh * P + cc * CHUNK:hh * P + (cc + 1) * CHUNK],
                                          state[:, hh, :], start=True, stop=True)
                m = PE.run(mm)
                V.after(m, m_u)
                m_v = V.run(nc.vector.tensor_tensor(u.buf[rows_, :], u.buf[rows_, :], nb.buf[rows_, :], ALU.subtract))
                c.banks.give(nb, m_v)
                ob = c.banks.take()
                PE.after(*ob.free, m_attn)
                PE.after(m_v)
                for hh in range(HG):
                    cs = slice(hh * P + cc * CHUNK, hh * P + (cc + 1) * CHUNK)
                    o_ = ob.buf[:, hh * CHUNK:(hh + 1) * CHUNK]
                    nc.tensor.matmul(o_, state[:, hh, :], qe.buf[:, cs], start=True, stop=False)
                    mm = nc.tensor.matmul(o_, u.buf[rows_, hh * P:(hh + 1) * P], attn.buf[rows_, cs],
                                          start=False, stop=True)
                m_o = PE.run(mm)
                sb_ = c.banks.take()
                PE.after(*sb_.free)
                for hh in range(HG):
                    mm = nc.tensor.matmul(sb_.buf[:, hh * P:(hh + 1) * P], kd.buf[rows_, hh * P:(hh + 1) * P],
                                          u.buf[rows_, hh * P:(hh + 1) * P], start=True, stop=True)
                m_s = PE.run(mm)
                V.after(m_s, m_o)
                for hh in range(HG):
                    end = hh * P + (cc + 1) * CHUNK - 1
                    m = V.run(nc.vector.scalar_tensor_tensor(
                        out=state[:, hh, :], in0=state[:, hh, :], scalar=erow.buf[:, end:end + 1],
                        in1=sb_.buf[:, hh * P:(hh + 1) * P], op0=ALU.mult, op1=ALU.add))
                c.banks.give(sb_, m)
                st["ready"] = [m]
                t0 = i * P + cc * CHUNK
                m = c.copy(c.mixed[:, hg * HG:(hg + 1) * HG, t0:t0 + CHUNK],
                           ob.buf[:, 0:HG * CHUNK].rearrange("p (h t) -> p h t", h=HG), [m_o], "act")
                c.banks.give(ob, m)
                c.mixed_ready.append(m)
                yield
            last = [PE.last(), V.last(), m_qe]
            for s in (dec, erow, qe, vb, kd, xn, am):
                c.scratch.give(s, *last)
        pipelined((tile(i) for i in range(NT)), 1)
        c.barrier()

    sums = c.banks.take()
    for h in range(H):
        sq, m = c.square_tile(c.mixed[:, h, :], c.mixed_ready)
        PE.after(m, *sums.free)
        m = PE.run(nc.tensor.matmul(sums.buf[0:8, :], c.const("strip")[:, 15 - h:23 - h], sq.buf[:],
                                    start=h == 0, stop=h == H - 1))
        c.scratch.give(sq, m)
    rows = c.scratch.take()
    A.after(m, *rows.free)
    m = A.run(nc.scalar.activation(rows.buf[0:8, :], sums.buf[0:8, :], ACT.Sqrt, bias=c.eps[0:8, 0:1], scale=1.0 / GD))
    c.banks.give(sums, m)
    V.after(m)
    mr = V.run(nc.vector.reciprocal(rows.buf[0:8, :], rows.buf[0:8, :]))
    done = []
    for hf in range(H // 2):
        slot = c.weight_chunk(w_in, 3 * H * GD + hf * 256, 256)
        for m_ in range(2):
            h = 2 * hf + m_
            zb, m = c.feature_product(slot, m_, c.hT, KD, c.h_ready)
            z = c.scratch.take()
            A.after(m, *z.free)
            m = A.run(nc.scalar.activation(z.buf[:], zb.buf[:], ACT.Silu))
            c.banks.give(zb, m)
            bank = c.banks.take()
            PE.after(mr, *bank.free)
            m1 = PE.run(nc.tensor.matmul(bank.buf[:], c.const("ident", 8)[:, h:h + 1].to_broadcast([8, P]),
                                         rows.buf[0:8, :], start=True, stop=True))
            V.after(m1)
            m1 = V.run(nc.vector.scalar_tensor_tensor(out=c.mixed[:, h, :], in0=c.mixed[:, h, :],
                                                      scalar=c.col["gdn_norm"], in1=bank.buf[:],
                                                      op0=ALU.mult, op1=ALU.mult))
            c.banks.give(bank, m1)
            V.after(m, m1)
            m = V.run(nc.vector.tensor_tensor(c.mixed[:, h, :], c.mixed[:, h, :], z.buf[:], ALU.mult))
            c.scratch.give(z, m)
            done.append(m)
        c.weights.give(slot, PE.last())
    c.scratch.give(rows, PE.last())
    c.h_free = [PE.last()]
    c.mixed_ready = done
    c.barrier()
    c.scratch.slots = [s for s in c.scratch.slots if s in c.own_scratch]


def build(nc, io, at, out):
    with ExitStack() as ctx:
        c = Core(nc, ctx, io, at)
        c.own_scratch = list(c.scratch.slots)
        c.negmax = c.sb("negmax", [P, GROUPS, NT, DIL_H])
        c.den = c.sb("den", [P, GROUPS, NT, DIL_H])
        c.gate_cols = c.sb("gate_cols", [P, 8, NT, H])
        c.state = c.sb("state", [P, 4, GD])
        dram = lambda name, shape: nc.dram_tensor(name, shape, F32).ap()
        c.h2_dram, c.y_dram = dram("h2_dram", [S, D]), dram("y_dram", [NBLK * P, D])
        c.table_dram = dram("table_dram", [NBLK * P, 1])
        setup(c)
        c.mixed_ready = []
        c.norm_residual(lambda k: columns(c.col["norm_attn"], k))
        dilated(c)
        mla(c)
        merge(c)
        c.norm_residual(lambda k: columns(c.col["norm_ffn"], k))
        moe(c)
        for layer in range(2):
            c.modulation(layer)
            mod = lambda part, layer=layer: (lambda k: c.mod[:, layer, part, k:k + 1])
            c.DVE.after(c.mod_ready)
            c.ACT.after(c.mod_ready)
            c.norm_residual(mod(1), mod(0))
            (head_groups if layer == 0 else delta_net)(c)
            w = io["attn_w_out_2"] if layer == 0 else io["gdn_w_out_2"]
            project_out(c, w, c.mixed, KD, c.mixed_ready, gate=mod(2))
            c.norm_residual(mod(4), mod(3))
            swiglu(c, layer)
        c.norm_residual(lambda k: columns(c.col["final"], k))
        sem = c.sem("out_done")
        for k in range(KD):
            c.SP.after(c.h_ready[k])
            nc.sync.dma_start(out[k * P:(k + 1) * P, :], c.hT[:, k, :]).then_inc(sem, 16)
        nc.sync.wait_ge(sem, 16 * KD)


def kernel(**inputs):
    import concourse.bacc as bacc
    from concourse.bass_utils import run_bass_kernel_spmd

    a = {k: np.asarray(v) for k, v in inputs.items()}
    table, at = constants()
    cols = lambda v: np.ascontiguousarray(v.reshape(-1, P).T)
    twice = lambda v: np.ascontiguousarray(np.concatenate([v, v], -1).T)
    arrays = {
        "consts": table,
        "xT": np.ascontiguousarray(a["x"][0].T),
        "col_norm_attn": cols(a["norm_attn"]), "col_norm_ffn": cols(a["norm_ffn"]),
        "col_b_gate": cols(a["b_gate"]), "col_norm_ckv": cols(a["norm_ckv"]),
        "col_norm_mix": cols(a["norm_mix_g_2"]), "col_norm_ffn2": cols(a["norm_ffn_g_2"]),
        "col_final": cols(a["final_norm_g_2"]), "col_c": cols(a["c_2"]), "col_gdn_norm": cols(a["gdn_norm_g_2"]),
        "col_qdil": twice(a["q_norm_dil"][0]), "col_kdil": twice(a["k_norm_dil"][0]),
        "col_ada_b": np.ascontiguousarray(a["ada_b_2"].reshape(2, 6 * KD, P).transpose(2, 0, 1)),
        "col_conv": np.ascontiguousarray(a["gdn_conv_w_2"][0].reshape(CONV, 3 * H, P).transpose(2, 0, 1)),
        "col_pos": np.ascontiguousarray(np.concatenate([a["positions"].reshape(NT, P).T,
                                                        a["positions_2"].reshape(NT, P).T], 1)),
        "row_qmla": a["q_norm_mla"][0], "row_kmla": a["k_norm_mla"][0], "row_b_rg": a["b_router_group"][0],
        "row_b_re": a["b_router_expert"][0], "row_a_log": a["gdn_a_log_2"][0], "row_dt_bias": a["gdn_dt_bias_2"][0],
    }
    for name in ("w_in", "w_ukv", "w_o_mla", "w_o_dil", "w_out", "w_router_group", "w_router_expert", "w_gate",
                 "w_up", "w_down", "attn_w_in_2", "attn_w_out_2", "gdn_w_in_2", "gdn_w_out_2"):
        arrays[name] = a[name][0]
    for name in ("ada_w_2", "ffn_w_in_2", "ffn_w_out_2"):
        arrays[name] = a[name]
    nc = bacc.Bacc("TRN2", target_bir_lowering=False, num_devices=1)
    io = {n: nc.dram_tensor(n, v.shape, mybir.dt.from_np(v.dtype), kind="ExternalInput").ap()
          for n, v in arrays.items()}
    out = nc.dram_tensor("outT", [D, S], F32, kind="ExternalOutput").ap()
    build(nc, io, at, out)
    got = run_bass_kernel_spmd(nc, [arrays], core_ids=[0]).results[0]["outT"]
    return np.ascontiguousarray(got.T).reshape(1, S, D)
```

```python
from contextlib import ExitStack

import numpy as np
import concourse.bass as bass
from concourse import mybir

F32 = mybir.dt.float32
I32 = mybir.dt.int32
U32 = mybir.dt.uint32
ALU = mybir.AluOpType
ACT = mybir.ActivationFunctionType
AX = mybir.AxisListType

P = 128
S = 512
NT = S // P
D = 1024
KD = D // P
EPS = 1e-6
NEG = -1e30

MLA_H, NOPE, ROPE, MLA_V, KV_RANK = 8, 64, 32, 64, 256
MLA_D = NOPE + ROPE
GROUPS, DIL_H, HD = 3, 8, 64
DIL = (1, 4, 16)
STRIDE = S // P
N_GRP, PER_GRP = 4, 8
NE = N_GRP * PER_GRP
FF = 256
NBLK = 2 * S // P + NE - 1
H = 8
ROPE2 = HD // 4
GD = 128
CONV = 4
CHUNK = 64
LEVELS = 6
HID = -(-8 * D // (3 * 256)) * 256
KH = HID // P

C_MLAQ = 0
C_CKV = MLA_H * MLA_D
C_DIL = C_CKV + KV_RANK + ROPE
C_GATE = C_DIL + 3 * GROUPS * DIL_H * HD


def constants():
    r = np.arange(P)
    part, col = r[:, None], r[None, :]
    chunk = part // CHUNK == col // CHUNK
    strip = np.zeros((P, 31), np.float32)
    strip[:, 15] = 1
    i, j = r[:, None], np.arange(2 * P)[None, :]
    delta = i + P - j
    far = -NEG
    dist0 = np.where((delta >= 0) & (delta <= P), delta, far)
    dist1 = np.where(col <= part, (part - col) * DIL[1], far)
    same = (part - col) % (DIL[2] // STRIDE) == 0
    dist2 = np.where(same & (col <= part), (part - col) * STRIDE, far)
    slopes = 2.0 ** (-8.0 * (np.arange(DIL_H) + 1.0) / DIL_H)
    levels = [((col >> l) % 2 == 1) & ((part >> l) % 2 == 0) & (col >> (l + 1) == part >> (l + 1))
              for l in range(LEVELS)]
    half, half2 = ROPE // 2, ROPE2 // 2
    f1 = np.float32(10000.0) ** (-np.arange(half, dtype=np.float32) / np.float32(half))
    f2 = np.float32(500000.0) ** (-np.arange(half2, dtype=np.float32) * np.float32(2.0) / np.float32(ROPE2))
    parts = {
        "ident": np.eye(P), "ones": np.ones((P, P)),
        "before": part < col,
        "chunk_upto": chunk & (part <= col),
        "chunk_all": chunk,
        "neg_from": -(part >= col).astype(np.float32),
        "neg_ones": -np.ones((P, P)),
        "sb_keep": part < col,
        "sb_mask": np.where(part < col, 0.0, NEG),
        "causal": np.where(col <= part, 0.0, NEG),
        "levels": np.concatenate(levels, 1),
        "strip": strip,
        "freq1": np.tile(f1, (P, 1)), "freq2": np.tile(f2, (P, 1)),
        "expert": np.tile(np.arange(NE), (P, 1)), "group": np.tile(np.arange(8), (P, 1)),
        "block": np.tile(np.arange(NBLK), (P, 1)),
        "thresholds": np.tile(P * np.arange(NT), (P, 1)),
        "token": r[:, None] + P * np.arange(NT)[None, :],
        "dist0": dist0, "dist1": dist1, "dist2": dist2,
        "slope": np.concatenate([-s * np.eye(P) for s in slopes], 1),
    }
    at, n, out = {}, 0, []
    for name, a in parts.items():
        a = np.asarray(a, np.float32)
        at[name] = (n, a.shape[1])
        n += a.shape[1]
        out.append(a)
    return np.ascontiguousarray(np.concatenate(out, 1)), at


def offsets(widths):
    out, at = {}, 0
    for name, n in widths:
        out[name] = (at, n)
        at += n
    return out


COLS = offsets([("norm_attn", KD), ("norm_ffn", KD), ("b_gate", 2 * KD), ("norm_ckv", KV_RANK // P),
                ("norm_mix", 2 * KD), ("norm_ffn2", 2 * KD), ("final", KD), ("c", KD), ("gdn_norm", 1),
                ("qdil", GROUPS), ("kdil", GROUPS), ("ada_b", 2 * 6 * KD), ("conv", CONV * 3 * H)])
ROWS = offsets([("qmla", MLA_D), ("kmla", MLA_D), ("b_rg", N_GRP), ("b_re", NE), ("a_log", H), ("dt_bias", H)])


class Queue:

    def __init__(self, engine, sem):
        self.engine, self.sem, self.count, self.waited = engine, sem, 0, {}

    def after(self, *marks):
        for sem, value in marks:
            if self.waited.get(sem.name, 0) < value:
                self.engine.wait_ge(sem, value)
                self.waited[sem.name] = value
        return self

    def run(self, instruction):
        instruction.then_inc(self.sem, 1)
        self.count += 1
        return self.sem, self.count

    def last(self):
        return (self.sem, self.count) if self.count else None


class Slot:

    def __init__(self, buf):
        self.buf, self.free = buf, []


class Ring:

    def __init__(self, bufs):
        self.slots = [Slot(b) for b in bufs]

    def take(self):
        return self.slots.pop(0)

    def give(self, slot, *marks):
        slot.free = list(marks)
        self.slots.append(slot)


class Loads:

    def __init__(self, queue, bufs, sems):
        self.queue = queue
        self.ring = Ring(bufs)
        self.sems = dict(zip([id(s) for s in self.ring.slots], sems))
        self.counts = {id(s): 0 for s in self.ring.slots}

    def load(self, view, source, *marks):
        slot = self.ring.take()
        self.queue.after(*slot.free, *marks)
        self.queue.engine.dma_start(view(slot.buf), source).then_inc(self.sems[id(slot)], 16)
        self.counts[id(slot)] += 16
        slot.ready = (self.sems[id(slot)], self.counts[id(slot)])
        return slot

    def give(self, slot, *marks):
        self.ring.give(slot, *marks)


def pipelined(jobs, depth, background=None, every=1):
    jobs, live = iter(jobs), []
    more, rounds = True, 0
    while more or live:
        rounds += 1
        if more and len(live) < depth and (rounds % every == 0 or not live):
            job = next(jobs, None)
            more = job is not None
            if more:
                live.append(job)
        going = {id(j): next(j, "done") != "done" for j in reversed(live)}
        live = [j for j in live if going[id(j)]]
        if background is not None:
            background()


class Core:

    def __init__(self, nc, ctx, io, at):
        self.nc, self.ctx, self.io, self.at = nc, ctx, io, at
        self.nsem = 0
        self.PE = Queue(nc.tensor, self.sem("pe_done"))
        self.ACT = Queue(nc.scalar, self.sem("act_done"))
        self.DVE = Queue(nc.vector, self.sem("dve_done"))
        self.POOL = Queue(nc.gpsimd, self.sem("pool_done"))
        self.SP = Queue(nc.sync, self.sem("sp_done"))
        self.banks = Ring([ctx.enter_context(nc.psum_tensor(f"bank{i}", [P, 512], F32)) for i in range(8)])
        nw = 7
        self.weights = Loads(self.SP, [self.sb(f"weights{i}", [P, 2048]) for i in range(nw)],
                             [self.sem(f"weights{i}_in") for i in range(nw)])
        self.scratch = Ring([self.sb(f"scratch{i}", [P, 512]) for i in range(13)])
        self.small = Ring([self.sb(f"small{i}", [P, 32]) for i in range(12)])
        self.xT = self.sb("xT", [P, KD, S])
        self.hT = self.sb("hT", [P, KD, S])
        self.arena = self.sb("arena", [P, 24 * S])
        self.mixed = self.sb("mixed", [P, KD, S])
        self.mod = self.sb("mod", [P, 2, 6, KD])
        self.cols = self.sb("cols", [P, sum(n for _, n in COLS.values())])
        self.x_ready = [[] for _ in range(KD)]
        self.h_ready = []
        self.h_free = []
        self.later = []
        self.padded = Ring([self.sb(f"padded_q{i}", [P, H, P]) for i in range(2)])

    def sem(self, name):
        return self.ctx.enter_context(self.nc.semaphore(name))

    def sb(self, name, shape, dt=F32):
        return self.ctx.enter_context(self.nc.sbuf_tensor("sb_" + name, shape, dt))

    def const(self, name, rows=P):
        a, n = self.at[name]
        if a >= self.at["dist0"][0]:
            a -= self.at["dist0"][0]
            return self.mixed[:, 0:3, :].rearrange("p a t -> p (a t)")[0:rows, a:a + n]
        return self.consts[0:rows, a:a + n]

    def barrier(self):
        marks = [q.last() for q in (self.PE, self.ACT, self.DVE, self.POOL) if q.last()]
        for q in (self.PE, self.ACT, self.DVE, self.POOL):
            q.after(*marks)

    def load_once(self, queue, dst, src, name):
        sem = self.sem(name)
        queue.engine.dma_start(dst, src).then_inc(sem, 16)
        return sem, 16

    def weight_chunk(self, w, c0, n, kt=KD, k0=0):
        src = w[k0 * P:(k0 + kt) * P, c0:c0 + n].rearrange("(k p) n -> p k n", p=P)
        slot = self.weights.load(lambda b: b[:, 0:kt * n].rearrange("p (k n) -> p k n", k=kt), src)
        slot.w = slot.buf[:, 0:kt * n].rearrange("p (k n) -> p k n", k=kt)
        return slot

    def feature_product(self, slot, m, actT, kt, marks, bank=None, first=True, last=True):
        nc, PE = self.nc, self.PE
        if bank is None:
            bank = self.banks.take()
            PE.after(*bank.free)
        PE.after(slot.ready, *marks)
        for k in range(kt):
            mm = nc.tensor.matmul(bank.buf[:], slot.w[:, k, m * P:(m + 1) * P], actT[:, k, :],
                                  start=first and k == 0, stop=last and k == kt - 1)
        return bank, PE.run(mm)

    def token_product(self, slot, n, toks, kt, marks, c0=0, bank=None, at=0):
        nc, PE = self.nc, self.PE
        if bank is None:
            bank = self.banks.take()
            PE.after(*bank.free)
        PE.after(slot.ready, *marks)
        for k in range(kt):
            mm = nc.tensor.matmul(bank.buf[:, at:at + n], toks(k), slot.w[:, k, c0:c0 + n],
                                  start=k == 0, stop=k == kt - 1)
        return bank, PE.run(mm)

    def inv_rms_rows(self, squares, n, width):
        nc, PE, A, V = self.nc, self.PE, self.ACT, self.DVE
        bank = self.banks.take()
        PE.after(*bank.free)
        for k in range(n):
            sq, mark = squares(k)
            PE.after(mark)
            mm = PE.run(nc.tensor.matmul(bank.buf[:], self.const("ones"), sq.buf[:],
                                         start=k == 0, stop=k == n - 1))
            self.scratch.give(sq, mm)
        rms = self.scratch.take()
        A.after(mm, *rms.free)
        got = A.run(nc.scalar.activation(rms.buf[:], bank.buf[:], ACT.Sqrt, bias=self.eps[:, 0:1], scale=1.0 / width))
        self.banks.give(bank, got)
        V.after(got)
        return rms, V.run(nc.vector.reciprocal(rms.buf[:], rms.buf[:]))

    def square_tile(self, src, marks):
        sq = self.scratch.take()
        self.ACT.after(*marks, *sq.free)
        return sq, self.ACT.run(self.nc.scalar.activation(sq.buf[:], src, ACT.Square))

    def norm_residual(self, gain, shift=None, out=None):
        nc, V, A = self.nc, self.DVE, self.ACT
        out = self.hT if out is None else out
        inv, ready = self.inv_rms_rows(lambda k: self.square_tile(self.xT[:, k, :], self.x_ready[k]), KD, D)
        V.after(ready, *self.h_free)
        self.h_ready = []
        for k in range(KD):
            done = V.run(nc.vector.scalar_tensor_tensor(out=out[:, k, :], in0=self.xT[:, k, :], scalar=gain(k),
                                                        in1=inv.buf[:], op0=ALU.mult, op1=ALU.mult))
            if shift is not None:
                A.after(done)
                done = A.run(nc.scalar.activation(out[:, k, :], out[:, k, :], ACT.Identity, bias=shift(k)))
            self.h_ready.append(done)
        self.scratch.give(inv, V.last())

    def inv_rms_small(self, sums, width, mark, eps=True):
        nc, A, V = self.nc, self.ACT, self.DVE
        A.after(mark)
        got = A.run(nc.scalar.activation(sums, sums, ACT.Sqrt, bias=self.eps[:, 0:1], scale=1.0 / width))
        V.after(got)
        return V.run(nc.vector.reciprocal(sums, sums))

    def head_norm(self, src, heads, width, out, marks):
        nc, A, V = self.nc, self.ACT, self.DVE
        sq, ss = self.scratch.take(), self.small.take()
        A.after(*marks, *sq.free)
        sq3 = sq.buf[:, 0:heads * width].rearrange("p (h d) -> p h d", h=heads)
        m = A.run(nc.scalar.activation(sq3, src, ACT.Square))
        V.after(m, *ss.free)
        m = V.run(nc.vector.tensor_reduce(ss.buf[:, 0:heads], sq3, AX.X, ALU.add))
        self.scratch.give(sq, m)
        m = self.inv_rms_small(ss.buf[:, 0:heads], width, m)
        V.after(m)
        scale = ss.buf[:, 0:heads].unsqueeze(2).to_broadcast([P, heads, width])
        m = V.run(nc.vector.tensor_tensor(out, src, scale, ALU.mult))
        self.small.give(ss, m)
        return m

    def rope(self, t1, t2, cos, sin, heads, half, marks):
        nc, G = self.nc, self.POOL
        tmp = self.scratch.take()
        n = heads * half
        view = lambda i: tmp.buf[:, i * n:(i + 1) * n].rearrange("p (h d) -> p h d", h=heads)
        cosb = cos.unsqueeze(1).to_broadcast([P, heads, half])
        sinb = sin.unsqueeze(1).to_broadcast([P, heads, half])
        G.after(*marks, *tmp.free)
        for i, (t, f) in enumerate(((t1, cosb), (t2, sinb), (t2, cosb), (t1, sinb))):
            m = G.run(nc.gpsimd.tensor_tensor(view(i), t, f, ALU.mult))
        G.after(m)
        G.run(nc.gpsimd.tensor_tensor(t1, view(0), view(1), ALU.subtract))
        m = G.run(nc.gpsimd.tensor_tensor(t2, view(2), view(3), ALU.add))
        self.scratch.give(tmp, m)
        return m

    def transpose_blocks(self, blocks, rows, marks):
        nc, PE = self.nc, self.PE
        bank = self.banks.take()
        PE.after(*bank.free, *marks)
        for i, b in enumerate(blocks):
            mm = nc.tensor.transpose(bank.buf[0:rows, i * P:(i + 1) * P], b, self.const("ident"))
        return bank, PE.run(mm)

    def copy(self, out, src, marks, on=None):
        self.turn = not self.turn
        if on == "act" or (on is None and self.turn):
            self.ACT.after(*marks)
            return self.ACT.run(self.nc.scalar.copy(out, src))
        self.DVE.after(*marks)
        return self.DVE.run(self.nc.vector.tensor_copy(out, src))

    turn = False

    def add_residual(self, bank, m, j, gate=None):
        nc, V = self.nc, self.DVE
        V.after(m, *self.x_ready[j])
        x = self.xT[:, j, :]
        if gate is None:
            done = V.run(nc.vector.tensor_tensor(x, bank.buf[:], x, ALU.add))
        else:
            done = V.run(nc.vector.scalar_tensor_tensor(out=x, in0=bank.buf[:], scalar=gate, in1=x,
                                                        op0=ALU.mult, op1=ALU.add))
        self.banks.give(bank, done)
        self.x_ready[j] = [done]

    def idle(self):
        while self.later and next(self.later[0], "done") == "done":
            self.later.pop(0)

    def finish_background(self):
        while self.later:
            self.idle()

    def softmax_job(self, query, k, blocks, bias, scale, values, out, negmax, den, marks, done):
        nc, PE, A, V = self.nc, self.PE, self.ACT, self.DVE
        n = blocks * P
        bank = self.banks.take()
        q, q_marks = query()
        PE.after(*bank.free, *marks, *q_marks)
        nc.tensor.matmul(bank.buf[:, 0:n], q, k, start=True, stop=False)
        for i, (left, right, c) in enumerate(bias):
            w = right.shape[-1]
            mm = nc.tensor.matmul(bank.buf[:, c:c + w], left, right, start=False, stop=i == len(bias) - 1)
        m = PE.run(mm)
        V.after(m)
        m = V.run(nc.vector.tensor_reduce(negmax, bank.buf[:, 0:n], AX.X, ALU.max, negate=True))
        if scale != 1.0:
            V.after(m)
            m = V.run(nc.vector.tensor_scalar(negmax, negmax, scale, None, ALU.mult))
        p = self.scratch.take()
        A.after(m, *p.free)
        m = A.run(nc.scalar.activation(p.buf[:, 0:n], bank.buf[:, 0:n], ACT.Exp, bias=negmax, scale=scale,
                                       accum_out=den))
        self.banks.give(bank, m)
        yield
        yield
        tbank, m = self.transpose_blocks([p.buf[:, b * P:(b + 1) * P] for b in range(blocks)], P, [m])
        self.scratch.give(p, m)
        pT = self.scratch.take()
        m = self.copy(pT.buf[:, 0:n], tbank.buf[:, 0:n], [m, *pT.free])
        self.banks.give(tbank, m)
        yield
        yield
        target = out()
        PE.after(m)
        for b in range(blocks):
            mm = nc.tensor.matmul(target, pT.buf[:, b * P:(b + 1) * P], values(b), start=b == 0, stop=b == blocks - 1)
        m = PE.run(mm)
        self.scratch.give(pT, m)
        yield from done(m)

    def pad_queries(self, q, cols, marks):
        slot = self.padded.take()
        done = [self.copy(slot.buf[rows, r:H:2, :], q[rows, :, cols], [*slot.free, *marks])
                for r, rows in enumerate((slice(0, HD), slice(HD, P)))]
        return slot, done

    def head_pair_banks(self):
        pair = self.banks.take(), self.banks.take()
        self.PE.after(*pair[0].free, *pair[1].free)
        return pair

    @staticmethod
    def pair_columns(pair, h):
        return pair[h % 2].buf[:, (h // 2) * P:(h // 2 + 1) * P]

    @staticmethod
    def kept(buf, r):
        return buf.rearrange("p (a r d) -> p a r d", a=4, r=2)[:, :, r, :]

    def angles(self, pos, freq, n, cos, sin):
        nc, V, A = self.nc, self.DVE, self.ACT
        PI = float(np.float32(3.1415925))
        TWO_PI, ROUND = 6.283185307179586, 12582912.0
        parts = [6.28125, 0.0019350051879882812, TWO_PI - 6.28125 - 0.0019350051879882812]
        a, t, r = self.scratch.take(), self.scratch.take(), self.scratch.take()
        V.after(*a.free, *t.free, *r.free)
        w = NT * n
        for i in range(NT):
            m = V.run(nc.vector.tensor_scalar(a.buf[:, i * n:(i + 1) * n], freq, pos[:, i:i + 1], None, ALU.mult))
        for out, turn, add in ((sin, 0.0, 0.0), (cos, 0.25, TWO_PI / 4)):
            V.after(m)
            m = V.run(nc.vector.tensor_scalar(t.buf[:, 0:w], a.buf[:, 0:w], 1 / TWO_PI, turn, ALU.mult, ALU.add))
            V.after(m)
            m = V.run(nc.vector.tensor_scalar(t.buf[:, 0:w], t.buf[:, 0:w], ROUND, None, ALU.add))
            V.after(m)
            m = V.run(nc.vector.tensor_scalar(t.buf[:, 0:w], t.buf[:, 0:w], -ROUND, None, ALU.add))
            src = a
            for c in parts:
                V.after(m)
                m = V.run(nc.vector.scalar_tensor_tensor(out=r.buf[:, 0:w], in0=t.buf[:, 0:w], scalar=-c,
                                                         in1=src.buf[:, 0:w], op0=ALU.mult, op1=ALU.add))
                src = r
            V.after(m)
            m = V.run(nc.vector.tensor_scalar(r.buf[:, 0:w], r.buf[:, 0:w], float(add), PI, ALU.add, ALU.min))
            V.after(m)
            m = V.run(nc.vector.tensor_scalar(r.buf[:, 0:w], r.buf[:, 0:w], -PI, None, ALU.max))
            A.after(m)
            m = A.run(nc.scalar.activation(out.rearrange("p t f -> p (t f)"), r.buf[:, 0:w], ACT.Sin))
        for s in (a, t, r):
            self.scratch.give(s, m)
        return m

    def modulation(self, layer):
        nc, PE, V = self.nc, self.PE, self.DVE
        W = 256
        out = self.mod[:, layer, :, :].rearrange("p s k -> p (s k)")
        for c in range(6 * D // W):
            slot = self.weight_chunk(self.io["ada_w_2"][layer], c * W, W)
            acc = self.scratch.take()
            V.after(slot.ready, *acc.free, self.cond_ready)
            m = V.run(nc.vector.tensor_scalar(acc.buf[:, 0:W], slot.w[:, 0, :], self.cond[:, 0:1], None, ALU.mult))
            for k in range(1, KD):
                V.after(m)
                m = V.run(nc.vector.scalar_tensor_tensor(out=acc.buf[:, 0:W], in0=slot.w[:, k, :],
                                                         scalar=self.cond[:, k:k + 1], in1=acc.buf[:, 0:W],
                                                         op0=ALU.mult, op1=ALU.add))
                if k % 4 == 3 and k < KD - 1:
                    yield
            self.weights.give(slot, m)
            yield
            bank = self.banks.take()
            PE.after(m, *bank.free)
            for j in range(W // P):
                mm = nc.tensor.matmul(bank.buf[:, j * P:(j + 1) * P], acc.buf[:, j * P:(j + 1) * P],
                                      self.const("ones"), start=True, stop=True)
            m = PE.run(mm)
            self.scratch.give(acc, m)
            V.after(m)
            n = W // P
            m = V.run(nc.vector.tensor_tensor(out[:, c * n:(c + 1) * n],
                                              bank.buf[:, 0:W].rearrange("p (j t) -> p j t", j=n)[:, :, 0],
                                              self.ada_b[:, layer, c * n:(c + 1) * n], ALU.add))
            self.banks.give(bank, m)
            yield
        for s, g in ((1, self.col["norm_mix"]), (4, self.col["norm_ffn2"])):
            V.after(m)
            gain = g[:, layer * KD:(layer + 1) * KD]
            m = V.run(nc.vector.scalar_tensor_tensor(out=self.mod[:, layer, s, :], in0=self.mod[:, layer, s, :],
                                                     scalar=1.0, in1=gain, op0=ALU.add, op1=ALU.mult))
        self.mod_ready = m


def setup(c):
    nc, io = c.nc, c.io
    ncst = c.at["dist0"][0]
    c.consts = c.sb("consts", [P, ncst])
    c.consts_in = c.load_once(c.SP, c.consts[:], io["consts"][:, 0:ncst], "consts_in")
    x_in = [c.load_once(c.SP, c.xT[:, k, :], io["xT"][k * P:(k + 1) * P, :], f"x{k}_in") for k in range(KD)]
    c.dilated_consts_in = c.load_once(c.SP, c.mixed[:, 0:3, :].rearrange("p a t -> p (a t)"),
                                      io["consts"][:, ncst:], "dilated_consts_in")
    c.x_ready = [[m] for m in x_in]
    c.col = {name: c.cols[:, i:i + n] for name, (i, n) in COLS.items()}
    c.ada_b = c.col["ada_b"].rearrange("p (l j) -> p l j", l=2)
    c.conv_w = c.col["conv"].rearrange("p (t j) -> p t j", t=CONV)
    nrow = sum(n for _, n in ROWS.values())
    c.rows = c.sb("rows", [P, nrow])
    c.row = {name: c.rows[:, i:i + n] for name, (i, n) in ROWS.items()}
    c.pos = c.sb("pos", [P, 2 * NT], I32)
    sem = c.sem("parameters_in")
    for dst, src in ((c.cols[:], io["cols"]), (c.rows[:], io["rows"].partition_broadcast(P)), (c.pos[:], io["positions"])):
        nc.gpsimd.dma_start(dst, src).then_inc(sem, 16)
    c.small_in = (sem, 48)
    c.eps = c.sb("eps", [P, 1])
    c.posf = c.sb("posf", [P, 2 * NT])
    c.cos1, c.sin1 = c.sb("cos1", [P, NT, ROPE // 2]), c.sb("sin1", [P, NT, ROPE // 2])
    c.cos2, c.sin2 = c.sb("cos2", [P, NT, ROPE2 // 2]), c.sb("sin2", [P, NT, ROPE2 // 2])
    m = c.DVE.run(nc.vector.memset(c.eps[:], EPS))
    c.PE.after(c.consts_in)
    c.ACT.after(m)
    for slot in c.padded.slots:
        slot.free = [c.POOL.run(nc.gpsimd.memset(slot.buf[:], 0.0))]
    c.DVE.after(c.consts_in, c.small_in)
    c.ACT.after(c.small_in)
    c.POOL.after(c.small_in, c.consts_in)


def setup_tables(c):
    nc = c.nc
    m = c.DVE.run(nc.vector.tensor_copy(c.posf[:], c.pos[:]))
    m = c.DVE.run(nc.vector.tensor_scalar(c.col["qdil"], c.col["qdil"], HD ** -0.5, None, ALU.mult))
    c.DVE.after(m)
    c.ACT.after(m)
    c.cond = c.sb("cond", [P, KD])
    c.cond_ready = c.ACT.run(nc.scalar.activation(c.cond[:], c.col["c"], ACT.Silu))
    c.angles(c.posf[:, 0:NT], c.const("freq1"), ROPE // 2, c.cos1[:], c.sin1[:])
    c.rope_ready = c.angles(c.posf[:, NT:2 * NT], c.const("freq2"), ROPE2 // 2, c.cos2[:], c.sin2[:])


def columns(table, j):
    return table[:, j:j + 1]


def folded(g, i):
    return slice(i * P, (i + 1) * P) if g == 0 else slice(i, S, STRIDE)


def fold(c, g, i):
    return lambda k: c.hT[:, k, folded(g, i)]


def dilated(c):
    nc, PE, A, V, G = c.nc, c.PE, c.ACT, c.DVE, c.POOL
    w_in = c.io["w_in"]
    WD = DIL_H * HD
    q, k, v = (c.arena[:, j * 4 * S:(j + 1) * 4 * S].rearrange("p (a t) -> p a t", a=4) for j in range(3))
    outs = [c.arena[:, (3 + g) * 4 * S:(4 + g) * 4 * S].rearrange("p (a t) -> p a t", a=4) for g in range(GROUPS)]
    negmax, den = c.negmax, c.den
    c.PE.after(c.dilated_consts_in)
    free = []
    for g in range(GROUPS):
        ready = []

        def projections(g=g, ready=ready, free=free):
            for part, dst in ((0, q), (1, k), (2, v)):
                for half in range(2):
                    slot = c.weight_chunk(w_in, C_DIL + (part * GROUPS + g) * WD + half * 256, 256)
                    for i in range(NT):
                        yield tile(i, slot, half, dst, part, g, ready, free)

        def tile(i, slot, half, dst, part, g, ready, free):
            heads = DIL_H // 2
            bank, m = c.token_product(slot, 256, fold(c, g, i), KD, c.h_ready)
            if i == NT - 1:
                c.weights.give(slot, m)
            yield
            if part == 2:
                m = c.copy(v[:, i, half * 256:(half + 1) * 256], bank.buf[:, 0:256], [m, *free])
                c.banks.give(bank, m)
                ready.append(m)
                return
            n = c.scratch.take()
            V.after(*n.free)
            src = bank.buf[:, 0:256].rearrange("p (h d) -> p h d", h=heads)
            m = c.head_norm(src, heads, HD, n.buf[:, 0:256].rearrange("p (h d) -> p h d", h=heads), [m])
            c.banks.give(bank, m)
            yield
            yield
            tb, m = c.transpose_blocks([n.buf[:, j * P:(j + 1) * P] for j in range(2)], P, [m])
            c.scratch.give(n, m)
            gain = columns(c.col["qdil" if part == 0 else "kdil"], g)
            A.after(m, *free)
            m = A.run(nc.scalar.activation(dst[:, 2 * half:2 * half + 2, i * P:(i + 1) * P],
                                           tb.buf[:, 0:256].rearrange("p (a t) -> p a t", a=2),
                                           ACT.Identity, scale=gain))
            c.banks.give(tb, m)
            ready.append(m)
        pipelined(projections(), 4, c.idle)

        last = []

        def heads_of(g=g, ready=ready, last=last):
            for i in range(NT):
                lo = i - 1 if g == 0 and i > 0 else i
                tile_ = {}
                for h in range(DIL_H):
                    yield head(g, i, lo, h, tile_, ready, last)

        def head(g, i, lo, h, t, ready, last):
            blocks = i - lo + 1
            dist = c.const(f"dist{g}")
            bias = [(c.const("slope")[:, h * P:(h + 1) * P], dist[:, (2 - blocks) * P:] if g == 0 else dist, 0)]

            def query():
                if h == 0:
                    t["q"], t["q_in"] = c.pad_queries(q, slice(i * P, (i + 1) * P), ready)
                return t["q"].buf[:, h, :], t["q_in"]

            def out():
                if h == 0:
                    t["out"] = c.head_pair_banks()
                if h == DIL_H - 1:
                    c.padded.give(t["q"], c.PE.last())
                return c.pair_columns(t["out"], h)

            def done(m):
                if h < DIL_H - 1:
                    return
                for r in range(2):
                    mc = c.copy(c.kept(outs[g][:, i, :], r), c.kept(t["out"][r].buf[:], r), [m])
                    c.banks.give(t["out"][r], mc)
                    last.append(mc)
                last.append(m)
                yield
            return c.softmax_job(query, k[:, h // 2, lo * P:(i + 1) * P], blocks, bias, 1.0,
                                 lambda b: v[:, lo + b, (h // 2) * P:(h // 2 + 1) * P], out,
                                 negmax[:, g, i, h:h + 1], den[:, g, i, h:h + 1], ready, done)
        pipelined(heads_of(), 6, c.idle)
        free = last
    t8 = c.arena[0:DIL_H, 0:7 * S].rearrange("p (a t) -> p a t", a=7)
    c.barrier()
    for n, src in enumerate((negmax, den)):
        for g in range(GROUPS):
            bank = c.banks.take()
            PE.after(*bank.free)
            for i in range(NT):
                mm = nc.tensor.transpose(bank.buf[0:DIL_H, i * P:(i + 1) * P], src[:, g, i, :], c.const("ident"))
            m = PE.run(mm)
            for i in range(NT):
                V.after(m)
                m = V.run(nc.vector.tensor_copy(t8[:, n * GROUPS + g, folded(g, i)],
                                             bank.buf[0:DIL_H, i * P:(i + 1) * P]))
            c.banks.give(bank, m)
    low = t8[:, 6, :]
    V.after(m)
    m = V.run(nc.vector.tensor_tensor(low, t8[:, 0, :], t8[:, 1, :], ALU.min))
    V.after(m)
    m = V.run(nc.vector.tensor_tensor(low, low, t8[:, 2, :], ALU.min))
    for g in range(GROUPS):
        V.after(m)
        m = V.run(nc.vector.tensor_tensor(t8[:, g, :], low, t8[:, g, :], ALU.subtract))
    A.after(m)
    m = A.run(nc.scalar.activation(t8[:, 0:3, :], t8[:, 0:3, :], ACT.Exp))
    V.after(m)
    m = V.run(nc.vector.tensor_tensor(t8[:, 3:6, :], t8[:, 0:3, :], t8[:, 3:6, :], ALU.mult))
    V.after(m)
    m = V.run(nc.vector.tensor_tensor(low, t8[:, 3, :], t8[:, 4, :], ALU.add))
    V.after(m)
    m = V.run(nc.vector.tensor_tensor(low, low, t8[:, 5, :], ALU.add))
    V.after(m)
    m = V.run(nc.vector.reciprocal(low, low))
    V.after(m)
    m = V.run(nc.vector.tensor_tensor(t8[:, 0:3, :], t8[:, 0:3, :],
                                      low.unsqueeze(1).to_broadcast([DIL_H, 3, S]), ALU.mult))
    bank = c.banks.take()
    PE.after(m, *bank.free)
    for g in range(GROUPS):
        for i in range(NT):
            at = (g * NT + i) * DIL_H
            mm = nc.tensor.matmul(bank.buf[:, at:at + DIL_H], t8[:, g, folded(g, i)], c.const("ident", DIL_H)[:, 0:DIL_H],
                                  start=True, stop=True)
    m = PE.run(mm)
    coef = c.scratch.take()
    ncf = GROUPS * NT * DIL_H
    ready = c.copy(coef.buf[:, 0:ncf], bank.buf[:, 0:ncf], [m, *coef.free], "dve")
    c.banks.give(bank, ready)
    written = {}

    def spread(g, i):
        o3 = outs[g][:, i, :].rearrange("p (h d) -> p h d", h=DIL_H)
        at = (g * NT + i) * DIL_H
        cb = coef.buf[:, at:at + DIL_H].unsqueeze(2).to_broadcast([P, DIL_H, HD])
        V.after(ready)
        m = V.run(nc.vector.tensor_tensor(o3, o3, cb, ALU.mult))
        yield
        tb, m = c.transpose_blocks([outs[g][:, i, j * P:(j + 1) * P] for j in range(4)], P, [m])
        yield
        for j in range(4):
            dst, src = c.mixed[:, 4 + j, folded(g, i)], tb.buf[:, j * P:(j + 1) * P]
            if g == 0:
                V.after(m)
                written[j] = V.run(nc.vector.tensor_copy(dst, src))
            else:
                V.after(m, written[j])
                written[j] = V.run(nc.vector.tensor_tensor(dst, src, dst, ALU.add))
        c.banks.give(tb, written[3])
    pipelined((spread(g, i) for g in range(GROUPS) for i in range(NT)), 3)
    c.scratch.give(coef, *written.values())
    c.barrier()


def mla(c):
    nc, PE, A, V, G = c.nc, c.PE, c.ACT, c.DVE, c.POOL
    w_in, w_ukv = c.io["w_in"], c.io["w_ukv"]
    q, k = (c.arena[:, j * 8 * S:(j + 1) * 8 * S].rearrange("p (a t) -> p a t", a=8) for j in range(2))
    v = c.arena[:, 16 * S:20 * S].rearrange("p (a n) -> p a n", a=NT)
    ckvT = c.arena[:, 20 * S:22 * S].rearrange("p (a t) -> p a t", a=2)
    krope = c.arena[:, 22 * S:22 * S + NT * ROPE].rearrange("p (a n) -> p a n", a=NT)
    ready = []

    def finish_heads(n, heads, h0, i, gain, dst, m):
        n3 = n.buf[:, 0:heads * MLA_D].rearrange("p (h d) -> p h d", h=heads)
        G.after(m)
        m = G.run(nc.gpsimd.tensor_tensor(n3, n3, gain.unsqueeze(1).to_broadcast([P, heads, MLA_D]), ALU.mult))
        half = ROPE // 2
        m = c.rope(n3[:, :, NOPE:NOPE + half], n3[:, :, NOPE + half:], c.cos1[:, i, :], c.sin1[:, i, :],
                   heads, half, [m, c.rope_ready])
        yield
        yield
        tb, m = c.transpose_blocks([n.buf[:, j * MLA_D:(j + 1) * MLA_D] for j in range(heads)], MLA_D, [m])
        c.scratch.give(n, m)
        m = c.copy(dst[0:MLA_D, h0:h0 + heads, i * P:(i + 1) * P],
                   tb.buf[0:MLA_D, 0:heads * P].rearrange("p (a t) -> p a t", a=heads), [m])
        c.banks.give(tb, m)
        ready.append(m)

    heads_q = 2
    wq = heads_q * MLA_D

    def qtile(i, slot, part):
        bank, m = c.token_product(slot, wq, fold(c, 0, i), KD, c.h_ready)
        if i == NT - 1:
            c.weights.give(slot, m)
        yield
        n = c.scratch.take()
        V.after(*n.free)
        m = c.head_norm(bank.buf[:, 0:wq].rearrange("p (h d) -> p h d", h=heads_q), heads_q, MLA_D,
                        n.buf[:, 0:wq].rearrange("p (h d) -> p h d", h=heads_q), [m])
        c.banks.give(bank, m)
        yield from finish_heads(n, heads_q, part * heads_q, i, c.row["qmla"], q, m)

    def queries():
        for part in range(MLA_H // heads_q):
            slot = c.weight_chunk(w_in, C_MLAQ + part * wq, wq)
            for i in range(NT):
                yield qtile(i, slot, part)
    pipelined(queries(), 5, c.idle)

    slot = c.weight_chunk(w_in, C_CKV, KV_RANK)
    slot2 = c.weight_chunk(w_in, C_CKV + KV_RANK, ROPE)

    def ckv(i):
        bank, m = c.token_product(slot, KV_RANK, fold(c, 0, i), KD, c.h_ready)
        bank, m = c.token_product(slot2, ROPE, fold(c, 0, i), KD, c.h_ready, bank=bank, at=KV_RANK)
        slot.used = m
        yield
        n = c.scratch.take()
        V.after(*n.free)
        m0 = c.copy(krope[:, i, :], bank.buf[:, KV_RANK:KV_RANK + ROPE], [m], "act")
        m = c.head_norm(bank.buf[:, 0:KV_RANK].unsqueeze(1), 1, KV_RANK, n.buf[:, 0:KV_RANK].unsqueeze(1), [m, m0])
        c.banks.give(bank, m)
        yield
        tb, m = c.transpose_blocks([n.buf[:, j * P:(j + 1) * P] for j in range(2)], P, [m])
        c.scratch.give(n, m)
        for j in range(2):
            A.after(m)
            m = A.run(nc.scalar.activation(ckvT[:, j, i * P:(i + 1) * P], tb.buf[:, j * P:(j + 1) * P],
                                           ACT.Identity, scale=columns(c.col["norm_ckv"], j)))
        c.banks.give(tb, m)
        ckv_ready.append(m)
    ckv_ready = []
    pipelined((ckv(i) for i in range(NT)), 3, c.idle)
    c.weights.give(slot, slot.used)
    c.weights.give(slot2, slot.used)

    slot = c.weight_chunk(w_ukv, 0, MLA_H * (NOPE + MLA_V), kt=KV_RANK // P)

    def kvtile(i, half):
        heads = 4
        bank, m = c.token_product(slot, 512, lambda kk: ckvT[:, kk, i * P:(i + 1) * P], 2, ckv_ready, c0=512 * half)
        slot.used = m
        yield
        b3 = bank.buf[:, :].rearrange("p (h d) -> p h d", h=heads)
        n = c.scratch.take()
        n3 = n.buf[:, 0:heads * MLA_D].rearrange("p (h d) -> p h d", h=heads)
        vd = v[:, i, half * 256:(half + 1) * 256].rearrange("p (h d) -> p h d", h=heads)
        m = c.copy(vd, b3[:, :, NOPE:], [m], "act")
        ready.append(m)
        m = c.copy(n3[:, :, 0:NOPE], b3[:, :, 0:NOPE], [m, *n.free], "act")
        c.banks.give(bank, m)
        G.after(*n.free, *ckv_ready)
        m2 = G.run(nc.gpsimd.tensor_copy(n3[:, :, NOPE:], krope[:, i, :].unsqueeze(1).to_broadcast([P, heads, ROPE])))
        m = c.head_norm(n3, heads, MLA_D, n3, [m, m2])
        yield from finish_heads(n, heads, half * heads, i, c.row["kmla"], k, m)
    pipelined((kvtile(i, half) for half in range(2) for i in range(NT)), 5, c.idle)
    c.weights.give(slot, slot.used)
    causal_softmax(c, q, lambda h: k[0:MLA_D, h, :], v, MLA_D ** -0.5, ready, 0, pairs=False)


def causal_softmax(c, q, keys, v, scale, ready, out0, pairs):
    nc, PE, V = c.nc, c.PE, c.DVE

    def head(i, h, t):
        def query():
            if not pairs:
                return q[0:MLA_D, h, i * P:(i + 1) * P], []
            if h == 0:
                t["q"], t["q_in"] = c.pad_queries(q, slice(i * P, (i + 1) * P), ready)
            return t["q"].buf[:, h, :], t["q_in"]

        def out():
            if h == 0:
                t["out"] = c.head_pair_banks()
            if pairs and h == H - 1:
                c.padded.give(t["q"], c.PE.last())
            return c.pair_columns(t["out"], h)

        def done(m):
            if h < H - 1:
                return
            sums, o = t["sums"], c.scratch.take()
            V.after(m, *o.free)
            mr = V.run(nc.vector.reciprocal(sums.buf[:, 0:H], sums.buf[:, 0:H]))
            V.after(mr)
            for r in range(2):
                mo = V.run(nc.vector.tensor_tensor(
                    c.kept(o.buf[:], r), c.kept(t["out"][r].buf[:], r),
                    sums.buf[:, r:H:2].unsqueeze(2).to_broadcast([P, H // 2, HD]), ALU.mult))
                c.banks.give(t["out"][r], mo)
            c.small.give(sums, mo)
            c.small.give(t["negmax"], mo)
            yield
            tb, mt = c.transpose_blocks([o.buf[:, j * P:(j + 1) * P] for j in range(4)], P, [mo])
            c.scratch.give(o, mt)
            mt = c.copy(c.mixed[:, out0:out0 + 4, i * P:(i + 1) * P],
                        tb.buf[:].rearrange("p (a t) -> p a t", a=4), [mt])
            c.banks.give(tb, mt)
            c.mixed_ready.append(mt)
        if h == 0:
            t["sums"], t["negmax"] = c.small.take(), c.small.take()
            V.after(*t["negmax"].free)
            c.ACT.after(*t["sums"].free)
        return (yield from c.softmax_job(
            query, keys(h)[:, 0:(i + 1) * P], i + 1, [(c.const("ident"), c.const("causal"), i * P)], scale,
            lambda b: v[:, b, (h // 2) * P:(h // 2 + 1) * P], out,
            t["negmax"].buf[:, h:h + 1], t["sums"].buf[:, h:h + 1], ready, done))

    def heads_of():
        for i in range(NT):
            t = {}
            for h in range(H):
                yield head(i, h, t)
    pipelined(heads_of(), 6, c.idle)


def merge(c):
    nc, PE, A, V = c.nc, c.PE, c.ACT, c.DVE
    merged = c.arena[:, 0:KD * S].rearrange("p (a t) -> p a t", a=KD)
    c.barrier()
    ready = []
    for jj in range(KD // 2):
        gates = [c.weight_chunk(c.io["w_in"], C_GATE + n * D + jj * 256, 256) for n in range(2)]
        projs = [c.weight_chunk(c.io[w], jj * 256, 256, kt=4) for w in ("w_o_mla", "w_o_dil")]

        def column(m_, jj=jj, gates=gates, projs=projs):
            j = 2 * jj + m_
            got = []
            for n in range(2):
                gb, m = c.feature_product(gates[n], m_, c.hT, KD, c.h_ready)
                gates[n].used = m
                gs = c.scratch.take()
                A.after(m, *gs.free)
                m = A.run(nc.scalar.activation(gs.buf[:], gb.buf[:], ACT.Sigmoid,
                                               bias=columns(c.col["b_gate"], n * KD + j)))
                c.banks.give(gb, m)
                pb, m2 = c.feature_product(projs[n], m_, c.mixed[:, 4 * n:4 * n + 4, :], 4, c.mixed_ready)
                projs[n].used = m2
                got.append((gs, m, pb, m2))
            yield
            for gs, m, pb, m2 in got:
                V.after(m, m2)
                m = V.run(nc.vector.tensor_tensor(gs.buf[:], gs.buf[:], pb.buf[:], ALU.mult))
                c.banks.give(pb, m)
            V.after(m)
            m = V.run(nc.vector.tensor_tensor(merged[:, j, :], got[0][0].buf[:], got[1][0].buf[:], ALU.add))
            ready.append(m)
            for g in got:
                c.scratch.give(g[0], m)
        pipelined((column(m_) for m_ in range(2)), 2, c.idle)
        for s in gates + projs:
            c.weights.give(s, s.used)
    c.h_free = [PE.last()]
    project_out(c, c.io["w_out"], merged, KD, ready)


def project_out(c, w, actT, kt, ready, gate=None):
    per = 16 // 2
    for jj in range(KD // 2):
        banks = [None, None]
        for k0 in range(0, kt, per):
            n = min(per, kt - k0)
            slot = c.weight_chunk(w, jj * 256, 256, kt=n, k0=k0)
            for m_ in range(2):
                banks[m_], m = c.feature_product(slot, m_, actT[:, k0:k0 + n, :], n, ready, bank=banks[m_],
                                                 first=k0 == 0, last=k0 + n == kt)
            c.weights.give(slot, m)
        for m_ in range(2):
            j = 2 * jj + m_
            c.add_residual(banks[m_], m, j, None if gate is None else gate(j))


def moe(c):
    nc, io, PE, A, V, G = c.nc, c.io, c.PE, c.ACT, c.DVE, c.POOL
    c.barrier()
    L = c.arena
    at = [0]

    def take(n, dt=None):
        a = L[:, at[0]:at[0] + n]
        at[0] += n
        return a if dt is None else a.bitcast(dt)
    NL = N_GRP + NE
    logits = take(NT * NL).rearrange("p (t n) -> p t n", t=NT)
    g8 = take(NT * 8).rearrange("p (t n) -> p t n", t=NT)
    top = take(NT * 8).rearrange("p (t n) -> p t n", t=NT)
    idx = take(NT * 8, U32).rearrange("p (t n) -> p t n", t=NT)
    pick = take(2 * NT).rearrange("p (n t) -> p n t", n=2)
    onehot = take(2 * NT * NE).rearrange("p (n t e) -> p n t e", n=2, t=NT)
    both = take(NT * NE).rearrange("p (t e) -> p t e", t=NT)
    place = take(NT * NE).rearrange("p (t e) -> p t e", t=NT)
    tmp = take(NT * NE).rearrange("p (t e) -> p t e", t=NT)
    stat = take(8 * NT).rearrange("p (n t) -> p n t", n=8)
    slotf = take(2 * NT)
    sloti = take(2 * NT, I32)
    blocks = take(8 + NBLK)
    block_e = take(NBLK, I32)
    tokens = take(NBLK, I32)
    table = take(P)
    xb = [take(D) for _ in range(3)]
    xbT = [take(D) for _ in range(2)]
    yb = [take(D) for _ in range(3)]

    stored = []
    h2_sem = c.sem("h2_out")
    n_stored = 0
    for i in range(NT):
        for half in range(2):
            tb, m = c.transpose_blocks([c.hT[:, 4 * half + j, i * P:(i + 1) * P] for j in range(4)], P, c.h_ready)
            s = c.scratch.take()
            m = c.copy(s.buf[:], tb.buf[:], [m, *s.free])
            c.banks.give(tb, m)
            G.after(m)
            nc.gpsimd.dma_start(c.h2_dram[i * P:(i + 1) * P, half * 512:(half + 1) * 512], s.buf[:]).then_inc(h2_sem, 16)
            n_stored += 16
            c.scratch.give(s, (h2_sem, n_stored))
    h2_stored = (h2_sem, n_stored)

    wg = c.weight_chunk(io["w_router_group"], 0, N_GRP)
    we = c.weight_chunk(io["w_router_expert"], 0, NE)
    bank = c.banks.take()
    PE.after(*bank.free)
    for i in range(NT):
        c.token_product(wg, N_GRP, fold(c, 0, i), KD, c.h_ready, bank=bank, at=i * NL)
        _, m = c.token_product(we, NE, fold(c, 0, i), KD, c.h_ready, bank=bank, at=i * NL + N_GRP)
    c.weights.give(wg, m)
    c.weights.give(we, m)
    c.h_free = [m]
    first = ROWS["b_rg"][0]
    bias = c.rows[:, first:first + NL].unsqueeze(1).to_broadcast([P, NT, NL])

    def v(ins):
        return V.run(ins)
    V.after(m)
    m = v(nc.vector.tensor_tensor(logits, bank.buf[:, 0:NT * NL].rearrange("p (t n) -> p t n", t=NT), bias, ALU.add))
    c.banks.give(bank, m)
    m2 = v(nc.vector.memset(g8, NEG))
    V.after(m, m2)
    m = v(nc.vector.tensor_copy(g8[:, :, 0:N_GRP], logits[:, :, 0:N_GRP]))
    for i in range(NT):
        V.after(m)
        m = v(nc.vector.max(top[:, i, :], g8[:, i, :]))
        V.after(m)
        m = v(nc.vector.max_index(idx[:, i, :], top[:, i, :], g8[:, i, :]))
    V.after(m)
    m = v(nc.vector.tensor_copy(stat[:, 0, :], idx[:, :, 0]))
    m = v(nc.vector.tensor_tensor(g8[:, :, 0:N_GRP], g8[:, :, 0:N_GRP],
                                  top[:, :, 0:1].to_broadcast([P, NT, N_GRP]), ALU.subtract))
    A.after(m)
    m = A.run(nc.scalar.activation(g8[:, :, 0:N_GRP], g8[:, :, 0:N_GRP], ACT.Exp))
    V.after(m)
    m = v(nc.vector.tensor_reduce(stat[:, 1, :], g8[:, :, 0:N_GRP], AX.X, ALU.add))
    V.after(m)
    m = v(nc.vector.reciprocal(stat[:, 1, :], stat[:, 1, :]))
    chosen = g8[:, :, N_GRP:2 * N_GRP]
    m = v(nc.vector.tensor_tensor(chosen, c.const("group")[:, 0:N_GRP].unsqueeze(1).to_broadcast([P, NT, N_GRP]),
                                  stat[:, 0, :].unsqueeze(2).to_broadcast([P, NT, N_GRP]), ALU.is_equal))
    V.after(m)
    m = v(nc.vector.tensor_scalar(chosen, chosen, -1.0, -NEG, ALU.add, ALU.mult))
    V.after(m)
    for i in range(NT):
        m = v(nc.vector.tensor_tensor(tmp[:, i, :].rearrange("p (g e) -> p g e", g=N_GRP),
                                      logits[:, i, N_GRP:].rearrange("p (g e) -> p g e", g=N_GRP),
                                      chosen[:, i, :].unsqueeze(2).to_broadcast([P, N_GRP, PER_GRP]), ALU.add))
    for i in range(NT):
        V.after(m)
        m = v(nc.vector.max(top[:, i, :], tmp[:, i, :]))
        V.after(m)
        m = v(nc.vector.max_index(idx[:, i, :], top[:, i, :], tmp[:, i, :]))
    V.after(m)
    m = v(nc.vector.tensor_tensor(stat[:, 2, :], top[:, :, 1], top[:, :, 0], ALU.subtract))
    A.after(m)
    m = A.run(nc.scalar.activation(stat[:, 2, :], stat[:, 2, :], ACT.Exp))
    for n in range(2):
        m3 = v(nc.vector.tensor_copy(pick[:, n, :], idx[:, :, n]))
    V.after(m, m3)
    m = v(nc.vector.tensor_scalar(stat[:, 3, :], stat[:, 2, :], 1.0, None, ALU.add))
    V.after(m)
    m = v(nc.vector.reciprocal(stat[:, 3, :], stat[:, 3, :]))
    V.after(m)
    m = v(nc.vector.tensor_tensor(stat[:, 4, :], stat[:, 1, :], stat[:, 3, :], ALU.mult))
    V.after(m)
    share = v(nc.vector.tensor_tensor(stat[:, 5, :], stat[:, 4, :], stat[:, 2, :], ALU.mult))
    V.after(share)
    for n in range(2):
        m = v(nc.vector.tensor_tensor(onehot[:, n, :, :], c.const("expert").unsqueeze(1).to_broadcast([P, NT, NE]),
                                      pick[:, n, :].unsqueeze(2).to_broadcast([P, NT, NE]), ALU.is_equal))
    V.after(m)
    m = v(nc.vector.tensor_tensor(both, onehot[:, 0, :, :], onehot[:, 1, :, :], ALU.add))
    rank, count = c.banks.take(), c.banks.take()
    PE.after(m, *rank.free, *count.free)
    for i in range(NT):
        for j in range(i + 1):
            mm = nc.tensor.matmul(rank.buf[:, i * NE:(i + 1) * NE], c.const("before" if j == i else "ones"),
                                  both[:, j, :], start=j == 0, stop=j == i)
        nc.tensor.matmul(count.buf[0:NE, 0:1], both[:, i, :], c.const("ones")[:, 0:1], start=i == 0, stop=i == NT - 1)
    m = PE.run(nc.tensor.matmul(rank.buf[:, NT * NE:NT * NE + 1], c.const("ones"), c.const("ones")[:, 0:1],
                                start=True, stop=True))
    cnt, nblk, end, per = blocks[0:NE, 0:1], blocks[0:NE, 1:2], blocks[0:NE, 2:3], blocks[0:NE, 4:8]
    V.after(m)
    m = v(nc.vector.tensor_copy(cnt, count.buf[0:NE, 0:1]))
    V.after(m)
    m = v(nc.vector.tensor_scalar(per, c.const("thresholds", NE), cnt, None, ALU.is_lt))
    V.after(m)
    m = v(nc.vector.tensor_reduce(nblk, per, AX.X, ALU.add))
    PE.after(m)
    before = c.const("before", NE)[:, 0:NE]
    nc.tensor.matmul(count.buf[0:NE, 1:2], before, nblk, start=True, stop=False)
    nc.tensor.matmul(count.buf[0:NE, 1:2], c.const("ident", NE)[:, 0:NE], nblk, start=False, stop=True)
    m = PE.run(nc.tensor.matmul(count.buf[:, 2:2 + NE], nblk.to_broadcast([NE, P]), before, start=True, stop=True))
    V.after(m)
    m = v(nc.vector.tensor_copy(end, count.buf[0:NE, 1:2]))
    V.after(m)
    m = v(nc.vector.tensor_scalar(blocks[0:NE, 8:8 + NBLK], c.const("block", NE), end, None, ALU.is_ge))
    PE.after(m)
    m2 = PE.run(nc.tensor.matmul(rank.buf[0:1, 256:256 + NBLK], c.const("ones", NE)[:, 0:1],
                                 blocks[0:NE, 8:8 + NBLK], start=True, stop=True))
    V.after(m2)
    expert_ready = v(nc.vector.tensor_scalar(block_e[0:1, :], rank.buf[0:1, 256:256 + NBLK], float(NE - 1), None, ALU.min))
    V.after(m)
    m = v(nc.vector.tensor_scalar(tmp[:, 0, :], count.buf[:, 2:2 + NE], float(P), None, ALU.mult))
    c.banks.give(count, m)
    V.after(m)
    m = v(nc.vector.tensor_tensor(place, rank.buf[:, 0:NT * NE].rearrange("p (t e) -> p t e", t=NT),
                                  tmp[:, 0, :].unsqueeze(1).to_broadcast([P, NT, NE]), ALU.add))
    c.banks.give(rank, m)
    for n in range(2):
        V.after(m)
        m = v(nc.vector.tensor_tensor(tmp, onehot[:, n, :, :], place, ALU.mult))
        V.after(m)
        m = v(nc.vector.tensor_reduce(slotf[:, n * NT:(n + 1) * NT], tmp, AX.X, ALU.add))
    V.after(m)
    slots_ready = v(nc.vector.tensor_copy(sloti, slotf))
    m = G.run(nc.gpsimd.memset(table[0:NBLK, :], 0.0))
    G.after(m)
    tsem = c.sem("token_table")
    nc.gpsimd.dma_start(c.table_dram.rearrange("(b p) o -> b (p o)", p=P), table[0:NBLK, :]).then_inc(tsem, 16)
    G.after((tsem, 16), slots_ready)
    for n in range(2):
        for i in range(NT):
            nc.gpsimd.indirect_dma_start(
                out=c.table_dram, out_offset=bass.IndirectOffsetOnAxis(ap=sloti[:, n * NT + i:n * NT + i + 1], axis=0),
                in_=c.const("token")[:, i:i + 1], in_offset=None).then_inc(tsem, 16)
    G.after((tsem, 16 * (1 + 2 * NT)))
    nc.gpsimd.dma_start(table[0:NBLK, :], c.table_dram.rearrange("(b p) o -> b (p o)", p=P)).then_inc(tsem, 16)
    bank = c.banks.take()
    PE.after(*bank.free, (tsem, 16 * (2 + 2 * NT)))
    m = PE.run(nc.tensor.transpose(bank.buf[:, 0:NBLK], table[0:NBLK, :], c.const("ident", NBLK)[:, 0:NBLK]))
    V.after(m)
    tokens_ready = v(nc.vector.tensor_copy(tokens, bank.buf[:, 0:NBLK]))
    c.banks.give(bank, tokens_ready)

    gathers = [c.sem(f"gather{j}") for j in range(3)]
    outs = [c.sem(f"tile_out{j}") for j in range(3)]
    x_free = [[] for _ in range(3)]
    xT_free = [[] for _ in range(2)]
    c.SP.after(expert_ready)
    G.after(tokens_ready, h2_stored)

    def expert_weights(name, e, kt):
        view = lambda buf: buf.rearrange("p (k n) -> p k n", k=kt)
        src = io[name][bass.ds(e, 1), :, :].rearrange("e (k p) n -> p (e k) n", p=P)
        s = c.weights.load(view, src)
        s.w = view(s.buf)
        return s

    def tile(b):
        j = b % 3
        G.after(*x_free[j])
        nc.gpsimd.indirect_dma_start(out=xb[j], out_offset=None, in_=c.h2_dram,
                                     in_offset=bass.IndirectOffsetOnAxis(ap=tokens[:, b:b + 1], axis=0)
                                     ).then_inc(gathers[j], 16)
        yield
        e = nc.sync.value_load(block_e[0:1, b:b + 1], min_val=0, max_val=NE - 1)
        w = [expert_weights("w_gate", e, KD), expert_weights("w_up", e, KD)]
        xt = xbT[b % 2]
        marks = []
        for half in range(2):
            tb, m = c.transpose_blocks([xb[j][:, (4 * half + q) * P:(4 * half + q + 1) * P] for q in range(4)], P,
                                       [(gathers[j], 16 * (b // 3 + 1))])
            x_free[j] = [m]
            m = c.copy(xt[:, half * 512:(half + 1) * 512], tb.buf[:], [m, *xT_free[b % 2]])
            marks.append(m)
            c.banks.give(tb, m)
        yield
        toks = lambda k: xt[:, k * P:(k + 1) * P]
        gb, m1 = c.token_product(w[0], FF, toks, KD, marks)
        ub, m2 = c.token_product(w[1], FF, toks, KD, marks)
        xT_free[b % 2] = [m2]
        c.weights.give(w[0], m1)
        c.weights.give(w[1], m2)
        w.append(expert_weights("w_down", e, FF // P))
        he = c.scratch.take()
        A.after(m1, *he.free)
        m = A.run(nc.scalar.activation(he.buf[:, 0:FF], gb.buf[:, 0:FF], ACT.Silu))
        c.banks.give(gb, m)
        V.after(m, m2)
        m = V.run(nc.vector.tensor_tensor(he.buf[:, 0:FF], he.buf[:, 0:FF], ub.buf[:, 0:FF], ALU.mult))
        c.banks.give(ub, m)
        yield
        tb, m = c.transpose_blocks([he.buf[:, q * P:(q + 1) * P] for q in range(2)], P, [m])
        m = c.copy(he.buf[:, FF:2 * FF], tb.buf[:, 0:FF], [m])
        c.banks.give(tb, m)
        yield
        PE.after(m, w[2].ready)
        done = []
        for half in range(2):
            bk = c.banks.take()
            PE.after(*bk.free)
            for q in range(2):
                mm = nc.tensor.matmul(bk.buf[:], he.buf[:, FF + q * P:FF + (q + 1) * P],
                                      w[2].w[:, q, half * 512:(half + 1) * 512], start=q == 0, stop=q == 1)
            m = PE.run(mm)
            out_free = [(outs[j], 16 * (b // 3))] if b >= 3 else []
            mc = c.copy(yb[j][:, half * 512:(half + 1) * 512], bk.buf[:], [m, *out_free])
            c.banks.give(bk, mc)
            done.append(mc)
        c.scratch.give(he, m)
        c.weights.give(w[2], m)
        G.after(*done)
        nc.gpsimd.dma_start(c.y_dram[b * P:(b + 1) * P, :], yb[j]).then_inc(outs[j], 16)
    pipelined((tile(b) for b in range(NBLK)), 5)

    for j in range(3):
        G.after((outs[j], 16 * len(range(j, NBLK, 3))))
    c.barrier()
    tail = [c.sem(f"combine{i}") for i in range(NT)]
    both_y = xb + yb
    tail_free = [[] for _ in range(3)]
    for i in range(NT):
        pair = (both_y[2 * (i % 3)], both_y[2 * (i % 3) + 1])
        G.after(*tail_free[i % 3])
        for n in range(2):
            nc.gpsimd.indirect_dma_start(out=pair[n], out_offset=None, in_=c.y_dram,
                                         in_offset=bass.IndirectOffsetOnAxis(ap=sloti[:, n * NT + i:n * NT + i + 1], axis=0)
                                         ).then_inc(tail[i], 16)
        V.after((tail[i], 32))
        m = V.run(nc.vector.tensor_scalar(pair[1], pair[1], stat[:, 5, i:i + 1], None, ALU.mult))
        V.after(m)
        m = V.run(nc.vector.scalar_tensor_tensor(out=pair[0], in0=pair[0], scalar=stat[:, 4, i:i + 1], in1=pair[1],
                                                 op0=ALU.mult, op1=ALU.add))
        for half in range(2):
            tb, mt = c.transpose_blocks([pair[0][:, (4 * half + q) * P:(4 * half + q + 1) * P] for q in range(4)],
                                        P, [m])
            x = c.xT[:, 4 * half:4 * half + 4, i * P:(i + 1) * P]
            V.after(mt, *[mk for k in range(4) for mk in c.x_ready[4 * half + k]])
            mv = V.run(nc.vector.tensor_tensor(x, x, tb.buf[:].rearrange("p (a t) -> p a t", a=4), ALU.add))
            c.banks.give(tb, mv)
            tail_free[i % 3] = [mv]
    c.x_ready = [[V.last()] for _ in range(KD)]


def head_groups(c):
    nc, PE, A, V, G = c.nc, c.PE, c.ACT, c.DVE, c.POOL
    w_in = c.io["attn_w_in_2"]
    qa, ka, va, qb, kb, vb = (c.arena[:, j * 4 * S:(j + 1) * 4 * S].rearrange("p (a t) -> p a t", a=4)
                              for j in range(6))
    c.barrier()
    c.mixed_ready = []
    ready = []
    heads, half = 4, ROPE2 // 2
    def tile(i, slot, part, dst, hf):
        bank, m = c.token_product(slot, 256, fold(c, 0, i), KD, c.h_ready)
        if i == NT - 1:
            c.weights.give(slot, m)
        yield
        if part in (2, 5):
            m = c.copy(dst[:, i, hf * 256:(hf + 1) * 256], bank.buf[:, 0:256], [m])
            c.banks.give(bank, m)
            ready.append(m)
            return
        n = c.scratch.take()
        m = c.copy(n.buf[:, 0:256], bank.buf[:, 0:256], [m, *n.free])
        c.banks.give(bank, m)
        n3 = n.buf[:, 0:256].rearrange("p (h d) -> p h d", h=heads)
        m = c.rope(n3[:, :, 0:half], n3[:, :, half:2 * half], c.cos2[:, i, :], c.sin2[:, i, :], heads, half,
                   [m, c.rope_ready])
        yield
        yield
        tb, m = c.transpose_blocks([n.buf[:, j * P:(j + 1) * P] for j in range(2)], P, [m])
        c.scratch.give(n, m)
        m = c.copy(dst[:, 2 * hf:2 * hf + 2, i * P:(i + 1) * P],
                   tb.buf[:, 0:256].rearrange("p (a t) -> p a t", a=2), [m])
        c.banks.give(tb, m)
        ready.append(m)

    def tiles():
        for part, dst in ((0, qa), (1, ka), (2, va), (5, vb)):
            for hf in range(2):
                slot = c.weight_chunk(w_in, part * 512 + hf * 256, 256)
                for i in range(NT):
                    yield tile(i, slot, part, dst, hf)
    pipelined(tiles(), 5, c.idle)
    for part, dst in ((3, qb), (4, kb)):
        for hf in range(2):
            slot = c.weight_chunk(w_in, part * 512 + hf * 256, 256)
            for m_ in range(2):
                bank, m = c.feature_product(slot, m_, c.hT, KD, c.h_ready)
                A.after(m)
                mc = A.run(nc.scalar.activation(dst[:, 2 * hf + m_, :], bank.buf[:], ACT.Copy,
                                                scale=1.0 if part == 3 else HD ** -0.5))
                c.banks.give(bank, mc)
                ready.append(mc)
            c.weights.give(slot, m)
    c.h_free = [PE.last()]
    causal_softmax(c, qa, lambda h: ka[:, h // 2, :], va, HD ** -0.5, ready, 0, pairs=True)
    c.barrier()

    o = qa
    padded = c.arena[:, 4 * S:12 * S].rearrange("p (h t) -> p h t", h=H)
    m = V.run(nc.vector.memset(padded, 0.0))
    PE.after(*[c.copy(padded[rows, r:H:2, :], qb[rows, :, :], [m])
               for r, rows in enumerate((slice(0, HD), slice(HD, P)))])

    def head(h):
        t = h // 2
        sp = []
        for j in range(NT):
            n = S - j * P
            zb = c.banks.take()
            PE.after(*zb.free)
            m = PE.run(nc.tensor.matmul(zb.buf[:, 0:n], kb[:, t, j * P:(j + 1) * P], padded[:, h, j * P:S],
                                        start=True, stop=True))
            s = c.scratch.take()
            A.after(m, *s.free)
            m = A.run(nc.scalar.activation(s.buf[:, 0:n], zb.buf[:, 0:n], ACT.Abs))
            A.after(m)
            m = A.run(nc.scalar.activation(s.buf[:, 0:n], s.buf[:, 0:n], ACT.Exp, scale=-1.0))
            A.after(m)
            m = A.run(nc.scalar.activation(s.buf[:, 0:n], s.buf[:, 0:n], ACT.Ln, bias=1.0))
            V.after(m)
            m = V.run(nc.vector.scalar_tensor_tensor(out=s.buf[:, 0:n], in0=zb.buf[:, 0:n], scalar=0.0,
                                                     in1=s.buf[:, 0:n], op0=ALU.max, op1=ALU.add))
            c.banks.give(zb, m)
            V.after(m)
            m = V.run(nc.vector.tensor_tensor(s.buf[:, 0:P], s.buf[:, 0:P], c.const("sb_keep"), ALU.mult))
            sp.append((s, m))
        yield
        ws = []
        for i in range(NT):
            n = S - i * P
            cb = c.banks.take()
            PE.after(*cb.free)
            nc.tensor.matmul(cb.buf[:, 0:n], kb[:, t, i * P:(i + 1) * P], padded[:, h, i * P:S], start=True, stop=False)
            nc.tensor.matmul(cb.buf[:, 0:P], c.const("ident"), c.const("sb_mask"), start=False, stop=False)
            for j in range(i, NT):
                PE.after(sp[j][1])
                mm = nc.tensor.matmul(cb.buf[:, (j - i) * P:n], c.const("neg_from" if j == i else "neg_ones"),
                                      sp[j][0].buf[:, 0:S - j * P], start=False, stop=j == NT - 1)
            m = PE.run(mm)
            w = sp[i][0]
            A.after(m)
            m = A.run(nc.scalar.activation(w.buf[:, 0:n], cb.buf[:, 0:n], ACT.Exp))
            c.banks.give(cb, m)
            ws.append((w, m))
        yield
        ob = c.banks.take()
        PE.after(*ob.free, *[m for _, m in ws])
        for q in range(NT):
            for i in range(q + 1):
                mm = nc.tensor.matmul(ob.buf[:, q * P:(q + 1) * P], ws[i][0].buf[:, (q - i) * P:(q - i + 1) * P],
                                      vb[:, i, t * P:(t + 1) * P], start=i == 0, stop=i == q)
        m = PE.run(mm)
        for w, _ in ws:
            c.scratch.give(w, m)
        m = c.copy(o[:, :, h * HD:(h + 1) * HD], c.kept(ob.buf[:], h % 2), [m])
        c.banks.give(ob, m)
        done.append(m)
    done = []
    pipelined((head(h) for h in range(H)), 3, c.idle)
    for i in range(NT):
        tb, m = c.transpose_blocks([o[:, i, j * P:(j + 1) * P] for j in range(4)], P, done)
        m = c.copy(c.mixed[:, 4:8, i * P:(i + 1) * P], tb.buf[:].rearrange("p (a t) -> p a t", a=4), [m])
        c.banks.give(tb, m)
        c.mixed_ready.append(m)


def swiglu(c, layer):
    nc, A, V = c.nc, c.ACT, c.DVE
    w_in, w_out = c.io["ffn_w_in_2"][layer], c.io["ffn_w_out_2"][layer]
    hid = c.arena[:, 0:KH * S].rearrange("p (a t) -> p a t", a=KH)
    c.barrier()
    ready = []
    for jj in range(KH // 2):
        gs, us = c.weight_chunk(w_in, jj * 256, 256), c.weight_chunk(w_in, HID + jj * 256, 256)
        for m_ in range(2):
            gb, m1 = c.feature_product(gs, m_, c.hT, KD, c.h_ready)
            ub, m2 = c.feature_product(us, m_, c.hT, KD, c.h_ready)
            dst = hid[:, 2 * jj + m_, :]
            A.after(m1)
            m = A.run(nc.scalar.activation(dst, gb.buf[:], ACT.Silu))
            c.banks.give(gb, m)
            V.after(m, m2)
            m = V.run(nc.vector.tensor_tensor(dst, dst, ub.buf[:], ALU.mult))
            c.banks.give(ub, m)
            ready.append(m)
        c.weights.give(gs, m1)
        c.weights.give(us, m2)
        c.idle()
    c.h_free = [c.PE.last()]
    project_out(c, w_out, hid, KH, ready[-1:], gate=lambda j: c.mod[:, layer, 5, j:j + 1])


def delta_net(c):
    nc, PE, A, V, G = c.nc, c.PE, c.ACT, c.DVE, c.POOL
    w_in = c.io["gdn_w_in_2"]
    HG = 4
    c.barrier()
    qT, kT, ktok, vtok = (c.arena[:, j * HG * S:(j + 1) * HG * S].rearrange("p (a t) -> p a t", a=HG)
                          for j in range(4))
    for j in range(8):
        c.scratch.give(Slot(c.arena[:, (16 + j) * S:(17 + j) * S]))
    for t in c.padded.slots:
        for j in range(2):
            slot = Slot(t.buf[:, 4 * j:4 * j + 4, :].rearrange("p h t -> p (h t)"))
            c.scratch.give(slot, *t.free)
    g4 = lambda a: a.rearrange("p (h t) -> p h t", h=HG)

    slot = c.weight_chunk(w_in, 4 * H * GD, 2 * H)
    bank = c.banks.take()
    PE.after(*bank.free)
    for i in range(NT):
        _, m = c.token_product(slot, 2 * H, fold(c, 0, i), KD, c.h_ready, bank=bank, at=i * 2 * H)
    c.weights.give(slot, m)
    col = c.gate_cols
    x, t, g, beta, gcum, kdec1, bexp, kdec0 = (col[:, j, :, :] for j in range(8))
    kdec = kdec0
    b3 = bank.buf[:, 0:NT * 2 * H].rearrange("p (t n) -> p t n", t=NT)
    over = lambda r: r.unsqueeze(1).to_broadcast([P, NT, H])
    V.after(m)
    m = V.run(nc.vector.tensor_tensor(x, b3[:, :, 0:H], over(c.row["dt_bias"]), ALU.add))
    A.after(m)
    m1 = A.run(nc.scalar.activation(beta, b3[:, :, H:], ACT.Sigmoid))
    c.banks.give(bank, m1)
    m = A.run(nc.scalar.activation(t, x, ACT.Abs))
    A.after(m)
    m = A.run(nc.scalar.activation(t, t, ACT.Exp, scale=-1.0))
    A.after(m)
    m = A.run(nc.scalar.activation(t, t, ACT.Ln, bias=1.0))
    m = A.run(nc.scalar.activation(c.row["a_log"], c.row["a_log"], ACT.Exp))
    V.after(m)
    m = V.run(nc.vector.scalar_tensor_tensor(out=g, in0=x, scalar=0.0, in1=t, op0=ALU.max, op1=ALU.add))
    V.after(m)
    m = V.run(nc.vector.scalar_tensor_tensor(out=g, in0=g, scalar=-1.0, in1=over(c.row["a_log"]),
                                             op0=ALU.mult, op1=ALU.mult))
    bank = c.banks.take()
    PE.after(m, *bank.free)
    flat = lambda a: a.rearrange("p t h -> p (t h)")
    nc.tensor.matmul(bank.buf[:, 0:NT * H], c.const("chunk_upto"), flat(g), start=True, stop=True)
    m = PE.run(nc.tensor.matmul(bank.buf[:, NT * H:2 * NT * H], c.const("chunk_all"), flat(g), start=True, stop=True))
    V.after(m)
    m = V.run(nc.vector.tensor_copy(flat(gcum), bank.buf[:, 0:NT * H]))
    V.after(m)
    m = V.run(nc.vector.tensor_tensor(flat(kdec), bank.buf[:, NT * H:2 * NT * H], flat(gcum), ALU.subtract))
    c.banks.give(bank, m)
    A.after(m)
    mk = A.run(nc.scalar.activation(kdec, kdec, ACT.Exp))
    m = A.run(nc.scalar.activation(bexp, gcum, ACT.Exp))
    V.after(mk)
    in_second = c.const("chunk_all")[:, P - 1:P]
    mk = V.run(nc.vector.tensor_scalar(flat(kdec1), flat(kdec), in_second, None, ALU.mult))
    V.after(mk)
    mk = V.run(nc.vector.tensor_tensor(flat(kdec0), flat(kdec0), flat(kdec1), ALU.subtract))
    V.after(mk)
    V.after(m, m1)
    cols_ready = V.run(nc.vector.tensor_tensor(bexp, bexp, beta, ALU.mult))

    state = c.state
    c.mixed_ready = []
    for hg in range(H // HG):
        sums = c.banks.take()
        PE.after(*sums.free)
        staged, tail = [], []

        def channel(slot, m_, part, hh, sums=sums, staged=staged, tail=tail, hg=hg):
            ct = part * H + hg * HG + hh
            bank, m = c.feature_product(slot, m_, c.hT, KD, c.h_ready)
            if m_ == 1:
                c.weights.give(slot, m)
            yield
            acc = c.scratch.take()
            V.after(m, *acc.free)
            tap = lambda d: c.conv_w[:, CONV - 1 - d, ct:ct + 1]
            m = V.run(nc.vector.tensor_scalar(acc.buf[:], bank.buf[:], tap(0), None, ALU.mult))
            for d in range(1, CONV):
                V.after(m)
                m = V.run(nc.vector.scalar_tensor_tensor(
                    out=acc.buf[:, d:S], in0=bank.buf[:, 0:S - d], scalar=tap(d), in1=acc.buf[:, d:S],
                    op0=ALU.mult, op1=ALU.add))
            c.banks.give(bank, m)
            dst = acc.buf[:] if part == 2 else (qT, kT)[part][:, hh, :]
            A.after(m)
            m = A.run(nc.scalar.activation(dst, acc.buf[:], ACT.Silu))
            if part < 2:
                A.after(m)
                m = A.run(nc.scalar.activation(acc.buf[:], dst, ACT.Square))
            yield
            yield
            if part < 2:
                row = part * HG + hh
                PE.after(m)
                m = PE.run(nc.tensor.matmul(sums.buf[0:8, :], c.const("strip")[:, 15 - row:23 - row],
                                            acc.buf[:], start=row == 0, stop=row == 7))
                c.scratch.give(acc, m)
                staged.append(m)
            else:
                tb, m = c.transpose_blocks([acc.buf[:, i * P:(i + 1) * P] for i in range(NT)], P, [m])
                c.scratch.give(acc, m)
                m = c.copy(vtok[:, :, hh * P:(hh + 1) * P], tb.buf[:].rearrange("p (i d) -> p i d", i=NT), [m])
                c.banks.give(tb, m)
                tail.append(m)

        def channels(hg=hg, channel=channel):
            for part in range(3):
                for hf in range(2):
                    slot = c.weight_chunk(w_in, part * H * GD + hg * HG * GD + hf * 256, 256)
                    for m_ in range(2):
                        yield channel(slot, m_, part, 2 * hf + m_)
        pipelined(channels(), 4)
        rows = c.scratch.take()
        V.after(*rows.free)
        A.after(*staged, V.run(nc.vector.memset(rows.buf[:], 0.0)))
        m = A.run(nc.scalar.activation(rows.buf[0:8, :], sums.buf[0:8, :], ACT.Sqrt, bias=c.eps[0:8, 0:1]))
        c.banks.give(sums, m)
        V.after(m)
        mr = V.run(nc.vector.reciprocal(rows.buf[0:8, :], rows.buf[0:8, :]))
        def normalise(row, mr=mr, rows=rows, tail=tail):
            dst = (qT if row < HG else kT)[:, row % HG, :]
            bank = c.banks.take()
            PE.after(mr, *bank.free)
            m = PE.run(nc.tensor.matmul(bank.buf[:], c.const("ident")[:, row:row + 1].to_broadcast([P, P]),
                                        rows.buf[:], start=True, stop=True))
            V.after(m)
            m = V.run(nc.vector.scalar_tensor_tensor(out=dst, in0=dst, scalar=GD ** -0.5 if row < HG else 1.0,
                                                     in1=bank.buf[:], op0=ALU.mult, op1=ALU.mult))
            c.banks.give(bank, m)
            tail.append(m)
            if row < HG:
                return
            hh = row - HG
            yield
            tb, m = c.transpose_blocks([kT[:, hh, i * P:(i + 1) * P] for i in range(NT)], P, [m])
            m = c.copy(ktok[:, :, hh * P:(hh + 1) * P], tb.buf[:].rearrange("p (i d) -> p i d", i=NT), [m])
            c.banks.give(tb, m)
            tail.append(m)
        pipelined((normalise(row) for row in range(8)), 3)
        c.scratch.give(rows, PE.last())
        V.after(*tail)
        state_ready = [V.run(nc.vector.memset(state[:], 0.0))]
        st = {"ready": state_ready}

        def product(left, right, width=P, marks=()):
            bank = c.banks.take()
            PE.after(*bank.free, *marks)
            for hh in range(HG):
                mm = nc.tensor.matmul(bank.buf[:, hh * width:(hh + 1) * width], left(hh), right(hh),
                                      start=True, stop=True)
            return bank, PE.run(mm)

        def block(s, hh):
            return s.buf[:, hh * P:(hh + 1) * P]

        def tile(i, hg=hg, tail=tail, st=st):
            tok = slice(i * P, (i + 1) * P)
            hs = slice(hg * HG, (hg + 1) * HG)
            per_head = lambda a: a[:, i, hs].unsqueeze(2).to_broadcast([P, HG, P])
            over_heads = lambda a: a.unsqueeze(1).to_broadcast([P, HG, P])
            rb, m = product(lambda hh: g[:, i, hg * HG + hh:hg * HG + hh + 1].to_broadcast([P, P]),
                            lambda hh: c.const("chunk_upto"), marks=[cols_ready, *tail])
            dec, erow = c.scratch.take(), c.scratch.take()
            V.after(m, *dec.free)
            for hh in range(HG):
                m = V.run(nc.vector.tensor_scalar(block(dec, hh), rb.buf[:, hh * P:(hh + 1) * P],
                                                  gcum[:, i, hg * HG + hh:hg * HG + hh + 1], 0.0,
                                                  ALU.subtract, ALU.min))
            A.after(m, *erow.free)
            m_e = A.run(nc.scalar.activation(erow.buf[:], rb.buf[:], ACT.Exp))
            c.banks.give(rb, m_e)
            m = A.run(nc.scalar.activation(dec.buf[:], dec.buf[:], ACT.Exp))
            G.after(m)
            m_dec = G.run(nc.gpsimd.tensor_tensor(g4(dec.buf[:]), g4(dec.buf[:]), over_heads(c.const("chunk_upto")), ALU.mult))
            yield
            gb, m1 = product(lambda hh: kT[:, hh, tok], lambda hh: kT[:, hh, tok], marks=tail)
            bb, m2 = product(lambda hh: beta[:, i, hg * HG + hh:hg * HG + hh + 1].to_broadcast([P, P]),
                             lambda hh: c.const("ident"))
            at_ = c.scratch.take()
            V.after(m1, m_dec, *at_.free)
            m = V.run(nc.vector.tensor_tensor(at_.buf[:], gb.buf[:], dec.buf[:], ALU.mult))
            c.banks.give(gb, m)
            V.after(m, m2)
            m_at = V.run(nc.vector.tensor_tensor(at_.buf[:], at_.buf[:], bb.buf[:], ALU.mult))
            c.banks.give(bb, m_at)
            qb, m3 = product(lambda hh: kT[:, hh, tok], lambda hh: qT[:, hh, tok])
            V.after(m3)
            m_attn = V.run(nc.vector.tensor_tensor(dec.buf[:], qb.buf[:], dec.buf[:], ALU.mult))
            attn = dec
            c.banks.give(qb, m_attn)
            kb, vb, q0, q1, kd = (c.scratch.take() for _ in range(5))
            G.after(m_e, cols_ready, *tail, *kb.free, *vb.free, *q0.free, *q1.free, *kd.free)
            for n, s in enumerate((q0, q1)):
                mine, other = (slice(n * CHUNK, (n + 1) * CHUNK), slice((1 - n) * CHUNK, (2 - n) * CHUNK))
                t0 = i * P + n * CHUNK
                G.run(nc.gpsimd.tensor_tensor(g4(s.buf[:])[:, :, mine], qT[:, :, t0:t0 + CHUNK],
                                              g4(erow.buf[:])[:, :, mine], ALU.mult))
                m_q = G.run(nc.gpsimd.memset(g4(s.buf[:])[:, :, other], 0.0))
            G.run(nc.gpsimd.tensor_tensor(g4(kb.buf[:]), g4(ktok[:, i, :]), per_head(bexp), ALU.mult))
            m_kb = G.run(nc.gpsimd.tensor_tensor(g4(vb.buf[:]), g4(vtok[:, i, :]), per_head(beta), ALU.mult))
            ends = c.small.take()
            A.after(m_e, *ends.free)
            m_ends = A.run(nc.scalar.copy(ends.buf[:, 0:2 * HG].rearrange("p (h n) -> p h n", n=2),
                                          g4(erow.buf[:])[:, :, CHUNK - 1:P:CHUNK]))
            m_kd = G.run(nc.gpsimd.tensor_tensor(g4(kd.buf[:]), g4(ktok[:, i, :]), per_head(kdec1), ALU.mult))
            G.after(m_kd)
            m_k0 = G.run(nc.gpsimd.tensor_tensor(g4(ktok[:, i, :]), g4(ktok[:, i, :]), per_head(kdec0), ALU.mult))
            c.scratch.give(erow, m_ends, m_q)
            yield
            level = lambda l: over_heads(c.const("levels")[:, l * P:(l + 1) * P])
            xt, xn, am = c.scratch.take(), c.scratch.take(), c.scratch.take()
            V.after(m_at, *xt.free, *xn.free, *am.free)
            m = V.run(nc.vector.tensor_tensor(g4(am.buf[:]), g4(at_.buf[:]), level(0), ALU.mult))
            V.after(m)
            m = V.run(nc.vector.tensor_tensor(g4(xt.buf[:]), over_heads(c.const("ident")), g4(am.buf[:]), ALU.subtract))
            tb, mt = c.transpose_blocks([block(xt, hh) for hh in range(HG)], P, [m])
            m_x = c.copy(xn.buf[:], tb.buf[:], [mt], "act")
            c.banks.give(tb, m_x)
            m_xt, m_b = m, m
            yield
            for l in range(1, LEVELS):
                V.after(m_b)
                m = V.run(nc.vector.tensor_tensor(g4(am.buf[:]), g4(at_.buf[:]), level(l), ALU.mult))
                bk, m = product(lambda hh: block(am, hh), lambda hh: block(xn, hh), marks=[m, m_x])
                m = c.copy(am.buf[:], bk.buf[:], [m], "act")
                c.banks.give(bk, m)
                yield
                if l < LEVELS - 1:
                    b1, ma = product(lambda hh: block(xt, hh), lambda hh: block(am, hh), marks=[m, m_xt])
                b2, mb = product(lambda hh: block(am, hh), lambda hh: block(xt, hh), marks=[m, m_xt])
                m_b = mb
                if l < LEVELS - 1:
                    V.after(ma)
                    m_x = V.run(nc.vector.tensor_tensor(xn.buf[:], xn.buf[:], b1.buf[:], ALU.subtract))
                    c.banks.give(b1, m_x)
                V.after(mb)
                m_xt = V.run(nc.vector.tensor_tensor(xt.buf[:], xt.buf[:], b2.buf[:], ALU.subtract))
                c.banks.give(b2, m_xt)
                yield
            ub, m1 = product(lambda hh: block(xt, hh), lambda hh: block(vb, hh), marks=[m_xt, m_kb])
            wb, m2 = product(lambda hh: block(kb, hh), lambda hh: block(xt, hh))
            u, w = xn, am
            m_u = c.copy(u.buf[:], ub.buf[:], [m1, m_b], "act")
            m_w = c.copy(w.buf[:], wb.buf[:], [m2, m_b], "act")
            c.banks.give(ub, m_u)
            c.banks.give(wb, m_w)
            c.scratch.give(xt, m2)
            c.scratch.give(kb, m2)
            c.scratch.give(at_, m_xt)
            yield
            ob = c.banks.take()
            for cc, q_ in enumerate((q0, q1)):
                rows_ = slice(cc * CHUNK, (cc + 1) * CHUNK)
                nb = c.banks.take()
                PE.after(*nb.free, m_w, m_q, *st["ready"])
                for hh in range(HG):
                    mm = nc.tensor.matmul(nb.buf[rows_, hh * P:(hh + 1) * P],
                                          w.buf[:, hh * P + cc * CHUNK:hh * P + (cc + 1) * CHUNK],
                                          state[:, hh, :], start=True, stop=True)
                m = PE.run(mm)
                V.after(m, m_u)
                m_v = V.run(nc.vector.tensor_tensor(u.buf[rows_, :], u.buf[rows_, :], nb.buf[rows_, :], ALU.subtract))
                c.banks.give(nb, m_v)
                if cc == 0:
                    PE.after(*ob.free)
                for hh in range(HG):
                    mm = nc.tensor.matmul(ob.buf[:, hh * P:(hh + 1) * P], state[:, hh, :], block(q_, hh),
                                          start=cc == 0 and hh == 0, stop=False, skip_group_check=True)
                m_o = PE.run(mm)
                sb_ = c.banks.take()
                PE.after(*sb_.free, m_v, m_k0)
                for hh in range(HG):
                    keys = ktok[:, i, hh * P:(hh + 1) * P] if cc == 0 else block(kd, hh)
                    mm = nc.tensor.matmul(sb_.buf[:, hh * P:(hh + 1) * P], keys, block(u, hh), start=True, stop=True)
                m_s = PE.run(mm)
                V.after(m_s, m_o, m_ends)
                for hh in range(HG):
                    m = V.run(nc.vector.scalar_tensor_tensor(
                        out=state[:, hh, :], in0=state[:, hh, :], scalar=ends.buf[:, 2 * hh + cc:2 * hh + cc + 1],
                        in1=sb_.buf[:, hh * P:(hh + 1) * P], op0=ALU.mult, op1=ALU.add))
                c.banks.give(sb_, m)
                st["ready"] = [m]
                yield
            PE.after(m_v, m_attn)
            for hh in range(HG):
                mm = nc.tensor.matmul(ob.buf[:, hh * P:(hh + 1) * P], block(u, hh), block(attn, hh),
                                      start=False, stop=True, skip_group_check=True)
            m_o = PE.run(mm)
            m = c.copy(c.mixed[:, hg * HG:(hg + 1) * HG, tok], g4(ob.buf[:]), [m_o], "act")
            c.banks.give(ob, m)
            c.mixed_ready.append(m)
            c.small.give(ends, V.last())
            for s in (dec, q0, q1, vb, kd, xn, am):
                c.scratch.give(s, m_o, m_k0)
        pipelined((tile(i) for i in range(NT)), 2, every=3)
        c.barrier()

    sums = c.banks.take()
    for h in range(H):
        sq, m = c.square_tile(c.mixed[:, h, :], c.mixed_ready)
        PE.after(m, *sums.free)
        m = PE.run(nc.tensor.matmul(sums.buf[0:8, :], c.const("strip")[:, 15 - h:23 - h], sq.buf[:],
                                    start=h == 0, stop=h == H - 1))
        c.scratch.give(sq, m)
    rows = c.scratch.take()
    V.after(*rows.free)
    A.after(m, V.run(nc.vector.memset(rows.buf[:], 0.0)))
    m = A.run(nc.scalar.activation(rows.buf[0:8, :], sums.buf[0:8, :], ACT.Sqrt, bias=c.eps[0:8, 0:1], scale=1.0 / GD))
    c.banks.give(sums, m)
    V.after(m)
    mr = V.run(nc.vector.reciprocal(rows.buf[0:8, :], rows.buf[0:8, :]))
    done = []
    for hf in range(H // 2):
        slot = c.weight_chunk(w_in, 3 * H * GD + hf * 256, 256)
        for m_ in range(2):
            h = 2 * hf + m_
            zb, m = c.feature_product(slot, m_, c.hT, KD, c.h_ready)
            z = c.scratch.take()
            A.after(m, *z.free)
            m = A.run(nc.scalar.activation(z.buf[:], zb.buf[:], ACT.Silu))
            c.banks.give(zb, m)
            bank = c.banks.take()
            PE.after(mr, *bank.free)
            m1 = PE.run(nc.tensor.matmul(bank.buf[:], c.const("ident")[:, h:h + 1].to_broadcast([P, P]),
                                         rows.buf[:], start=True, stop=True))
            V.after(m1)
            m1 = V.run(nc.vector.scalar_tensor_tensor(out=c.mixed[:, h, :], in0=c.mixed[:, h, :],
                                                      scalar=c.col["gdn_norm"], in1=bank.buf[:],
                                                      op0=ALU.mult, op1=ALU.mult))
            c.banks.give(bank, m1)
            V.after(m, m1)
            m = V.run(nc.vector.tensor_tensor(c.mixed[:, h, :], c.mixed[:, h, :], z.buf[:], ALU.mult))
            c.scratch.give(z, m)
            done.append(m)
        c.weights.give(slot, PE.last())
    c.scratch.give(rows, PE.last())
    c.h_free = [PE.last()]
    c.mixed_ready = done
    c.barrier()
    c.scratch.slots = [s for s in c.scratch.slots if s in c.own_scratch]


def build(nc, io, at, out):
    with ExitStack() as ctx:
        c = Core(nc, ctx, io, at)
        c.own_scratch = list(c.scratch.slots)
        c.negmax = c.sb("negmax", [P, GROUPS, NT, DIL_H])
        c.den = c.sb("den", [P, GROUPS, NT, DIL_H])
        c.gate_cols = c.sb("gate_cols", [P, 8, NT, H])
        c.state = c.sb("state", [P, 4, GD])
        dram = lambda name, shape: nc.dram_tensor(name, shape, F32).ap()
        c.h2_dram, c.y_dram = dram("h2_dram", [S, D]), dram("y_dram", [NBLK * P, D])
        c.table_dram = dram("table_dram", [NBLK * P, 1])
        setup(c)
        c.mixed_ready = []
        c.norm_residual(lambda k: columns(c.col["norm_attn"], k))
        setup_tables(c)
        c.later.append(c.modulation(0))
        dilated(c)
        mla(c)
        merge(c)
        c.norm_residual(lambda k: columns(c.col["norm_ffn"], k))
        moe(c)
        for layer in range(2):
            c.finish_background()
            mod = lambda part, layer=layer: (lambda k: c.mod[:, layer, part, k:k + 1])
            c.DVE.after(c.mod_ready)
            c.ACT.after(c.mod_ready)
            c.norm_residual(mod(1), mod(0))
            if layer == 0:
                c.later.append(c.modulation(1))
            (head_groups if layer == 0 else delta_net)(c)
            w = io["attn_w_out_2"] if layer == 0 else io["gdn_w_out_2"]
            project_out(c, w, c.mixed, KD, c.mixed_ready, gate=mod(2))
            c.norm_residual(mod(4), mod(3))
            swiglu(c, layer)
        c.norm_residual(lambda k: columns(c.col["final"], k))
        sem = c.sem("out_done")
        for k in range(KD):
            c.SP.after(c.h_ready[k])
            nc.sync.dma_start(out[k * P:(k + 1) * P, :], c.hT[:, k, :]).then_inc(sem, 16)
        nc.sync.wait_ge(sem, 16 * KD)


def kernel(**inputs):
    import concourse.bacc as bacc
    from concourse.bass_utils import run_bass_kernel_spmd

    a = {k: np.asarray(v) for k, v in inputs.items()}
    table, at = constants()
    cols = lambda v: np.ascontiguousarray(v.reshape(-1, P).T)
    twice = lambda v: np.ascontiguousarray(np.concatenate([v, v], -1).T)
    column = {
        "norm_attn": cols(a["norm_attn"]), "norm_ffn": cols(a["norm_ffn"]), "b_gate": cols(a["b_gate"]),
        "norm_ckv": cols(a["norm_ckv"]), "norm_mix": cols(a["norm_mix_g_2"]), "norm_ffn2": cols(a["norm_ffn_g_2"]),
        "final": cols(a["final_norm_g_2"]), "c": cols(a["c_2"]), "gdn_norm": cols(a["gdn_norm_g_2"]),
        "qdil": twice(a["q_norm_dil"][0]), "kdil": twice(a["k_norm_dil"][0]),
        "ada_b": cols(a["ada_b_2"]), "conv": cols(a["gdn_conv_w_2"]),
    }
    row = {"qmla": a["q_norm_mla"][0], "kmla": a["k_norm_mla"][0], "b_rg": a["b_router_group"][0],
           "b_re": a["b_router_expert"][0], "a_log": a["gdn_a_log_2"][0], "dt_bias": a["gdn_dt_bias_2"][0]}
    arrays = {
        "consts": table,
        "xT": np.ascontiguousarray(a["x"][0].T),
        "cols": np.ascontiguousarray(np.concatenate([column[name] for name in COLS], 1)),
        "rows": np.ascontiguousarray(np.concatenate([row[name] for name in ROWS])),
        "positions": np.ascontiguousarray(np.concatenate([a["positions"].reshape(NT, P).T,
                                                          a["positions_2"].reshape(NT, P).T], 1)),
    }
    for name in ("w_in", "w_ukv", "w_o_mla", "w_o_dil", "w_out", "w_router_group", "w_router_expert", "w_gate",
                 "w_up", "w_down", "attn_w_in_2", "attn_w_out_2", "gdn_w_in_2", "gdn_w_out_2"):
        arrays[name] = a[name][0]
    for name in ("ada_w_2", "ffn_w_in_2", "ffn_w_out_2"):
        arrays[name] = a[name]
    nc = bacc.Bacc("TRN2", target_bir_lowering=False, num_devices=1)
    io = {n: nc.dram_tensor(n, v.shape, mybir.dt.from_np(v.dtype), kind="ExternalInput").ap()
          for n, v in arrays.items()}
    out = nc.dram_tensor("outT", [D, S], F32, kind="ExternalOutput").ap()
    build(nc, io, at, out)
    got = run_bass_kernel_spmd(nc, [arrays], core_ids=[0]).results[0]["outT"]
    return np.ascontiguousarray(got.T).reshape(1, S, D)
```

```python
from contextlib import ExitStack

import numpy as np
import concourse.bass as bass
from concourse import mybir

F32 = mybir.dt.float32
F32R = mybir.dt.float32r
I32 = mybir.dt.int32
U32 = mybir.dt.uint32
ALU = mybir.AluOpType
ACT = mybir.ActivationFunctionType
AX = mybir.AxisListType

P = 128
S = 512
NT = S // P
D = 1024
KD = D // P
EPS = 1e-6
NEG = -1e30

MLA_H, NOPE, ROPE, MLA_V, KV_RANK = 8, 64, 32, 64, 256
MLA_D = NOPE + ROPE
GROUPS, DIL_H, HD = 3, 8, 64
DIL = (1, 4, 16)
STRIDE = S // P
N_GRP, PER_GRP = 4, 8
NE = N_GRP * PER_GRP
FF = 256
NBLK = 2 * S // P + NE - 1
MOE_WIDTH = 2900 + 8 * D
H = 8
ROPE2 = HD // 4
GD = 128
CONV = 4
CHUNK = 64
LEVELS = 6
SLOT_BITS = 7
HID = -(-8 * D // (3 * 256)) * 256
KH = HID // P

C_MLAQ = 0
C_CKV = MLA_H * MLA_D
C_DIL = C_CKV + KV_RANK + ROPE
C_GATE = C_DIL + 3 * GROUPS * DIL_H * HD


def constants():
    r = np.arange(P)
    part, col = r[:, None], r[None, :]
    chunk = part // CHUNK == col // CHUNK
    strip = np.zeros((P, 31), np.float32)
    strip[:, 15] = 1
    i, j = r[:, None], np.arange(2 * P)[None, :]
    delta = i + P - j
    far = -NEG
    dist0 = np.where((delta >= 0) & (delta <= P), delta, far)
    dist1 = np.where(col <= part, (part - col) * DIL[1], far)
    same = (part - col) % (DIL[2] // STRIDE) == 0
    dist2 = np.where(same & (col <= part), (part - col) * STRIDE, far)
    slopes = 2.0 ** (-8.0 * (np.arange(DIL_H) + 1.0) / DIL_H)
    levels = [((col >> l) % 2 == 1) & ((part >> l) % 2 == 0) & (col >> (l + 1) == part >> (l + 1))
              for l in range(LEVELS)]
    half, half2 = ROPE // 2, ROPE2 // 2
    f1 = np.float32(10000.0) ** (-np.arange(half, dtype=np.float32) / np.float32(half))
    f2 = np.float32(500000.0) ** (-np.arange(half2, dtype=np.float32) * np.float32(2.0) / np.float32(ROPE2))
    parts = {
        "ident": np.eye(P), "ones": np.ones((P, P)),
        "before": part < col,
        "chunk_upto": chunk & (part <= col),
        "chunk_all": chunk,
        "neg_from": -(part >= col).astype(np.float32),
        "neg_ones": -np.ones((P, P)),
        "sb_keep": part < col,
        "sb_mask": np.where(part < col, 0.0, NEG),
        "causal": np.where(col <= part, 0.0, NEG),
        "levels": np.concatenate(levels, 1),
        "strip": strip,
        "freq1": np.tile(f1, (P, 1)), "freq2": np.tile(f2, (P, 1)),
        "expert": np.tile(np.arange(NE), (P, 1)), "group": np.tile(np.arange(8), (P, 1)),
        "block": np.tile(np.arange(NBLK), (P, 1)),
        "thresholds": np.tile(P * np.arange(NT), (P, 1)),
        "token": r[:, None] + P * np.arange(NT)[None, :],
        "dist0": dist0, "dist1": dist1, "dist2": dist2,
        "slope": np.concatenate([-s * np.eye(P) for s in slopes], 1),
        "slot": np.tile(np.arange(P), (P, 1)),
    }
    at, n, out = {}, 0, []
    for name, a in parts.items():
        a = np.asarray(a, np.float32)
        at[name] = (n, a.shape[1])
        n += a.shape[1]
        out.append(a)
    return np.ascontiguousarray(np.concatenate(out, 1)), at


def offsets(widths):
    out, at = {}, 0
    for name, n in widths:
        out[name] = (at, n)
        at += n
    return out


COLS = offsets([("norm_attn", KD), ("norm_ffn", KD), ("b_gate", 2 * KD), ("norm_ckv", KV_RANK // P),
                ("norm_mix", 2 * KD), ("norm_ffn2", 2 * KD), ("final", KD), ("c", KD), ("gdn_norm", 1),
                ("qdil", GROUPS), ("kdil", GROUPS), ("ada_b", 2 * 6 * KD), ("conv", CONV * 3 * H)])
ROWS = offsets([("qmla", MLA_D), ("kmla", MLA_D), ("b_rg", N_GRP), ("b_re", NE), ("a_log", H), ("dt_bias", H)])


class Queue:

    def __init__(self, engine, sem):
        self.engine, self.sem, self.count, self.waited = engine, sem, 0, {}

    def after(self, *marks):
        for sem, value in marks:
            if self.waited.get(sem.name, 0) < value:
                self.engine.wait_ge(sem, value)
                self.waited[sem.name] = value
        return self

    def run(self, instruction):
        instruction.then_inc(self.sem, 1)
        self.count += 1
        return self.sem, self.count

    def last(self):
        return (self.sem, self.count) if self.count else None


class Slot:

    def __init__(self, buf):
        self.buf, self.free = buf, []


class Ring:

    def __init__(self, bufs):
        self.slots = [Slot(b) for b in bufs]

    def take(self):
        return self.slots.pop(0)

    def give(self, slot, *marks):
        slot.free = list(marks)
        self.slots.append(slot)


class Loads:

    def __init__(self, queue, bufs, sems):
        self.queue = queue
        self.ring = Ring(bufs)
        self.sems = dict(zip([id(s) for s in self.ring.slots], sems))
        self.counts = {id(s): 0 for s in self.ring.slots}

    def load(self, view, source, *marks):
        slot = self.ring.take()
        self.queue.after(*slot.free, *marks)
        self.queue.engine.dma_start(view(slot.buf), source).then_inc(self.sems[id(slot)], 16)
        self.counts[id(slot)] += 16
        slot.ready = (self.sems[id(slot)], self.counts[id(slot)])
        return slot

    def give(self, slot, *marks):
        self.ring.give(slot, *marks)

    def extend(self, bufs, sems, marks):
        new = [Slot(b) for b in bufs]
        for slot, sem in zip(new, sems):
            slot.free = list(marks)
            self.sems[id(slot)], self.counts[id(slot)] = sem, 0
            self.ring.slots.append(slot)
        return new

    def drop(self, slots):
        self.ring.slots = [s for s in self.ring.slots if s not in slots]


def pipelined(jobs, depth, background=None, every=1):
    jobs, live = iter(jobs), []
    more, rounds = True, 0
    while more or live:
        rounds += 1
        if more and len(live) < depth and (rounds % every == 0 or not live):
            job = next(jobs, None)
            more = job is not None
            if more:
                live.append(job)
        going = {id(j): next(j, "done") != "done" for j in reversed(live)}
        live = [j for j in live if going[id(j)]]
        if background is not None:
            background()


class Core:

    def __init__(self, nc, ctx, io, at):
        self.nc, self.ctx, self.io, self.at = nc, ctx, io, at
        self.areas, self.nareas = [ctx], 0
        self.nsem = 0
        self.PE = Queue(nc.tensor, self.sem("pe_done"))
        self.ACT = Queue(nc.scalar, self.sem("act_done"))
        self.DVE = Queue(nc.vector, self.sem("dve_done"))
        self.POOL = Queue(nc.gpsimd, self.sem("pool_done"))
        self.SP = Queue(nc.sync, self.sem("sp_done"))
        self.banks = Ring([ctx.enter_context(nc.psum_tensor(f"bank{i}", [P, 512], F32)) for i in range(8)])
        nw = 4
        self.weights = Loads(self.SP, [self.sb(f"weights{i}", [P, 2048]) for i in range(nw)],
                             [self.sem(f"weights{i}_in") for i in range(nw)])
        self.scratch = Ring([self.sb(f"scratch{i}", [P, 512]) for i in range(13)])
        self.small = Ring([self.sb(f"small{i}", [P, 32]) for i in range(12)])
        self.xT = self.sb("xT", [P, KD, S])
        self.mod = self.sb("mod", [P, 2, 6, KD])
        self.cols = self.sb("cols", [P, sum(n for _, n in COLS.values())])
        self.x_ready = [[] for _ in range(KD)]
        self.h_ready = []
        self.h_free = []
        self.later = []

    def sem(self, name):
        return self.ctx.enter_context(self.nc.semaphore(name))

    def sb(self, name, shape, dt=F32):
        if len(self.areas) > 1:
            name = f"{name}_{self.nareas}"
        return self.areas[-1].enter_context(self.nc.sbuf_tensor("sb_" + name, shape, dt))

    def open_area(self):
        self.barrier()
        self.areas.append(ExitStack())
        self.nareas += 1

    def close_area(self):
        self.barrier()
        self.areas.pop().close()

    def attention_area(self):
        self.open_area()
        self.hT = self.sb("hT", [P, KD, S])
        self.mixed = self.sb("mixed", [P, KD, S])

    def open_scores_area(self):
        self.open_area()
        self.arena = self.sb("arena", [P, 24 * S])
        self.padded = Ring([self.sb(f"padded_q{i}", [P, H, P]) for i in range(2)])
        marks = self.engine_marks()
        self.extra = self.weights.extend([self.sb(f"more_weights{i}", [P, 2048]) for i in range(3)],
                                         [self.sem(f"more_weights{i}_in{self.nareas}") for i in range(3)], marks)
        for slot in self.padded.slots:
            slot.free = [self.DVE.run(self.nc.vector.memset(slot.buf[:], 0.0))]

    def close_scores_area(self):
        self.weights.drop(self.extra)
        self.close_area()

    def split_area(self, n):
        self.splits = Ring([(self.sb(f"w_hi{i}", [P, KD, P], F32R), self.sb(f"w_lo{i}", [P, KD, P], F32R))
                            for i in range(n)])

    def pair(self, name, n):
        return self.sb(name + "_hi", [P, n, S], F32R), self.sb(name + "_lo", [P, n, S], F32R)

    def engine_marks(self):
        return [q.last() for q in (self.PE, self.ACT, self.DVE, self.POOL) if q.last()]

    def const(self, name, rows=P):
        a, n = self.at[name]
        if a >= self.at["dist0"][0]:
            a -= self.at["dist0"][0]
            return self.mixed[:, 0:3, :].rearrange("p a t -> p (a t)")[0:rows, a:a + n]
        return self.consts[0:rows, a:a + n]

    def barrier(self):
        marks = self.engine_marks()
        for q in (self.PE, self.ACT, self.DVE, self.POOL):
            q.after(*marks)

    def load_once(self, queue, dst, src, name):
        sem = self.sem(name)
        queue.engine.dma_start(dst, src).then_inc(sem, 16)
        return sem, 16

    def weight_chunk(self, w, c0, n, kt=KD, k0=0):
        src = w[k0 * P:(k0 + kt) * P, c0:c0 + n].rearrange("(k p) n -> p k n", p=P)
        slot = self.weights.load(lambda b: b[:, 0:kt * n].rearrange("p (k n) -> p k n", k=kt), src)
        slot.w = slot.buf[:, 0:kt * n].rearrange("p (k n) -> p k n", k=kt)
        return slot

    def router_chunk(self):
        n = N_GRP + NE
        view = lambda b, c0, w: b[:, 0:KD * n].rearrange("p (k n) -> p k n", k=KD)[:, :, c0:c0 + w]
        src = lambda name: self.io[name].rearrange("(k p) n -> p k n", p=P)
        slot = self.weights.load(lambda b: view(b, 0, N_GRP), src("w_router_group"))
        sem = slot.ready[0]
        self.SP.engine.dma_start(view(slot.buf, N_GRP, NE), src("w_router_expert")).then_inc(sem, 16)
        self.weights.counts[id(slot)] += 16
        slot.ready = (sem, slot.ready[1] + 16)
        slot.w = view(slot.buf, 0, n)
        return slot

    def feature_product(self, slot, m, actT, kt, marks, bank=None, first=True, last=True):
        nc, PE = self.nc, self.PE
        if bank is None:
            bank = self.banks.take()
            PE.after(*bank.free)
        PE.after(slot.ready, *marks)
        n = min(P, slot.w.shape[-1])
        for k in range(kt):
            mm = nc.tensor.matmul(bank.buf[0:n, :], slot.w[:, k, m * P:m * P + n], actT[:, k, :],
                                  start=first and k == 0, stop=last and k == kt - 1)
        return bank, PE.run(mm)

    def token_product(self, slot, n, toks, kt, marks, c0=0, bank=None, at=0):
        nc, PE = self.nc, self.PE
        if bank is None:
            bank = self.banks.take()
            PE.after(*bank.free)
        PE.after(slot.ready, *marks)
        for k in range(kt):
            mm = nc.tensor.matmul(bank.buf[:, at:at + n], toks(k), slot.w[:, k, c0:c0 + n],
                                  start=k == 0, stop=k == kt - 1)
        return bank, PE.run(mm)

    def split(self, hi, lo, src, marks, free=()):
        nc, A, V = self.nc, self.ACT, self.DVE
        A.after(*marks, *free)
        m = A.run(nc.scalar.copy(hi, src))
        V.after(m)
        return V.run(nc.vector.tensor_tensor(lo, src, hi.bitcast(F32), ALU.subtract))

    def split_weights(self, w, c0, kt=KD, k0=0):
        raw = self.weight_chunk(w, c0, P, kt=kt, k0=k0)
        s = self.splits.take()
        hi, lo = s.buf
        m = self.split(hi[:, 0:kt, :], lo[:, 0:kt, :], raw.w, [raw.ready], s.free)
        self.weights.give(raw, m)
        s.ready = m
        return s

    def split_product(self, s, act, kt, marks, bank=None, first=True, last=True):
        nc, PE = self.nc, self.PE
        if bank is None:
            bank = self.banks.take()
            PE.after(*bank.free)
        PE.after(s.ready)
        terms = ((0, 0), (0, 1), (1, 0))
        for k in range(kt):
            PE.after(marks[k])
            for t, (a, b) in enumerate(terms):
                mm = nc.tensor.matmul(bank.buf[:], s.buf[a][:, k, :], act[b][:, k, :],
                                      start=first and k == 0 and t == 0, stop=last and k == kt - 1 and t == 2)
        m = PE.run(mm)
        self.splits.give(s, m)
        return bank, m

    def inv_rms_rows(self, squares, n, width):
        nc, PE, A, V = self.nc, self.PE, self.ACT, self.DVE
        bank = self.banks.take()
        PE.after(*bank.free)
        for k in range(n):
            sq, mark = squares(k)
            PE.after(mark)
            mm = PE.run(nc.tensor.matmul(bank.buf[:], self.const("ones"), sq.buf[:],
                                         start=k == 0, stop=k == n - 1))
            self.scratch.give(sq, mm)
        rms = self.scratch.take()
        A.after(mm, *rms.free)
        got = A.run(nc.scalar.activation(rms.buf[:], bank.buf[:], ACT.Sqrt, bias=self.eps[:, 0:1], scale=1.0 / width))
        self.banks.give(bank, got)
        V.after(got)
        return rms, V.run(nc.vector.reciprocal(rms.buf[:], rms.buf[:]))

    def square_tile(self, src, marks):
        sq = self.scratch.take()
        self.ACT.after(*marks, *sq.free)
        return sq, self.ACT.run(self.nc.scalar.activation(sq.buf[:], src, ACT.Square))

    def norm_residual(self, gain, shift=None, split=None):
        nc, V, A = self.nc, self.DVE, self.ACT
        inv, ready = self.inv_rms_rows(lambda k: self.square_tile(self.xT[:, k, :], self.x_ready[k]), KD, D)
        V.after(ready, *self.h_free)
        self.h_ready, self.h_free = [], []
        halves = []

        def rest(k, slot, rounded):
            V.after(rounded)
            done = V.run(nc.vector.scalar_tensor_tensor(
                out=split[1][:, k, :], in0=slot.buf[:], scalar=shift(k), in1=split[0][:, k, :].bitcast(F32),
                op0=ALU.add, op1=ALU.subtract))
            self.scratch.give(slot, done)
            self.h_ready.append(done)
        for k in range(KD):
            slot = self.scratch.take() if split else None
            h = slot.buf[:] if split else self.hT[:, k, :]
            if split:
                V.after(*slot.free)
            done = V.run(nc.vector.scalar_tensor_tensor(out=h, in0=self.xT[:, k, :], scalar=gain(k),
                                                        in1=inv.buf[:], op0=ALU.mult, op1=ALU.mult))
            if not split:
                if shift is not None:
                    A.after(done)
                    done = A.run(nc.scalar.activation(h, h, ACT.Identity, bias=shift(k)))
                self.h_ready.append(done)
                continue
            A.after(done)
            done = A.run(nc.scalar.activation(split[0][:, k, :], h, ACT.Identity, bias=shift(k)))
            halves.append((k, slot, done))
            if k > 0:
                rest(*halves[k - 1])
        if split:
            rest(*halves[-1])
        self.scratch.give(inv, self.h_ready[-1], V.last())

    def inv_rms_small(self, sums, width, mark, eps=True):
        nc, A, V = self.nc, self.ACT, self.DVE
        A.after(mark)
        got = A.run(nc.scalar.activation(sums, sums, ACT.Sqrt, bias=self.eps[:, 0:1], scale=1.0 / width))
        V.after(got)
        return V.run(nc.vector.reciprocal(sums, sums))

    def head_norm(self, src, heads, width, out, marks):
        nc, A, V = self.nc, self.ACT, self.DVE
        sq, ss = self.scratch.take(), self.small.take()
        A.after(*marks, *sq.free)
        sq3 = sq.buf[:, 0:heads * width].rearrange("p (h d) -> p h d", h=heads)
        m = A.run(nc.scalar.activation(sq3, src, ACT.Square))
        V.after(m, *ss.free)
        m = V.run(nc.vector.tensor_reduce(ss.buf[:, 0:heads], sq3, AX.X, ALU.add))
        self.scratch.give(sq, m)
        m = self.inv_rms_small(ss.buf[:, 0:heads], width, m)
        V.after(m)
        scale = ss.buf[:, 0:heads].unsqueeze(2).to_broadcast([P, heads, width])
        m = V.run(nc.vector.tensor_tensor(out, src, scale, ALU.mult))
        self.small.give(ss, m)
        return m

    def rope(self, t1, t2, cos, sin, heads, half, marks):
        nc, G = self.nc, self.POOL
        tmp = self.scratch.take()
        n = heads * half
        view = lambda i: tmp.buf[:, i * n:(i + 1) * n].rearrange("p (h d) -> p h d", h=heads)
        cosb = cos.unsqueeze(1).to_broadcast([P, heads, half])
        sinb = sin.unsqueeze(1).to_broadcast([P, heads, half])
        G.after(*marks, *tmp.free)
        for i, (t, f) in enumerate(((t1, cosb), (t2, sinb), (t2, cosb), (t1, sinb))):
            m = G.run(nc.gpsimd.tensor_tensor(view(i), t, f, ALU.mult))
        G.after(m)
        G.run(nc.gpsimd.tensor_tensor(t1, view(0), view(1), ALU.subtract))
        m = G.run(nc.gpsimd.tensor_tensor(t2, view(2), view(3), ALU.add))
        self.scratch.give(tmp, m)
        return m

    def transpose_blocks(self, blocks, rows, marks):
        nc, PE = self.nc, self.PE
        bank = self.banks.take()
        PE.after(*bank.free, *marks)
        for i, b in enumerate(blocks):
            mm = nc.tensor.transpose(bank.buf[0:rows, i * P:(i + 1) * P], b, self.const("ident"))
        return bank, PE.run(mm)

    def copy(self, out, src, marks, on=None):
        self.turn = not self.turn
        if on == "act" or (on is None and self.turn):
            self.ACT.after(*marks)
            return self.ACT.run(self.nc.scalar.copy(out, src))
        self.DVE.after(*marks)
        return self.DVE.run(self.nc.vector.tensor_copy(out, src))

    turn = False

    def add_residual(self, bank, m, j, gate=None):
        nc, V = self.nc, self.DVE
        V.after(m, *self.x_ready[j])
        x = self.xT[:, j, :]
        if gate is None:
            done = V.run(nc.vector.tensor_tensor(x, bank.buf[:], x, ALU.add))
        else:
            done = V.run(nc.vector.scalar_tensor_tensor(out=x, in0=bank.buf[:], scalar=gate, in1=x,
                                                        op0=ALU.mult, op1=ALU.add))
        self.banks.give(bank, done)
        self.x_ready[j] = [done]

    def idle(self):
        while self.later and next(self.later[0], "done") == "done":
            self.later.pop(0)

    def finish_background(self):
        while self.later:
            self.idle()

    def softmax_job(self, query, k, blocks, bias, scale, values, out, negmax, den, marks, done):
        nc, PE, A, V = self.nc, self.PE, self.ACT, self.DVE
        n = blocks * P
        bank = self.banks.take()
        q, q_marks = query()
        PE.after(*bank.free, *marks, *q_marks)
        nc.tensor.matmul(bank.buf[:, 0:n], q, k, start=True, stop=False)
        for i, (left, right, c) in enumerate(bias):
            w = right.shape[-1]
            mm = nc.tensor.matmul(bank.buf[:, c:c + w], left, right, start=False, stop=i == len(bias) - 1)
        m = PE.run(mm)
        V.after(m)
        m = V.run(nc.vector.tensor_reduce(negmax, bank.buf[:, 0:n], AX.X, ALU.max, negate=True))
        if scale != 1.0:
            V.after(m)
            m = V.run(nc.vector.tensor_scalar(negmax, negmax, scale, None, ALU.mult))
        p = self.scratch.take()
        A.after(m, *p.free)
        m = A.run(nc.scalar.activation(p.buf[:, 0:n], bank.buf[:, 0:n], ACT.Exp, bias=negmax, scale=scale,
                                       accum_out=den))
        self.banks.give(bank, m)
        yield
        yield
        tbank, m = self.transpose_blocks([p.buf[:, b * P:(b + 1) * P] for b in range(blocks)], P, [m])
        self.scratch.give(p, m)
        pT = self.scratch.take()
        m = self.copy(pT.buf[:, 0:n], tbank.buf[:, 0:n], [m, *pT.free])
        self.banks.give(tbank, m)
        yield
        yield
        target = out()
        PE.after(m)
        for b in range(blocks):
            mm = nc.tensor.matmul(target, pT.buf[:, b * P:(b + 1) * P], values(b), start=b == 0, stop=b == blocks - 1)
        m = PE.run(mm)
        self.scratch.give(pT, m)
        yield from done(m)

    def pad_queries(self, q, cols, marks):
        slot = self.padded.take()
        done = [self.copy(slot.buf[rows, r:H:2, :], q[rows, :, cols], [*slot.free, *marks])
                for r, rows in enumerate((slice(0, HD), slice(HD, P)))]
        return slot, done

    def head_pair_banks(self):
        pair = self.banks.take(), self.banks.take()
        self.PE.after(*pair[0].free, *pair[1].free)
        return pair

    @staticmethod
    def pair_columns(pair, h):
        return pair[h % 2].buf[:, (h // 2) * P:(h // 2 + 1) * P]

    @staticmethod
    def kept(buf, r):
        return buf.rearrange("p (a r d) -> p a r d", a=4, r=2)[:, :, r, :]

    def angles(self, pos, freq, n, cos, sin):
        nc, V, A = self.nc, self.DVE, self.ACT
        PI = float(np.float32(3.1415925))
        TWO_PI, ROUND = 6.283185307179586, 12582912.0
        parts = [6.28125, 0.0019350051879882812, TWO_PI - 6.28125 - 0.0019350051879882812]
        a, t, r = self.scratch.take(), self.scratch.take(), self.scratch.take()
        V.after(*a.free, *t.free, *r.free)
        w = NT * n
        yield
        for i in range(NT):
            m = V.run(nc.vector.tensor_scalar(a.buf[:, i * n:(i + 1) * n], freq, pos[:, i:i + 1], None, ALU.mult))
        for out, turn, add in ((sin, 0.0, 0.0), (cos, 0.25, TWO_PI / 4)):
            yield
            V.after(m)
            m = V.run(nc.vector.tensor_scalar(t.buf[:, 0:w], a.buf[:, 0:w], 1 / TWO_PI, turn, ALU.mult, ALU.add))
            V.after(m)
            m = V.run(nc.vector.tensor_scalar(t.buf[:, 0:w], t.buf[:, 0:w], ROUND, None, ALU.add))
            V.after(m)
            m = V.run(nc.vector.tensor_scalar(t.buf[:, 0:w], t.buf[:, 0:w], -ROUND, None, ALU.add))
            src = a
            for c in parts:
                yield
                V.after(m)
                m = V.run(nc.vector.scalar_tensor_tensor(out=r.buf[:, 0:w], in0=t.buf[:, 0:w], scalar=-c,
                                                         in1=src.buf[:, 0:w], op0=ALU.mult, op1=ALU.add))
                src = r
            V.after(m)
            m = V.run(nc.vector.tensor_scalar(r.buf[:, 0:w], r.buf[:, 0:w], float(add), PI, ALU.add, ALU.min))
            V.after(m)
            m = V.run(nc.vector.tensor_scalar(r.buf[:, 0:w], r.buf[:, 0:w], -PI, None, ALU.max))
            A.after(m)
            m = A.run(nc.scalar.activation(out.rearrange("p t f -> p (t f)"), r.buf[:, 0:w], ACT.Sin))
        for s in (a, t, r):
            self.scratch.give(s, m)
        self.rope_ready = m

    def modulation(self, layer):
        nc, PE, V = self.nc, self.PE, self.DVE
        W = 256
        out = self.mod[:, layer, :, :].rearrange("p s k -> p (s k)")
        for c in range(6 * D // W):
            slot = self.weight_chunk(self.io["ada_w_2"][layer], c * W, W)
            acc = self.scratch.take()
            V.after(slot.ready, *acc.free, self.cond_ready)
            m = V.run(nc.vector.tensor_scalar(acc.buf[:, 0:W], slot.w[:, 0, :], self.cond[:, 0:1], None, ALU.mult))
            for k in range(1, KD):
                V.after(m)
                m = V.run(nc.vector.scalar_tensor_tensor(out=acc.buf[:, 0:W], in0=slot.w[:, k, :],
                                                         scalar=self.cond[:, k:k + 1], in1=acc.buf[:, 0:W],
                                                         op0=ALU.mult, op1=ALU.add))
                if k % 4 == 3 and k < KD - 1:
                    yield
            self.weights.give(slot, m)
            yield
            bank = self.banks.take()
            PE.after(m, *bank.free)
            for j in range(W // P):
                mm = nc.tensor.matmul(bank.buf[:, j * P:(j + 1) * P], acc.buf[:, j * P:(j + 1) * P],
                                      self.const("ones"), start=True, stop=True)
            m = PE.run(mm)
            self.scratch.give(acc, m)
            V.after(m)
            n = W // P
            m = V.run(nc.vector.tensor_tensor(out[:, c * n:(c + 1) * n],
                                              bank.buf[:, 0:W].rearrange("p (j t) -> p j t", j=n)[:, :, 0],
                                              self.ada_b[:, layer, c * n:(c + 1) * n], ALU.add))
            self.banks.give(bank, m)
            yield
        for s, g in ((1, self.col["norm_mix"]), (4, self.col["norm_ffn2"])):
            V.after(m)
            gain = g[:, layer * KD:(layer + 1) * KD]
            m = V.run(nc.vector.scalar_tensor_tensor(out=self.mod[:, layer, s, :], in0=self.mod[:, layer, s, :],
                                                     scalar=1.0, in1=gain, op0=ALU.add, op1=ALU.mult))
        self.mod_ready = m


def setup(c):
    nc, io = c.nc, c.io
    ncst = c.at["dist0"][0]
    c.consts = c.sb("consts", [P, ncst])
    c.consts_in = c.load_once(c.SP, c.consts[:], io["consts"][:, 0:ncst], "consts_in")
    x_in = [c.load_once(c.SP, c.xT[:, k, :], io["xT"][k * P:(k + 1) * P, :], f"x{k}_in") for k in range(KD)]
    nrow = sum(n for _, n in ROWS.values())
    c.rows = c.sb("rows", [P, nrow])
    c.pos = c.sb("pos", [P, 2 * NT], I32)
    c.eps = c.sb("eps", [P, 1])
    c.posf = c.sb("posf", [P, 2 * NT])
    c.cos1, c.sin1 = c.sb("cos1", [P, NT, ROPE // 2]), c.sb("sin1", [P, NT, ROPE // 2])
    c.cos2, c.sin2 = c.sb("cos2", [P, NT, ROPE2 // 2]), c.sb("sin2", [P, NT, ROPE2 // 2])
    c.cond = c.sb("cond", [P, KD])
    c.attention_area()
    c.dilated_consts_in = c.load_once(c.SP, c.mixed[:, 0:3, :].rearrange("p a t -> p (a t)"),
                                      io["consts"][:, ncst:c.at["slot"][0]], "dilated_consts_in")
    c.x_ready = [[m] for m in x_in]
    c.col = {name: c.cols[:, i:i + n] for name, (i, n) in COLS.items()}
    c.ada_b = c.col["ada_b"].rearrange("p (l j) -> p l j", l=2)
    c.conv_w = c.col["conv"].rearrange("p (t j) -> p t j", t=CONV)
    c.row = {name: c.rows[:, i:i + n] for name, (i, n) in ROWS.items()}
    sem = c.sem("parameters_in")
    for dst, src in ((c.cols[:], io["cols"]), (c.rows[:], io["rows"].partition_broadcast(P)), (c.pos[:], io["positions"])):
        nc.gpsimd.dma_start(dst, src).then_inc(sem, 16)
    c.small_in = (sem, 48)
    m = c.DVE.run(nc.vector.memset(c.eps[:], EPS))
    c.PE.after(c.consts_in)
    c.ACT.after(m)
    c.DVE.after(c.consts_in, c.small_in)
    c.ACT.after(c.small_in)
    c.POOL.after(c.small_in, c.consts_in)


def setup_tables(c):
    nc = c.nc
    m = c.DVE.run(nc.vector.tensor_copy(c.posf[:], c.pos[:]))
    m = c.DVE.run(nc.vector.tensor_scalar(c.col["qdil"], c.col["qdil"], HD ** -0.5, None, ALU.mult))
    c.DVE.after(m)
    c.ACT.after(m)
    c.cond_ready = c.ACT.run(nc.scalar.activation(c.cond[:], c.col["c"], ACT.Silu))
    c.later.append(c.angles(c.posf[:, 0:NT], c.const("freq1"), ROPE // 2, c.cos1[:], c.sin1[:]))
    c.later.append(c.angles(c.posf[:, NT:2 * NT], c.const("freq2"), ROPE2 // 2, c.cos2[:], c.sin2[:]))


def columns(table, j):
    return table[:, j:j + 1]


def folded(g, i):
    return slice(i * P, (i + 1) * P) if g == 0 else slice(i, S, STRIDE)


def fold(c, g, i):
    return lambda k: c.hT[:, k, folded(g, i)]


def dilated(c):
    nc, PE, A, V, G = c.nc, c.PE, c.ACT, c.DVE, c.POOL
    w_in = c.io["w_in"]
    WD = DIL_H * HD
    q, k, v = (c.arena[:, j * 4 * S:(j + 1) * 4 * S].rearrange("p (a t) -> p a t", a=4) for j in range(3))
    outs = [c.arena[:, (3 + g) * 4 * S:(4 + g) * 4 * S].rearrange("p (a t) -> p a t", a=4) for g in range(GROUPS)]
    negmax, den = (c.sb(name, [P, GROUPS, NT, DIL_H]) for name in ("negmax", "den"))
    c.PE.after(c.dilated_consts_in)
    free = []
    for g in range(GROUPS):
        ready = []

        def projections(g=g, ready=ready, free=free):
            for part, dst in ((0, q), (1, k), (2, v)):
                for half in range(2):
                    slot = c.weight_chunk(w_in, C_DIL + (part * GROUPS + g) * WD + half * 256, 256)
                    for i in range(NT):
                        yield tile(i, slot, half, dst, part, g, ready, free)

        def tile(i, slot, half, dst, part, g, ready, free):
            heads = DIL_H // 2
            bank, m = c.token_product(slot, 256, fold(c, g, i), KD, c.h_ready)
            if i == NT - 1:
                c.weights.give(slot, m)
            yield
            if part == 2:
                m = c.copy(v[:, i, half * 256:(half + 1) * 256], bank.buf[:, 0:256], [m, *free])
                c.banks.give(bank, m)
                ready.append(m)
                return
            n = c.scratch.take()
            V.after(*n.free)
            src = bank.buf[:, 0:256].rearrange("p (h d) -> p h d", h=heads)
            m = c.head_norm(src, heads, HD, n.buf[:, 0:256].rearrange("p (h d) -> p h d", h=heads), [m])
            c.banks.give(bank, m)
            yield
            yield
            tb, m = c.transpose_blocks([n.buf[:, j * P:(j + 1) * P] for j in range(2)], P, [m])
            c.scratch.give(n, m)
            gain = columns(c.col["qdil" if part == 0 else "kdil"], g)
            A.after(m, *free)
            m = A.run(nc.scalar.activation(dst[:, 2 * half:2 * half + 2, i * P:(i + 1) * P],
                                           tb.buf[:, 0:256].rearrange("p (a t) -> p a t", a=2),
                                           ACT.Identity, scale=gain))
            c.banks.give(tb, m)
            ready.append(m)
        pipelined(projections(), 4, c.idle)

        last = []

        def heads_of(g=g, ready=ready, last=last):
            for i in range(NT):
                lo = i - 1 if g == 0 and i > 0 else i
                tile_ = {}
                for h in range(DIL_H):
                    yield head(g, i, lo, h, tile_, ready, last)

        def head(g, i, lo, h, t, ready, last):
            blocks = i - lo + 1
            dist = c.const(f"dist{g}")
            bias = [(c.const("slope")[:, h * P:(h + 1) * P], dist[:, (2 - blocks) * P:] if g == 0 else dist, 0)]

            def query():
                if h == 0:
                    t["q"], t["q_in"] = c.pad_queries(q, slice(i * P, (i + 1) * P), ready)
                return t["q"].buf[:, h, :], t["q_in"]

            def out():
                if h == 0:
                    t["out"] = c.head_pair_banks()
                if h == DIL_H - 1:
                    c.padded.give(t["q"], c.PE.last())
                return c.pair_columns(t["out"], h)

            def done(m):
                if h < DIL_H - 1:
                    return
                for r in range(2):
                    mc = c.copy(c.kept(outs[g][:, i, :], r), c.kept(t["out"][r].buf[:], r), [m])
                    c.banks.give(t["out"][r], mc)
                    last.append(mc)
                last.append(m)
                yield
            return c.softmax_job(query, k[:, h // 2, lo * P:(i + 1) * P], blocks, bias, 1.0,
                                 lambda b: v[:, lo + b, (h // 2) * P:(h // 2 + 1) * P], out,
                                 negmax[:, g, i, h:h + 1], den[:, g, i, h:h + 1], ready, done)
        pipelined(heads_of(), 6, c.idle)
        free = last
    t8 = c.arena[0:DIL_H, 0:7 * S].rearrange("p (a t) -> p a t", a=7)
    c.barrier()
    gathered = []
    for n, src in enumerate((negmax, den)):
        for g in range(GROUPS):
            bank = c.banks.take()
            PE.after(*bank.free)
            for i in range(NT):
                mm = nc.tensor.transpose(bank.buf[0:DIL_H, i * P:(i + 1) * P], src[:, g, i, :], c.const("ident"))
            m = PE.run(mm)
            dst, rows = t8[:, n * GROUPS + g, :], bank.buf[0:DIL_H, :]
            if g > 0:
                dst = dst.rearrange("p (t i) -> p i t", i=NT)
                rows = rows.rearrange("p (i t) -> p i t", i=NT)
            gathered.append(c.copy(dst, rows, [m]))
            c.banks.give(bank, gathered[-1])
    low = t8[:, 6, :]
    V.after(*gathered)
    m = V.run(nc.vector.tensor_tensor(low, t8[:, 0, :], t8[:, 1, :], ALU.min))
    V.after(m)
    m = V.run(nc.vector.tensor_tensor(low, low, t8[:, 2, :], ALU.min))
    for g in range(GROUPS):
        V.after(m)
        m = V.run(nc.vector.tensor_tensor(t8[:, g, :], low, t8[:, g, :], ALU.subtract))
    A.after(m)
    m = A.run(nc.scalar.activation(t8[:, 0:3, :], t8[:, 0:3, :], ACT.Exp))
    V.after(m)
    m = V.run(nc.vector.tensor_tensor(t8[:, 3:6, :], t8[:, 0:3, :], t8[:, 3:6, :], ALU.mult))
    V.after(m)
    m = V.run(nc.vector.tensor_tensor(low, t8[:, 3, :], t8[:, 4, :], ALU.add))
    V.after(m)
    m = V.run(nc.vector.tensor_tensor(low, low, t8[:, 5, :], ALU.add))
    V.after(m)
    m = V.run(nc.vector.reciprocal(low, low))
    V.after(m)
    m = V.run(nc.vector.tensor_tensor(t8[:, 0:3, :], t8[:, 0:3, :],
                                      low.unsqueeze(1).to_broadcast([DIL_H, 3, S]), ALU.mult))
    bank = c.banks.take()
    PE.after(m, *bank.free)
    for g in range(GROUPS):
        for i in range(NT):
            at = (g * NT + i) * DIL_H
            mm = nc.tensor.matmul(bank.buf[:, at:at + DIL_H], t8[:, g, folded(g, i)], c.const("ident", DIL_H)[:, 0:DIL_H],
                                  start=True, stop=True)
    m = PE.run(mm)
    coef = c.scratch.take()
    ncf = GROUPS * NT * DIL_H
    ready = c.copy(coef.buf[:, 0:ncf], bank.buf[:, 0:ncf], [m, *coef.free], "dve")
    c.banks.give(bank, ready)
    written = {}
    G.after(ready)
    V.after(ready)

    def weigh(queue, g, i):
        o3 = outs[g][:, i, :].rearrange("p (h d) -> p h d", h=DIL_H)
        at = (g * NT + i) * DIL_H
        cb = coef.buf[:, at:at + DIL_H].unsqueeze(2).to_broadcast([P, DIL_H, HD])
        return queue.run(queue.engine.tensor_tensor(o3, o3, cb, ALU.mult))

    def spread(g, i):
        if g == 0:
            m = weigh(G, 0, i)
        else:
            m1, m2 = weigh(G, 1, i), weigh(V, 2, i)
            V.after(m1, m2)
            m = V.run(nc.vector.tensor_tensor(outs[1][:, i, :], outs[1][:, i, :], outs[2][:, i, :], ALU.add))
        yield
        tb, m = c.transpose_blocks([outs[g][:, i, j * P:(j + 1) * P] for j in range(4)], P, [m])
        yield
        for j in range(4):
            dst, src = c.mixed[:, 4 + j, folded(g, i)], tb.buf[:, j * P:(j + 1) * P]
            if g == 0:
                V.after(m)
                written[j] = V.run(nc.vector.tensor_copy(dst, src))
            else:
                V.after(m, written[j])
                written[j] = V.run(nc.vector.tensor_tensor(dst, src, dst, ALU.add))
        c.banks.give(tb, written[3])
    pipelined((spread(g, i) for g in range(2) for i in range(NT)), 3)
    c.scratch.give(coef, *written.values())
    c.barrier()


def mla(c):
    nc, PE, A, V, G = c.nc, c.PE, c.ACT, c.DVE, c.POOL
    w_in, w_ukv = c.io["w_in"], c.io["w_ukv"]
    q, k = (c.arena[:, j * 8 * S:(j + 1) * 8 * S].rearrange("p (a t) -> p a t", a=8) for j in range(2))
    v = c.arena[:, 16 * S:20 * S].rearrange("p (a n) -> p a n", a=NT)
    ckvT = c.arena[:, 20 * S:22 * S].rearrange("p (a t) -> p a t", a=2)
    krope = c.arena[:, 22 * S:22 * S + NT * ROPE].rearrange("p (a n) -> p a n", a=NT)
    ready = []

    def finish_heads(n, heads, h0, i, gain, dst, m):
        n3 = n.buf[:, 0:heads * MLA_D].rearrange("p (h d) -> p h d", h=heads)
        G.after(m)
        m = G.run(nc.gpsimd.tensor_tensor(n3, n3, gain.unsqueeze(1).to_broadcast([P, heads, MLA_D]), ALU.mult))
        half = ROPE // 2
        m = c.rope(n3[:, :, NOPE:NOPE + half], n3[:, :, NOPE + half:], c.cos1[:, i, :], c.sin1[:, i, :],
                   heads, half, [m, c.rope_ready])
        yield
        yield
        tb, m = c.transpose_blocks([n.buf[:, j * MLA_D:(j + 1) * MLA_D] for j in range(heads)], MLA_D, [m])
        c.scratch.give(n, m)
        m = c.copy(dst[0:MLA_D, h0:h0 + heads, i * P:(i + 1) * P],
                   tb.buf[0:MLA_D, 0:heads * P].rearrange("p (a t) -> p a t", a=heads), [m])
        c.banks.give(tb, m)
        ready.append(m)

    heads_q = 2
    wq = heads_q * MLA_D

    def qtile(i, slot, part):
        bank, m = c.token_product(slot, wq, fold(c, 0, i), KD, c.h_ready)
        if i == NT - 1:
            c.weights.give(slot, m)
        yield
        n = c.scratch.take()
        V.after(*n.free)
        m = c.head_norm(bank.buf[:, 0:wq].rearrange("p (h d) -> p h d", h=heads_q), heads_q, MLA_D,
                        n.buf[:, 0:wq].rearrange("p (h d) -> p h d", h=heads_q), [m])
        c.banks.give(bank, m)
        yield from finish_heads(n, heads_q, part * heads_q, i, c.row["qmla"], q, m)

    def queries():
        for part in range(MLA_H // heads_q):
            slot = c.weight_chunk(w_in, C_MLAQ + part * wq, wq)
            for i in range(NT):
                yield qtile(i, slot, part)
    pipelined(queries(), 5, c.idle)

    slot = c.weight_chunk(w_in, C_CKV, KV_RANK)
    slot2 = c.weight_chunk(w_in, C_CKV + KV_RANK, ROPE)

    def ckv(i):
        bank, m = c.token_product(slot, KV_RANK, fold(c, 0, i), KD, c.h_ready)
        bank, m = c.token_product(slot2, ROPE, fold(c, 0, i), KD, c.h_ready, bank=bank, at=KV_RANK)
        slot.used = m
        yield
        n = c.scratch.take()
        V.after(*n.free)
        m0 = c.copy(krope[:, i, :], bank.buf[:, KV_RANK:KV_RANK + ROPE], [m], "act")
        m = c.head_norm(bank.buf[:, 0:KV_RANK].unsqueeze(1), 1, KV_RANK, n.buf[:, 0:KV_RANK].unsqueeze(1), [m, m0])
        c.banks.give(bank, m)
        yield
        tb, m = c.transpose_blocks([n.buf[:, j * P:(j + 1) * P] for j in range(2)], P, [m])
        c.scratch.give(n, m)
        for j in range(2):
            A.after(m)
            m = A.run(nc.scalar.activation(ckvT[:, j, i * P:(i + 1) * P], tb.buf[:, j * P:(j + 1) * P],
                                           ACT.Identity, scale=columns(c.col["norm_ckv"], j)))
        c.banks.give(tb, m)
        ckv_ready.append(m)
    ckv_ready = []
    pipelined((ckv(i) for i in range(NT)), 3, c.idle)
    c.weights.give(slot, slot.used)
    c.weights.give(slot2, slot.used)

    slot = c.weight_chunk(w_ukv, 0, MLA_H * (NOPE + MLA_V), kt=KV_RANK // P)

    def kvtile(i, half):
        heads = 4
        bank, m = c.token_product(slot, 512, lambda kk: ckvT[:, kk, i * P:(i + 1) * P], 2, ckv_ready, c0=512 * half)
        slot.used = m
        yield
        b3 = bank.buf[:, :].rearrange("p (h d) -> p h d", h=heads)
        n = c.scratch.take()
        n3 = n.buf[:, 0:heads * MLA_D].rearrange("p (h d) -> p h d", h=heads)
        vd = v[:, i, half * 256:(half + 1) * 256].rearrange("p (h d) -> p h d", h=heads)
        m = c.copy(vd, b3[:, :, NOPE:], [m], "act")
        ready.append(m)
        m = c.copy(n3[:, :, 0:NOPE], b3[:, :, 0:NOPE], [m, *n.free], "act")
        c.banks.give(bank, m)
        G.after(*n.free, *ckv_ready)
        m2 = G.run(nc.gpsimd.tensor_copy(n3[:, :, NOPE:], krope[:, i, :].unsqueeze(1).to_broadcast([P, heads, ROPE])))
        m = c.head_norm(n3, heads, MLA_D, n3, [m, m2])
        yield from finish_heads(n, heads, half * heads, i, c.row["kmla"], k, m)
    pipelined((kvtile(i, half) for half in range(2) for i in range(NT)), 5, c.idle)
    c.weights.give(slot, slot.used)
    causal_softmax(c, q, lambda h: k[0:MLA_D, h, :], v, MLA_D ** -0.5, ready, 0, pairs=False)


def causal_softmax(c, q, keys, v, scale, ready, out0, pairs):
    nc, PE, V = c.nc, c.PE, c.DVE

    def head(i, h, t):
        def query():
            if not pairs:
                return q[0:MLA_D, h, i * P:(i + 1) * P], []
            if h == 0:
                t["q"], t["q_in"] = c.pad_queries(q, slice(i * P, (i + 1) * P), ready)
            return t["q"].buf[:, h, :], t["q_in"]

        def out():
            if h == 0:
                t["out"] = c.head_pair_banks()
            if pairs and h == H - 1:
                c.padded.give(t["q"], c.PE.last())
            return c.pair_columns(t["out"], h)

        def done(m):
            if h < H - 1:
                return
            sums, o = t["sums"], c.scratch.take()
            V.after(m, *o.free)
            mr = V.run(nc.vector.reciprocal(sums.buf[:, 0:H], sums.buf[:, 0:H]))
            V.after(mr)
            for r in range(2):
                mo = V.run(nc.vector.tensor_tensor(
                    c.kept(o.buf[:], r), c.kept(t["out"][r].buf[:], r),
                    sums.buf[:, r:H:2].unsqueeze(2).to_broadcast([P, H // 2, HD]), ALU.mult))
                c.banks.give(t["out"][r], mo)
            c.small.give(sums, mo)
            c.small.give(t["negmax"], mo)
            yield
            tb, mt = c.transpose_blocks([o.buf[:, j * P:(j + 1) * P] for j in range(4)], P, [mo])
            c.scratch.give(o, mt)
            mt = c.copy(c.mixed[:, out0:out0 + 4, i * P:(i + 1) * P],
                        tb.buf[:].rearrange("p (a t) -> p a t", a=4), [mt])
            c.banks.give(tb, mt)
            c.mixed_ready.append(mt)
        if h == 0:
            t["sums"], t["negmax"] = c.small.take(), c.small.take()
            V.after(*t["negmax"].free)
            c.ACT.after(*t["sums"].free)
        return (yield from c.softmax_job(
            query, keys(h)[:, 0:(i + 1) * P], i + 1, [(c.const("ident"), c.const("causal"), i * P)], scale,
            lambda b: v[:, b, (h // 2) * P:(h // 2 + 1) * P], out,
            t["negmax"].buf[:, h:h + 1], t["sums"].buf[:, h:h + 1], ready, done))

    def heads_of():
        for i in range(NT):
            t = {}
            for h in range(H):
                yield head(i, h, t)
    pipelined(heads_of(), 6, c.idle)


def merge(c):
    nc, PE, A, V = c.nc, c.PE, c.ACT, c.DVE
    c.open_area()
    c.split_area(3)
    merged, h = c.pair("merged", KD), c.pair("h", KD)
    h_ready = [c.split(h[0][:, k, :], h[1][:, k, :], c.hT[:, k, :], c.h_ready) for k in range(KD)]
    ready = []

    def column(j):
        got = []
        gate = c.split_weights(c.io["w_in"], C_GATE + j * P)
        yield
        for n in range(2):
            gb, mg = c.split_product(gate, h, KD, h_ready)
            if n == 0:
                gate = c.split_weights(c.io["w_in"], C_GATE + D + j * P)
            w = c.weight_chunk(c.io[("w_o_mla", "w_o_dil")[n]], j * P, P, kt=4)
            pb, mp = c.feature_product(w, 0, c.mixed[:, 4 * n:4 * n + 4, :], 4, c.mixed_ready)
            c.weights.give(w, mp)
            got.append((gb, mg, pb, mp))
            yield
        gs = []
        for n, (gb, mg, pb, mp) in enumerate(got):
            g = c.scratch.take()
            A.after(mg, *g.free)
            m = A.run(nc.scalar.activation(g.buf[:], gb.buf[:], ACT.Sigmoid, bias=columns(c.col["b_gate"], n * KD + j)))
            c.banks.give(gb, m)
            V.after(m, mp)
            m = V.run(nc.vector.tensor_tensor(g.buf[:], g.buf[:], pb.buf[:], ALU.mult))
            c.banks.give(pb, m)
            gs.append(g)
        V.after(m)
        m = V.run(nc.vector.tensor_tensor(gs[0].buf[:], gs[0].buf[:], gs[1].buf[:], ALU.add))
        m = c.split(merged[0][:, j, :], merged[1][:, j, :], gs[0].buf[:], [m])
        for g in gs:
            c.scratch.give(g, m)
        ready.append(m)
    pipelined((column(j) for j in range(KD)), 3, c.idle, every=2)
    pipelined(split_project_out(c, c.io["w_out"], merged, KD, ready), 3, c.idle)
    c.close_area()


def pause(rounds):
    for _ in range(rounds - 1):
        yield


def split_project_out(c, w, act, kt, ready, gate=None, k0=0):
    def column(j):
        pieces = [(a, min(KD, kt - a)) for a in range(0, kt, KD)]
        ws = [c.split_weights(w, j * P, kt=n, k0=k0 + a) for a, n in pieces]
        yield
        bank = None
        for s, (a, n) in zip(ws, pieces):
            bank, m = c.split_product(s, [t[:, a:a + n, :] for t in act], n, ready[a:a + n], bank=bank,
                                      first=a == 0, last=a + n == kt)
        yield
        c.add_residual(bank, m, j, None if gate is None else gate(j))
    return [column(j) for j in range(KD)]


def project_mixed(c, w, gate):
    c.open_area()
    c.split_area(3)
    mixed = c.pair("mixed", KD)
    ready = [c.split(mixed[0][:, k, :], mixed[1][:, k, :], c.mixed[:, k, :], c.mixed_ready) for k in range(KD)]
    pipelined(split_project_out(c, w, mixed, KD, ready, gate), 3, c.idle)
    c.close_area()


def moe(c, router):
    nc, io, PE, A, V, G = c.nc, c.io, c.PE, c.ACT, c.DVE, c.POOL
    c.open_area()
    L = c.sb("moe", [P, MOE_WIDTH])
    at = [0]

    def take(n, dt=None):
        a = L[:, at[0]:at[0] + n]
        at[0] += n
        return a if dt is None else a.bitcast(dt)
    NL = N_GRP + NE
    logits = take(NT * NL).rearrange("p (t n) -> p t n", t=NT)
    g8 = take(NT * 8).rearrange("p (t n) -> p t n", t=NT)
    top = take(NT * 8).rearrange("p (t n) -> p t n", t=NT)
    idx = take(NT * 8, U32).rearrange("p (t n) -> p t n", t=NT)
    pick = take(2 * NT).rearrange("p (n t) -> p n t", n=2)
    onehot = take(2 * NT * NE).rearrange("p (n t e) -> p n t e", n=2, t=NT)
    both = take(NT * NE).rearrange("p (t e) -> p t e", t=NT)
    place = take(NT * NE).rearrange("p (t e) -> p t e", t=NT)
    tmp = take(NT * NE).rearrange("p (t e) -> p t e", t=NT)
    stat = take(8 * NT).rearrange("p (n t) -> p n t", n=8)
    slotf = take(2 * NT)
    sloti = take(2 * NT, I32)
    blocks = take(8 + NBLK)
    block_e = take(NBLK, I32)
    tokens = take(NBLK, I32)
    slot_row = take(P)
    tilei, withini = take(2 * NT, I32), take(2 * NT, I32)
    tilef, withinf = take(2 * NT), take(2 * NT)
    in_slot = take(2 * NT * P).rearrange("p (q n) -> p q n", q=2 * NT)
    in_tile = take(2 * NT * NBLK).rearrange("p (q n) -> p q n", q=2 * NT)
    xb = [take(D) for _ in range(3)]
    xbT = [take(D) for _ in range(2)]
    yb = [take(D) for _ in range(3)]

    a = c.at["slot"][0]
    c.SP.after(*c.engine_marks())
    slot_in = c.load_once(c.SP, slot_row, c.io["consts"][:, a:a + P], "slot_in")
    stored = []
    h2_sem = c.sem("h2_out")
    n_stored = 0
    for i in range(NT):
        for half in range(2):
            tb, m = c.transpose_blocks([c.hT[:, 4 * half + j, i * P:(i + 1) * P] for j in range(4)], P, c.h_ready)
            s = c.scratch.take()
            m = c.copy(s.buf[:], tb.buf[:], [m, *s.free])
            c.banks.give(tb, m)
            G.after(m)
            nc.gpsimd.dma_start(c.h2_dram[i * P:(i + 1) * P, half * 512:(half + 1) * 512], s.buf[:]).then_inc(h2_sem, 16)
            n_stored += 16
            c.scratch.give(s, (h2_sem, n_stored))
    assert at[0] <= MOE_WIDTH
    marks = c.engine_marks()
    extra = c.weights.extend([c.sb(f"more_weights{i}", [P, 2048]) for i in range(4)],
                             [c.sem(f"moe_weights{i}_in") for i in range(4)], marks)
    h2_stored = (h2_sem, n_stored)

    bank, m = c.feature_product(router, 0, c.hT, KD, c.h_ready)
    c.weights.give(router, m)
    c.h_free = [m]
    s = c.scratch.take()
    m = c.copy(s.buf[0:NL, :], bank.buf[0:NL, :], [m, *s.free])
    c.banks.give(bank, m)
    bank = c.banks.take()
    PE.after(m, *bank.free)
    for i in range(NT):
        mm = nc.tensor.transpose(bank.buf[:, i * NL:(i + 1) * NL], s.buf[0:NL, i * P:(i + 1) * P],
                                 c.const("ident", NL)[:, 0:NL])
    m = PE.run(mm)
    c.scratch.give(s, m)
    first = ROWS["b_rg"][0]
    bias = c.rows[:, first:first + NL].unsqueeze(1).to_broadcast([P, NT, NL])

    def v(ins):
        return V.run(ins)
    V.after(m)
    m = v(nc.vector.tensor_tensor(logits, bank.buf[:, 0:NT * NL].rearrange("p (t n) -> p t n", t=NT), bias, ALU.add))
    c.banks.give(bank, m)
    m2 = v(nc.vector.memset(g8, NEG))
    V.after(m, m2)
    m = v(nc.vector.tensor_copy(g8[:, :, 0:N_GRP], logits[:, :, 0:N_GRP]))
    for i in range(NT):
        V.after(m)
        m = v(nc.vector.max(top[:, i, :], g8[:, i, :]))
        V.after(m)
        m = v(nc.vector.max_index(idx[:, i, :], top[:, i, :], g8[:, i, :]))
    V.after(m)
    m = v(nc.vector.tensor_copy(stat[:, 0, :], idx[:, :, 0]))
    m = v(nc.vector.tensor_tensor(g8[:, :, 0:N_GRP], g8[:, :, 0:N_GRP],
                                  top[:, :, 0:1].to_broadcast([P, NT, N_GRP]), ALU.subtract))
    A.after(m)
    m = A.run(nc.scalar.activation(g8[:, :, 0:N_GRP], g8[:, :, 0:N_GRP], ACT.Exp))
    V.after(m)
    m = v(nc.vector.tensor_reduce(stat[:, 1, :], g8[:, :, 0:N_GRP], AX.X, ALU.add))
    V.after(m)
    m = v(nc.vector.reciprocal(stat[:, 1, :], stat[:, 1, :]))
    chosen = g8[:, :, N_GRP:2 * N_GRP]
    m = v(nc.vector.tensor_tensor(chosen, c.const("group")[:, 0:N_GRP].unsqueeze(1).to_broadcast([P, NT, N_GRP]),
                                  stat[:, 0, :].unsqueeze(2).to_broadcast([P, NT, N_GRP]), ALU.is_equal))
    V.after(m)
    m = v(nc.vector.tensor_scalar(chosen, chosen, -1.0, -NEG, ALU.add, ALU.mult))
    V.after(m)
    for i in range(NT):
        m = v(nc.vector.tensor_tensor(tmp[:, i, :].rearrange("p (g e) -> p g e", g=N_GRP),
                                      logits[:, i, N_GRP:].rearrange("p (g e) -> p g e", g=N_GRP),
                                      chosen[:, i, :].unsqueeze(2).to_broadcast([P, N_GRP, PER_GRP]), ALU.add))
    for i in range(NT):
        V.after(m)
        m = v(nc.vector.max(top[:, i, :], tmp[:, i, :]))
        V.after(m)
        m = v(nc.vector.max_index(idx[:, i, :], top[:, i, :], tmp[:, i, :]))
    V.after(m)
    m = v(nc.vector.tensor_tensor(stat[:, 2, :], top[:, :, 1], top[:, :, 0], ALU.subtract))
    A.after(m)
    m = A.run(nc.scalar.activation(stat[:, 2, :], stat[:, 2, :], ACT.Exp))
    for n in range(2):
        m3 = v(nc.vector.tensor_copy(pick[:, n, :], idx[:, :, n]))
    V.after(m, m3)
    m = v(nc.vector.tensor_scalar(stat[:, 3, :], stat[:, 2, :], 1.0, None, ALU.add))
    V.after(m)
    m = v(nc.vector.reciprocal(stat[:, 3, :], stat[:, 3, :]))
    V.after(m)
    m = v(nc.vector.tensor_tensor(stat[:, 4, :], stat[:, 1, :], stat[:, 3, :], ALU.mult))
    V.after(m)
    share = v(nc.vector.tensor_tensor(stat[:, 5, :], stat[:, 4, :], stat[:, 2, :], ALU.mult))
    V.after(share)
    for n in range(2):
        m = v(nc.vector.tensor_tensor(onehot[:, n, :, :], c.const("expert").unsqueeze(1).to_broadcast([P, NT, NE]),
                                      pick[:, n, :].unsqueeze(2).to_broadcast([P, NT, NE]), ALU.is_equal))
    V.after(m)
    m = v(nc.vector.tensor_tensor(both, onehot[:, 0, :, :], onehot[:, 1, :, :], ALU.add))
    rank, count = c.banks.take(), c.banks.take()
    PE.after(m, *rank.free, *count.free)
    for i in range(NT):
        for j in range(i + 1):
            mm = nc.tensor.matmul(rank.buf[:, i * NE:(i + 1) * NE], c.const("before" if j == i else "ones"),
                                  both[:, j, :], start=j == 0, stop=j == i)
        nc.tensor.matmul(count.buf[0:NE, 0:1], both[:, i, :], c.const("ones")[:, 0:1], start=i == 0, stop=i == NT - 1)
    m = PE.run(nc.tensor.matmul(rank.buf[:, NT * NE:NT * NE + 1], c.const("ones"), c.const("ones")[:, 0:1],
                                start=True, stop=True))
    cnt, nblk, end, per = blocks[0:NE, 0:1], blocks[0:NE, 1:2], blocks[0:NE, 2:3], blocks[0:NE, 4:8]
    V.after(m)
    m = v(nc.vector.tensor_copy(cnt, count.buf[0:NE, 0:1]))
    V.after(m)
    m = v(nc.vector.tensor_scalar(per, c.const("thresholds", NE), cnt, None, ALU.is_lt))
    V.after(m)
    m = v(nc.vector.tensor_reduce(nblk, per, AX.X, ALU.add))
    PE.after(m)
    before = c.const("before", NE)[:, 0:NE]
    nc.tensor.matmul(count.buf[0:NE, 1:2], before, nblk, start=True, stop=False)
    nc.tensor.matmul(count.buf[0:NE, 1:2], c.const("ident", NE)[:, 0:NE], nblk, start=False, stop=True)
    m = PE.run(nc.tensor.matmul(count.buf[:, 2:2 + NE], nblk.to_broadcast([NE, P]), before, start=True, stop=True))
    V.after(m)
    m = v(nc.vector.tensor_copy(end, count.buf[0:NE, 1:2]))
    V.after(m)
    m = v(nc.vector.tensor_scalar(blocks[0:NE, 8:8 + NBLK], c.const("block", NE), end, None, ALU.is_ge))
    PE.after(m)
    m2 = PE.run(nc.tensor.matmul(rank.buf[0:1, 256:256 + NBLK], c.const("ones", NE)[:, 0:1],
                                 blocks[0:NE, 8:8 + NBLK], start=True, stop=True))
    V.after(m2)
    expert_ready = v(nc.vector.tensor_scalar(block_e[0:1, :], rank.buf[0:1, 256:256 + NBLK], float(NE - 1), None, ALU.min))
    V.after(m)
    m = v(nc.vector.tensor_scalar(tmp[:, 0, :], count.buf[:, 2:2 + NE], float(P), None, ALU.mult))
    c.banks.give(count, m)
    V.after(m)
    m = v(nc.vector.tensor_tensor(place, rank.buf[:, 0:NT * NE].rearrange("p (t e) -> p t e", t=NT),
                                  tmp[:, 0, :].unsqueeze(1).to_broadcast([P, NT, NE]), ALU.add))
    c.banks.give(rank, m)
    for n in range(2):
        V.after(m)
        m = v(nc.vector.tensor_tensor(tmp, onehot[:, n, :, :], place, ALU.mult))
        V.after(m)
        m = v(nc.vector.tensor_reduce(slotf[:, n * NT:(n + 1) * NT], tmp, AX.X, ALU.add))
    V.after(m)
    m = v(nc.vector.tensor_copy(sloti, slotf))
    V.after(m)
    m = v(nc.vector.tensor_scalar(tilei, sloti, SLOT_BITS, None, ALU.logical_shift_right))
    m2 = v(nc.vector.tensor_scalar(withini, sloti, P - 1, None, ALU.bitwise_and))
    V.after(m, m2)
    v(nc.vector.tensor_copy(tilef, tilei))
    m = v(nc.vector.tensor_copy(withinf, withini))
    V.after(m, slot_in)
    bank = c.banks.take()
    PE.after(*bank.free)
    npairs = 2 * NT
    for q in range(npairs):
        v(nc.vector.tensor_scalar(in_slot[:, q, :], slot_row, withinf[:, q:q + 1], None, ALU.is_equal))
        m = v(nc.vector.tensor_scalar(in_tile[:, q, :], c.const("block"), tilef[:, q:q + 1],
                                      c.const("token")[:, q % NT:q % NT + 1], ALU.is_equal, ALU.mult))
        PE.after(m)
        mm = nc.tensor.matmul(bank.buf[:, 0:NBLK], in_slot[:, q, :], in_tile[:, q, :],
                              start=q == 0, stop=q == npairs - 1)
    m = PE.run(mm)
    V.after(m)
    tokens_ready = v(nc.vector.tensor_copy(tokens, bank.buf[:, 0:NBLK]))
    c.banks.give(bank, tokens_ready)

    gathers = [c.sem(f"gather{j}") for j in range(3)]
    outs = [c.sem(f"tile_out{j}") for j in range(3)]
    x_free = [[] for _ in range(3)]
    xT_free = [[] for _ in range(2)]
    c.SP.after(expert_ready)
    G.after(tokens_ready, h2_stored)

    def expert_weights(name, e, kt):
        view = lambda buf: buf.rearrange("p (k n) -> p k n", k=kt)
        src = io[name][bass.ds(e, 1), :, :].rearrange("e (k p) n -> p (e k) n", p=P)
        s = c.weights.load(view, src)
        s.w = view(s.buf)
        return s

    def tile(b):
        j = b % 3
        G.after(*x_free[j])
        nc.gpsimd.indirect_dma_start(out=xb[j], out_offset=None, in_=c.h2_dram,
                                     in_offset=bass.IndirectOffsetOnAxis(ap=tokens[:, b:b + 1], axis=0)
                                     ).then_inc(gathers[j], 16)
        yield
        e = nc.sync.value_load(block_e[0:1, b:b + 1], min_val=0, max_val=NE - 1)
        w = [expert_weights("w_gate", e, KD), expert_weights("w_up", e, KD)]
        xt = xbT[b % 2]
        marks = []
        for half in range(2):
            tb, m = c.transpose_blocks([xb[j][:, (4 * half + q) * P:(4 * half + q + 1) * P] for q in range(4)], P,
                                       [(gathers[j], 16 * (b // 3 + 1))])
            x_free[j] = [m]
            m = c.copy(xt[:, half * 512:(half + 1) * 512], tb.buf[:], [m, *xT_free[b % 2]])
            marks.append(m)
            c.banks.give(tb, m)
        yield
        toks = lambda k: xt[:, k * P:(k + 1) * P]
        gb, m1 = c.token_product(w[0], FF, toks, KD, marks)
        ub, m2 = c.token_product(w[1], FF, toks, KD, marks)
        xT_free[b % 2] = [m2]
        c.weights.give(w[0], m1)
        c.weights.give(w[1], m2)
        w.append(expert_weights("w_down", e, FF // P))
        he = c.scratch.take()
        A.after(m1, *he.free)
        m = A.run(nc.scalar.activation(he.buf[:, 0:FF], gb.buf[:, 0:FF], ACT.Silu))
        c.banks.give(gb, m)
        V.after(m, m2)
        m = V.run(nc.vector.tensor_tensor(he.buf[:, 0:FF], he.buf[:, 0:FF], ub.buf[:, 0:FF], ALU.mult))
        c.banks.give(ub, m)
        yield
        tb, m = c.transpose_blocks([he.buf[:, q * P:(q + 1) * P] for q in range(2)], P, [m])
        m = c.copy(he.buf[:, FF:2 * FF], tb.buf[:, 0:FF], [m])
        c.banks.give(tb, m)
        yield
        PE.after(m, w[2].ready)
        done = []
        for half in range(2):
            bk = c.banks.take()
            PE.after(*bk.free)
            for q in range(2):
                mm = nc.tensor.matmul(bk.buf[:], he.buf[:, FF + q * P:FF + (q + 1) * P],
                                      w[2].w[:, q, half * 512:(half + 1) * 512], start=q == 0, stop=q == 1)
            m = PE.run(mm)
            out_free = [(outs[j], 16 * (b // 3))] if b >= 3 else []
            mc = c.copy(yb[j][:, half * 512:(half + 1) * 512], bk.buf[:], [m, *out_free])
            c.banks.give(bk, mc)
            done.append(mc)
        c.scratch.give(he, m)
        c.weights.give(w[2], m)
        G.after(*done)
        nc.gpsimd.dma_start(c.y_dram[b * P:(b + 1) * P, :], yb[j]).then_inc(outs[j], 16)
    pipelined((tile(b) for b in range(NBLK)), 5)

    c.weights.drop(extra)
    for j in range(3):
        G.after((outs[j], 16 * len(range(j, NBLK, 3))))
    c.barrier()
    tail = [c.sem(f"combine{i}") for i in range(NT)]
    both_y = xb + yb
    tail_free = [[] for _ in range(3)]
    for i in range(NT):
        pair = (both_y[2 * (i % 3)], both_y[2 * (i % 3) + 1])
        G.after(*tail_free[i % 3])
        for n in range(2):
            nc.gpsimd.indirect_dma_start(out=pair[n], out_offset=None, in_=c.y_dram,
                                         in_offset=bass.IndirectOffsetOnAxis(ap=sloti[:, n * NT + i:n * NT + i + 1], axis=0)
                                         ).then_inc(tail[i], 16)
        V.after((tail[i], 32))
        m = V.run(nc.vector.tensor_scalar(pair[1], pair[1], stat[:, 5, i:i + 1], None, ALU.mult))
        V.after(m)
        m = V.run(nc.vector.scalar_tensor_tensor(out=pair[0], in0=pair[0], scalar=stat[:, 4, i:i + 1], in1=pair[1],
                                                 op0=ALU.mult, op1=ALU.add))
        for half in range(2):
            tb, mt = c.transpose_blocks([pair[0][:, (4 * half + q) * P:(4 * half + q + 1) * P] for q in range(4)],
                                        P, [m])
            x = c.xT[:, 4 * half:4 * half + 4, i * P:(i + 1) * P]
            V.after(mt, *[mk for k in range(4) for mk in c.x_ready[4 * half + k]])
            mv = V.run(nc.vector.tensor_tensor(x, x, tb.buf[:].rearrange("p (a t) -> p a t", a=4), ALU.add))
            c.banks.give(tb, mv)
            tail_free[i % 3] = [mv]
    c.x_ready = [[V.last()] for _ in range(KD)]
    c.close_area()


def head_groups(c):
    nc, PE, A, V, G = c.nc, c.PE, c.ACT, c.DVE, c.POOL
    w_in = c.io["attn_w_in_2"]
    c.open_scores_area()
    qa, ka, va, qb, kb, vb = (c.arena[:, j * 4 * S:(j + 1) * 4 * S].rearrange("p (a t) -> p a t", a=4)
                              for j in range(6))
    c.mixed_ready = []
    ready = []
    heads, half = 4, ROPE2 // 2
    def tile(i, slot, part, dst, hf):
        bank, m = c.token_product(slot, 256, fold(c, 0, i), KD, c.h_ready)
        if i == NT - 1:
            c.weights.give(slot, m)
        yield
        if part in (2, 5):
            m = c.copy(dst[:, i, hf * 256:(hf + 1) * 256], bank.buf[:, 0:256], [m])
            c.banks.give(bank, m)
            ready.append(m)
            return
        n = c.scratch.take()
        m = c.copy(n.buf[:, 0:256], bank.buf[:, 0:256], [m, *n.free])
        c.banks.give(bank, m)
        n3 = n.buf[:, 0:256].rearrange("p (h d) -> p h d", h=heads)
        m = c.rope(n3[:, :, 0:half], n3[:, :, half:2 * half], c.cos2[:, i, :], c.sin2[:, i, :], heads, half,
                   [m, c.rope_ready])
        yield
        yield
        tb, m = c.transpose_blocks([n.buf[:, j * P:(j + 1) * P] for j in range(2)], P, [m])
        c.scratch.give(n, m)
        m = c.copy(dst[:, 2 * hf:2 * hf + 2, i * P:(i + 1) * P],
                   tb.buf[:, 0:256].rearrange("p (a t) -> p a t", a=2), [m])
        c.banks.give(tb, m)
        ready.append(m)

    def tiles():
        for part, dst in ((0, qa), (1, ka), (2, va), (5, vb)):
            for hf in range(2):
                slot = c.weight_chunk(w_in, part * 512 + hf * 256, 256)
                for i in range(NT):
                    yield tile(i, slot, part, dst, hf)
    pipelined(tiles(), 5, c.idle)
    for part, dst in ((3, qb), (4, kb)):
        for hf in range(2):
            slot = c.weight_chunk(w_in, part * 512 + hf * 256, 256)
            for m_ in range(2):
                bank, m = c.feature_product(slot, m_, c.hT, KD, c.h_ready)
                A.after(m)
                mc = A.run(nc.scalar.activation(dst[:, 2 * hf + m_, :], bank.buf[:], ACT.Copy,
                                                scale=1.0 if part == 3 else HD ** -0.5))
                c.banks.give(bank, mc)
                ready.append(mc)
            c.weights.give(slot, m)
    c.h_free = [PE.last()]
    causal_softmax(c, qa, lambda h: ka[:, h // 2, :], va, HD ** -0.5, ready, 0, pairs=True)
    c.barrier()

    o = qa
    padded = c.arena[:, 4 * S:12 * S].rearrange("p (h t) -> p h t", h=H)
    for r, rows in enumerate((slice(0, HD), slice(HD, P))):
        other = (G, V)[r]
        zeroed = other.run(other.engine.memset(padded[rows, 1 - r:H:2, :], 0.0))
        PE.after(zeroed, c.copy(padded[rows, r:H:2, :], qb[rows, :, :], []))

    def head(h):
        t = h // 2
        part, sp = [], []
        for j in range(NT):
            n = S - j * P
            zb = c.banks.take()
            PE.after(*zb.free)
            m = PE.run(nc.tensor.matmul(zb.buf[:, 0:n], kb[:, t, j * P:(j + 1) * P], padded[:, h, j * P:S],
                                        start=True, stop=True))
            s = c.scratch.take()
            V.after(m, *s.free)
            m = V.run(nc.vector.tensor_scalar(s.buf[:, 0:n], zb.buf[:, 0:n], 0.0, None, ALU.max))
            V.after(m)
            m = V.run(nc.vector.scalar_tensor_tensor(out=s.buf[:, 0:n], in0=s.buf[:, 0:n], scalar=-2.0,
                                                     in1=zb.buf[:, 0:n], op0=ALU.mult, op1=ALU.add))
            A.after(m)
            m = A.run(nc.scalar.activation(s.buf[:, 0:n], s.buf[:, 0:n], ACT.Exp))
            part.append((s, zb, n, m))
        lns = []
        for s, zb, n, m in part:
            A.after(m)
            lns.append(A.run(nc.scalar.activation(s.buf[:, 0:n], s.buf[:, 0:n], ACT.Ln, bias=1.0)))
        for (s, zb, n, _), m in zip(part, lns):
            V.after(m)
            m = V.run(nc.vector.scalar_tensor_tensor(out=s.buf[:, 0:n], in0=zb.buf[:, 0:n], scalar=0.0,
                                                     in1=s.buf[:, 0:n], op0=ALU.max, op1=ALU.add))
            c.banks.give(zb, m)
            V.after(m)
            m = V.run(nc.vector.tensor_tensor(s.buf[:, 0:P], s.buf[:, 0:P], c.const("sb_keep"), ALU.mult))
            sp.append((s, m))
        yield
        ws = []
        for i in range(NT):
            n = S - i * P
            cb = c.banks.take()
            PE.after(*cb.free)
            nc.tensor.matmul(cb.buf[:, 0:n], kb[:, t, i * P:(i + 1) * P], padded[:, h, i * P:S], start=True, stop=False)
            nc.tensor.matmul(cb.buf[:, 0:P], c.const("ident"), c.const("sb_mask"), start=False, stop=False)
            for j in range(i, NT):
                PE.after(sp[j][1])
                mm = nc.tensor.matmul(cb.buf[:, (j - i) * P:n], c.const("neg_from" if j == i else "neg_ones"),
                                      sp[j][0].buf[:, 0:S - j * P], start=False, stop=j == NT - 1)
            m = PE.run(mm)
            w = sp[i][0]
            A.after(m)
            m = A.run(nc.scalar.activation(w.buf[:, 0:n], cb.buf[:, 0:n], ACT.Exp))
            c.banks.give(cb, m)
            ws.append((w, m))
        yield
        ob = c.banks.take()
        PE.after(*ob.free, *[m for _, m in ws])
        for q in range(NT):
            for i in range(q + 1):
                mm = nc.tensor.matmul(ob.buf[:, q * P:(q + 1) * P], ws[i][0].buf[:, (q - i) * P:(q - i + 1) * P],
                                      vb[:, i, t * P:(t + 1) * P], start=i == 0, stop=i == q)
        m = PE.run(mm)
        for w, _ in ws:
            c.scratch.give(w, m)
        m = c.copy(o[:, :, h * HD:(h + 1) * HD], c.kept(ob.buf[:], h % 2), [m], "dve")
        c.banks.give(ob, m)
        done.append(m)
    done = []
    pipelined((head(h) for h in range(H)), 3, c.idle)
    for i in range(NT):
        tb, m = c.transpose_blocks([o[:, i, j * P:(j + 1) * P] for j in range(4)], P, done)
        m = c.copy(c.mixed[:, 4:8, i * P:(i + 1) * P], tb.buf[:].rearrange("p (a t) -> p a t", a=4), [m])
        c.banks.give(tb, m)
        c.mixed_ready.append(m)
    c.close_scores_area()


def swiglu(c, layer, gain, shift):
    nc, A, V = c.nc, c.ACT, c.DVE
    w_in, w_out = c.io["ffn_w_in_2"][layer], c.io["ffn_w_out_2"][layer]
    c.open_area()
    c.split_area(4)
    h = c.pair("h", KD)
    per = -(-KH // 2) + 1
    hid = c.pair("hidden", per)
    c.norm_residual(gain, shift, split=h)
    jobs = []
    for k0 in range(0, KH, per):
        kt = min(per, KH - k0)
        ready = []

        def unit(j, k0=k0, ready=ready):
            ws = [c.split_weights(w_in, n * HID + j * P) for n in range(2)]
            yield
            (gb, m1), (ub, m2) = [c.split_product(s, h, KD, c.h_ready) for s in ws]
            yield
            s = c.scratch.take()
            A.after(m1, *s.free)
            m = A.run(nc.scalar.activation(s.buf[:], gb.buf[:], ACT.Silu))
            c.banks.give(gb, m)
            V.after(m, m2)
            m = V.run(nc.vector.tensor_tensor(s.buf[:], s.buf[:], ub.buf[:], ALU.mult))
            c.banks.give(ub, m)
            m = c.split(hid[0][:, j - k0, :], hid[1][:, j - k0, :], s.buf[:], [m, m2])
            c.scratch.give(s, m)
            ready.append(m)
        jobs += [unit(j) for j in range(k0, k0 + kt)] + [pause(1)]
        jobs += split_project_out(c, w_out, hid, kt, ready, gate=lambda j: c.mod[:, layer, 5, j:j + 1], k0=k0)
    pipelined(jobs, 3, c.idle)
    c.close_area()


def delta_net(c, gain, shift):
    nc, PE, A, V, G = c.nc, c.PE, c.ACT, c.DVE, c.POOL
    w_in = c.io["gdn_w_in_2"]
    HG = 4
    c.open_area()
    slot = c.weight_chunk(w_in, 4 * H * GD, 2 * H)
    h = c.pair("h", KD)
    c.norm_residual(gain, shift, split=h)
    qT, kT, ktok, vtok = (c.sb(name, [P, HG, S]) for name in ("qT", "kT", "ktok", "vtok"))
    g4 = lambda a: a.rearrange("p (h t) -> p h t", h=HG)

    ab = [c.sb(f"ab{n}", [P, KD, 2 * H], F32R) for n in range(2)]
    col = c.sb("gate_cols", [P, 8, NT, H])
    x, t, g, beta, gcum, kdec1, bexp, kdec0 = (col[:, j, :, :] for j in range(8))
    cols_ready = []

    def gates():
        ab_ready = c.split(ab[0][:], ab[1][:], slot.w, [slot.ready])
        c.weights.give(slot, ab_ready)
        yield
        bank = c.banks.take()
        PE.after(ab_ready, *c.h_ready, *bank.free)
        for i in range(NT):
            for k in range(KD):
                for term, (x_, w_) in enumerate(((0, 0), (0, 1), (1, 0))):
                    mm = nc.tensor.matmul(bank.buf[:, i * 2 * H:(i + 1) * 2 * H], h[x_][:, k, i * P:(i + 1) * P],
                                          ab[w_][:, k, :], start=k == 0 and term == 0, stop=k == KD - 1 and term == 2)
        m = PE.run(mm)
        yield
        b3 = bank.buf[:, 0:NT * 2 * H].rearrange("p (t n) -> p t n", t=NT)
        over = lambda r: r.unsqueeze(1).to_broadcast([P, NT, H])
        V.after(m)
        m = V.run(nc.vector.tensor_tensor(x, b3[:, :, 0:H], over(c.row["dt_bias"]), ALU.add))
        A.after(m)
        m1 = A.run(nc.scalar.activation(beta, b3[:, :, H:], ACT.Sigmoid))
        c.banks.give(bank, m1)
        m = A.run(nc.scalar.activation(t, x, ACT.Abs))
        A.after(m)
        m = A.run(nc.scalar.activation(t, t, ACT.Exp, scale=-1.0))
        A.after(m)
        m = A.run(nc.scalar.activation(t, t, ACT.Ln, bias=1.0))
        m = A.run(nc.scalar.activation(c.row["a_log"], c.row["a_log"], ACT.Exp))
        yield
        V.after(m)
        m = V.run(nc.vector.scalar_tensor_tensor(out=g, in0=x, scalar=0.0, in1=t, op0=ALU.max, op1=ALU.add))
        V.after(m)
        m = V.run(nc.vector.scalar_tensor_tensor(out=g, in0=g, scalar=-1.0, in1=over(c.row["a_log"]),
                                                 op0=ALU.mult, op1=ALU.mult))
        yield
        bank = c.banks.take()
        PE.after(m, *bank.free)
        flat = lambda a: a.rearrange("p t h -> p (t h)")
        nc.tensor.matmul(bank.buf[:, 0:NT * H], c.const("chunk_upto"), flat(g), start=True, stop=True)
        m = PE.run(nc.tensor.matmul(bank.buf[:, NT * H:2 * NT * H], c.const("chunk_all"), flat(g),
                                    start=True, stop=True))
        yield
        V.after(m)
        m = V.run(nc.vector.tensor_copy(flat(gcum), bank.buf[:, 0:NT * H]))
        V.after(m)
        m = V.run(nc.vector.tensor_tensor(flat(kdec0), bank.buf[:, NT * H:2 * NT * H], flat(gcum), ALU.subtract))
        c.banks.give(bank, m)
        A.after(m)
        mk = A.run(nc.scalar.activation(kdec0, kdec0, ACT.Exp))
        m = A.run(nc.scalar.activation(bexp, gcum, ACT.Exp))
        yield
        V.after(mk)
        in_second = c.const("chunk_all")[:, P - 1:P]
        mk = V.run(nc.vector.tensor_scalar(flat(kdec1), flat(kdec0), in_second, None, ALU.mult))
        V.after(mk)
        mk = V.run(nc.vector.tensor_tensor(flat(kdec0), flat(kdec0), flat(kdec1), ALU.subtract))
        V.after(mk, m, m1)
        cols_ready.append(V.run(nc.vector.tensor_tensor(bexp, bexp, beta, ALU.mult)))

    state = c.sb("state", [P, HG, GD])
    c.mixed_ready = []
    for hg in range(H // HG):
        c.open_area()
        c.split_area(4)
        sums = c.banks.take()
        PE.after(*sums.free)
        staged, tail = [], []

        def channel(part, hh, sums=sums, staged=staged, tail=tail, hg=hg):
            ct = part * H + hg * HG + hh
            w = c.split_weights(w_in, ct * P)
            yield
            bank, m = c.split_product(w, h, KD, c.h_ready)
            yield
            acc = c.scratch.take()
            V.after(m, *acc.free)
            tap = lambda d: c.conv_w[:, CONV - 1 - d, ct:ct + 1]
            m = V.run(nc.vector.tensor_scalar(acc.buf[:], bank.buf[:], tap(0), None, ALU.mult))
            for d in range(1, CONV):
                V.after(m)
                m = V.run(nc.vector.scalar_tensor_tensor(
                    out=acc.buf[:, d:S], in0=bank.buf[:, 0:S - d], scalar=tap(d), in1=acc.buf[:, d:S],
                    op0=ALU.mult, op1=ALU.add))
            c.banks.give(bank, m)
            dst = acc.buf[:] if part == 2 else (qT, kT)[part][:, hh, :]
            A.after(m)
            m = A.run(nc.scalar.activation(dst, acc.buf[:], ACT.Silu))
            if part < 2:
                A.after(m)
                m = A.run(nc.scalar.activation(acc.buf[:], dst, ACT.Square))
            yield
            yield
            if part < 2:
                row = part * HG + hh
                PE.after(m)
                m = PE.run(nc.tensor.matmul(sums.buf[0:8, :], c.const("strip")[:, 15 - row:23 - row],
                                            acc.buf[:], start=row == 0, stop=row == 7))
                c.scratch.give(acc, m)
                staged.append(m)
            else:
                tb, m = c.transpose_blocks([acc.buf[:, i * P:(i + 1) * P] for i in range(NT)], P, [m])
                c.scratch.give(acc, m)
                m = c.copy(vtok[:, :, hh * P:(hh + 1) * P], tb.buf[:].rearrange("p (i d) -> p i d", i=NT), [m])
                c.banks.give(tb, m)
                tail.append(m)

        jobs = [channel(part, hh) for part in range(3) for hh in range(HG)]
        if hg == 0:
            jobs.insert(2, gates())
        pipelined(jobs, 5)
        c.close_area()
        c.open_area()
        c.scratch.slots = [Slot(c.sb(f"more_scratch{j}", [P, 512])) for j in range(16)] + c.scratch.slots
        rows = c.scratch.take()
        V.after(*rows.free)
        A.after(*staged, V.run(nc.vector.memset(rows.buf[:], 0.0)))
        m = A.run(nc.scalar.activation(rows.buf[0:8, :], sums.buf[0:8, :], ACT.Sqrt, bias=c.eps[0:8, 0:1]))
        c.banks.give(sums, m)
        V.after(m)
        mr = V.run(nc.vector.reciprocal(rows.buf[0:8, :], rows.buf[0:8, :]))
        def normalise(row, mr=mr, rows=rows, tail=tail):
            dst = (qT if row < HG else kT)[:, row % HG, :]
            bank = c.banks.take()
            PE.after(mr, *bank.free)
            m = PE.run(nc.tensor.matmul(bank.buf[:], c.const("ident")[:, row:row + 1].to_broadcast([P, P]),
                                        rows.buf[:], start=True, stop=True))
            V.after(m)
            m = V.run(nc.vector.scalar_tensor_tensor(out=dst, in0=dst, scalar=GD ** -0.5 if row < HG else 1.0,
                                                     in1=bank.buf[:], op0=ALU.mult, op1=ALU.mult))
            c.banks.give(bank, m)
            tail.append(m)
            if row < HG:
                return
            hh = row - HG
            yield
            tb, m = c.transpose_blocks([kT[:, hh, i * P:(i + 1) * P] for i in range(NT)], P, [m])
            m = c.copy(ktok[:, :, hh * P:(hh + 1) * P], tb.buf[:].rearrange("p (i d) -> p i d", i=NT), [m])
            c.banks.give(tb, m)
            tail.append(m)
        pipelined((normalise(row) for row in range(8)), 3)
        c.scratch.give(rows, PE.last())
        V.after(*tail)
        state_ready = [V.run(nc.vector.memset(state[:], 0.0))]
        st = {"ready": state_ready}

        def product(left, right, width=P, marks=()):
            bank = c.banks.take()
            PE.after(*bank.free, *marks)
            for hh in range(HG):
                mm = nc.tensor.matmul(bank.buf[:, hh * width:(hh + 1) * width], left(hh), right(hh),
                                      start=True, stop=True)
            return bank, PE.run(mm)

        def block(s, hh):
            return s.buf[:, hh * P:(hh + 1) * P]

        def tile(i, hg=hg, tail=tail, st=st):
            tok = slice(i * P, (i + 1) * P)
            hs = slice(hg * HG, (hg + 1) * HG)
            per_head = lambda a: a[:, i, hs].unsqueeze(2).to_broadcast([P, HG, P])
            over_heads = lambda a: a.unsqueeze(1).to_broadcast([P, HG, P])
            rb, m = product(lambda hh: g[:, i, hg * HG + hh:hg * HG + hh + 1].to_broadcast([P, P]),
                            lambda hh: c.const("chunk_upto"), marks=[*cols_ready, *tail])
            dec, erow = c.scratch.take(), c.scratch.take()
            V.after(m, *dec.free)
            for hh in range(HG):
                m = V.run(nc.vector.tensor_scalar(block(dec, hh), rb.buf[:, hh * P:(hh + 1) * P],
                                                  gcum[:, i, hg * HG + hh:hg * HG + hh + 1], 0.0,
                                                  ALU.subtract, ALU.min))
            A.after(m, *erow.free)
            m_e = A.run(nc.scalar.activation(erow.buf[:], rb.buf[:], ACT.Exp))
            c.banks.give(rb, m_e)
            m = A.run(nc.scalar.activation(dec.buf[:], dec.buf[:], ACT.Exp))
            G.after(m)
            m_dec = G.run(nc.gpsimd.tensor_tensor(g4(dec.buf[:]), g4(dec.buf[:]), over_heads(c.const("chunk_upto")), ALU.mult))
            yield
            gb, m1 = product(lambda hh: kT[:, hh, tok], lambda hh: kT[:, hh, tok], marks=tail)
            bb, m2 = product(lambda hh: beta[:, i, hg * HG + hh:hg * HG + hh + 1].to_broadcast([P, P]),
                             lambda hh: c.const("ident"))
            at_ = c.scratch.take()
            V.after(m1, m_dec, *at_.free)
            m = V.run(nc.vector.tensor_tensor(at_.buf[:], gb.buf[:], dec.buf[:], ALU.mult))
            c.banks.give(gb, m)
            V.after(m, m2)
            m_at = V.run(nc.vector.tensor_tensor(at_.buf[:], at_.buf[:], bb.buf[:], ALU.mult))
            c.banks.give(bb, m_at)
            qb, m3 = product(lambda hh: kT[:, hh, tok], lambda hh: qT[:, hh, tok])
            V.after(m3)
            m_attn = V.run(nc.vector.tensor_tensor(dec.buf[:], qb.buf[:], dec.buf[:], ALU.mult))
            attn = dec
            c.banks.give(qb, m_attn)
            kb, vb, q0, q1, kd = (c.scratch.take() for _ in range(5))
            G.after(m_e, *cols_ready, *tail, *kb.free, *vb.free, *q0.free, *q1.free, *kd.free)
            for n, s in enumerate((q0, q1)):
                mine, other = (slice(n * CHUNK, (n + 1) * CHUNK), slice((1 - n) * CHUNK, (2 - n) * CHUNK))
                t0 = i * P + n * CHUNK
                G.run(nc.gpsimd.tensor_tensor(g4(s.buf[:])[:, :, mine], qT[:, :, t0:t0 + CHUNK],
                                              g4(erow.buf[:])[:, :, mine], ALU.mult))
                m_q = G.run(nc.gpsimd.memset(g4(s.buf[:])[:, :, other], 0.0))
            G.run(nc.gpsimd.tensor_tensor(g4(kb.buf[:]), g4(ktok[:, i, :]), per_head(bexp), ALU.mult))
            m_kb = G.run(nc.gpsimd.tensor_tensor(g4(vb.buf[:]), g4(vtok[:, i, :]), per_head(beta), ALU.mult))
            ends = c.small.take()
            A.after(m_e, *ends.free)
            m_ends = A.run(nc.scalar.copy(ends.buf[:, 0:2 * HG].rearrange("p (h n) -> p h n", n=2),
                                          g4(erow.buf[:])[:, :, CHUNK - 1:P:CHUNK]))
            m_kd = G.run(nc.gpsimd.tensor_tensor(g4(kd.buf[:]), g4(ktok[:, i, :]), per_head(kdec1), ALU.mult))
            G.after(m_kd)
            m_k0 = G.run(nc.gpsimd.tensor_tensor(g4(ktok[:, i, :]), g4(ktok[:, i, :]), per_head(kdec0), ALU.mult))
            c.scratch.give(erow, m_ends, m_q)
            yield
            level = lambda l: over_heads(c.const("levels")[:, l * P:(l + 1) * P])
            xt, xn, am = c.scratch.take(), c.scratch.take(), c.scratch.take()
            V.after(m_at, *xt.free, *xn.free, *am.free)
            m = V.run(nc.vector.tensor_tensor(g4(am.buf[:]), g4(at_.buf[:]), level(0), ALU.mult))
            V.after(m)
            m = V.run(nc.vector.tensor_tensor(g4(xt.buf[:]), over_heads(c.const("ident")), g4(am.buf[:]), ALU.subtract))
            tb, mt = c.transpose_blocks([block(xt, hh) for hh in range(HG)], P, [m])
            m_x = c.copy(xn.buf[:], tb.buf[:], [mt], "act")
            c.banks.give(tb, m_x)
            m_xt, m_b = m, m
            yield
            for l in range(1, LEVELS):
                V.after(m_b)
                m = V.run(nc.vector.tensor_tensor(g4(am.buf[:]), g4(at_.buf[:]), level(l), ALU.mult))
                bk, m = product(lambda hh: block(am, hh), lambda hh: block(xn, hh), marks=[m, m_x])
                m = c.copy(am.buf[:], bk.buf[:], [m], "act")
                c.banks.give(bk, m)
                yield
                if l < LEVELS - 1:
                    b1, ma = product(lambda hh: block(xt, hh), lambda hh: block(am, hh), marks=[m, m_xt])
                b2, mb = product(lambda hh: block(am, hh), lambda hh: block(xt, hh), marks=[m, m_xt])
                m_b = mb
                if l < LEVELS - 1:
                    V.after(ma)
                    m_x = V.run(nc.vector.tensor_tensor(xn.buf[:], xn.buf[:], b1.buf[:], ALU.subtract))
                    c.banks.give(b1, m_x)
                V.after(mb)
                m_xt = V.run(nc.vector.tensor_tensor(xt.buf[:], xt.buf[:], b2.buf[:], ALU.subtract))
                c.banks.give(b2, m_xt)
                yield
            ub, m1 = product(lambda hh: block(xt, hh), lambda hh: block(vb, hh), marks=[m_xt, m_kb])
            wb, m2 = product(lambda hh: block(kb, hh), lambda hh: block(xt, hh))
            u, w = xn, am
            m_u = c.copy(u.buf[:], ub.buf[:], [m1, m_b], "act")
            m_w = c.copy(w.buf[:], wb.buf[:], [m2, m_b], "act")
            c.banks.give(ub, m_u)
            c.banks.give(wb, m_w)
            c.scratch.give(xt, m2)
            c.scratch.give(kb, m2)
            c.scratch.give(at_, m_xt)
            yield
            ob = c.banks.take()
            for cc, q_ in enumerate((q0, q1)):
                rows_ = slice(cc * CHUNK, (cc + 1) * CHUNK)
                nb = c.banks.take()
                PE.after(*nb.free, m_w, m_q, *st["ready"])
                for hh in range(HG):
                    mm = nc.tensor.matmul(nb.buf[rows_, hh * P:(hh + 1) * P],
                                          w.buf[:, hh * P + cc * CHUNK:hh * P + (cc + 1) * CHUNK],
                                          state[:, hh, :], start=True, stop=True)
                m = PE.run(mm)
                V.after(m, m_u)
                m_v = V.run(nc.vector.tensor_tensor(u.buf[rows_, :], u.buf[rows_, :], nb.buf[rows_, :], ALU.subtract))
                c.banks.give(nb, m_v)
                if cc == 0:
                    PE.after(*ob.free)
                for hh in range(HG):
                    mm = nc.tensor.matmul(ob.buf[:, hh * P:(hh + 1) * P], state[:, hh, :], block(q_, hh),
                                          start=cc == 0 and hh == 0, stop=False, skip_group_check=True)
                m_o = PE.run(mm)
                sb_ = c.banks.take()
                PE.after(*sb_.free, m_v, m_k0)
                for hh in range(HG):
                    keys = ktok[:, i, hh * P:(hh + 1) * P] if cc == 0 else block(kd, hh)
                    mm = nc.tensor.matmul(sb_.buf[:, hh * P:(hh + 1) * P], keys, block(u, hh), start=True, stop=True)
                m_s = PE.run(mm)
                V.after(m_s, m_o, m_ends)
                for hh in range(HG):
                    m = V.run(nc.vector.scalar_tensor_tensor(
                        out=state[:, hh, :], in0=state[:, hh, :], scalar=ends.buf[:, 2 * hh + cc:2 * hh + cc + 1],
                        in1=sb_.buf[:, hh * P:(hh + 1) * P], op0=ALU.mult, op1=ALU.add))
                c.banks.give(sb_, m)
                st["ready"] = [m]
                yield
            PE.after(m_v, m_attn)
            for hh in range(HG):
                mm = nc.tensor.matmul(ob.buf[:, hh * P:(hh + 1) * P], block(u, hh), block(attn, hh),
                                      start=False, stop=True, skip_group_check=True)
            m_o = PE.run(mm)
            m = c.copy(c.mixed[:, hg * HG:(hg + 1) * HG, tok], g4(ob.buf[:]), [m_o], "act")
            c.banks.give(ob, m)
            c.mixed_ready.append(m)
            c.small.give(ends, V.last())
            for s in (dec, q0, q1, vb, kd, xn, am):
                c.scratch.give(s, m_o, m_k0)
        pipelined((tile(i) for i in range(NT)), 2, every=3)
        c.scratch.slots = [s for s in c.scratch.slots if s in c.own_scratch]
        c.close_area()

    sums = c.banks.take()
    for n in range(H):
        sq, m = c.square_tile(c.mixed[:, n, :], c.mixed_ready)
        PE.after(m, *sums.free)
        m = PE.run(nc.tensor.matmul(sums.buf[0:8, :], c.const("strip")[:, 15 - n:23 - n], sq.buf[:],
                                    start=n == 0, stop=n == H - 1))
        c.scratch.give(sq, m)
    rows = c.scratch.take()
    V.after(*rows.free)
    A.after(m, V.run(nc.vector.memset(rows.buf[:], 0.0)))
    m = A.run(nc.scalar.activation(rows.buf[0:8, :], sums.buf[0:8, :], ACT.Sqrt, bias=c.eps[0:8, 0:1], scale=1.0 / GD))
    c.banks.give(sums, m)
    V.after(m)
    mr = V.run(nc.vector.reciprocal(rows.buf[0:8, :], rows.buf[0:8, :]))
    done = []
    c.open_area()
    c.split_area(3)

    def gated(h_):
        w = c.split_weights(w_in, (3 * H + h_) * P)
        yield
        zb, m = c.split_product(w, h, KD, c.h_ready)
        bank = c.banks.take()
        PE.after(mr, *bank.free)
        m1 = PE.run(nc.tensor.matmul(bank.buf[:], c.const("ident")[:, h_:h_ + 1].to_broadcast([P, P]),
                                     rows.buf[:], start=True, stop=True))
        yield
        z = c.scratch.take()
        A.after(m, *z.free)
        m = A.run(nc.scalar.activation(z.buf[:], zb.buf[:], ACT.Silu))
        c.banks.give(zb, m)
        o = c.mixed[:, h_, :]
        V.after(m1)
        m1 = V.run(nc.vector.scalar_tensor_tensor(out=o, in0=o, scalar=c.col["gdn_norm"], in1=bank.buf[:],
                                                  op0=ALU.mult, op1=ALU.mult))
        c.banks.give(bank, m1)
        V.after(m, m1)
        m = V.run(nc.vector.tensor_tensor(o, o, z.buf[:], ALU.mult))
        c.scratch.give(z, m)
        done.append(m)
    pipelined((gated(h_) for h_ in range(H)), 3)
    c.scratch.give(rows, PE.last())
    c.mixed_ready = done
    c.close_area()
    c.close_area()


def build(nc, io, at, out):
    with ExitStack() as ctx:
        c = Core(nc, ctx, io, at)
        c.own_scratch = list(c.scratch.slots)
        dram = lambda name, shape: nc.dram_tensor(name, shape, F32).ap()
        c.h2_dram, c.y_dram = dram("h2_dram", [S, D]), dram("y_dram", [NBLK * P, D])
        setup(c)
        c.mixed_ready = []
        c.norm_residual(lambda k: columns(c.col["norm_attn"], k))
        setup_tables(c)
        c.open_scores_area()
        c.later.append(c.modulation(0))
        dilated(c)
        mla(c)
        c.close_scores_area()
        merge(c)
        router = c.router_chunk()
        c.norm_residual(lambda k: columns(c.col["norm_ffn"], k))
        moe(c, router)
        c.finish_background()
        c.DVE.after(c.mod_ready)
        c.ACT.after(c.mod_ready)
        mod = lambda layer, part: (lambda k: c.mod[:, layer, part, k:k + 1])
        c.norm_residual(mod(0, 1), mod(0, 0))
        c.later.append(c.modulation(1))
        head_groups(c)
        project_mixed(c, io["attn_w_out_2"], mod(0, 2))
        c.close_area()
        swiglu(c, 0, mod(0, 4), mod(0, 3))
        c.finish_background()
        c.DVE.after(c.mod_ready)
        c.ACT.after(c.mod_ready)
        c.open_area()
        c.mixed = c.sb("mixed", [P, KD, S])
        delta_net(c, mod(1, 1), mod(1, 0))
        project_mixed(c, io["gdn_w_out_2"], mod(1, 2))
        c.close_area()
        swiglu(c, 1, mod(1, 4), mod(1, 3))
        c.open_area()
        c.hT = c.sb("result", [P, KD, S])
        c.norm_residual(lambda k: columns(c.col["final"], k))
        sem = c.sem("out_done")
        for k in range(KD):
            c.SP.after(c.h_ready[k])
            nc.sync.dma_start(out[k * P:(k + 1) * P, :], c.hT[:, k, :]).then_inc(sem, 16)
        c.areas.pop().close()
        nc.sync.wait_ge(sem, 16 * KD)


def kernel(**inputs):
    import concourse.bacc as bacc
    from concourse.bass_utils import run_bass_kernel_spmd

    a = {k: np.asarray(v) for k, v in inputs.items()}
    table, at = constants()
    cols = lambda v: np.ascontiguousarray(v.reshape(-1, P).T)
    twice = lambda v: np.ascontiguousarray(np.concatenate([v, v], -1).T)
    column = {
        "norm_attn": cols(a["norm_attn"]), "norm_ffn": cols(a["norm_ffn"]), "b_gate": cols(a["b_gate"]),
        "norm_ckv": cols(a["norm_ckv"]), "norm_mix": cols(a["norm_mix_g_2"]), "norm_ffn2": cols(a["norm_ffn_g_2"]),
        "final": cols(a["final_norm_g_2"]), "c": cols(a["c_2"]), "gdn_norm": cols(a["gdn_norm_g_2"]),
        "qdil": twice(a["q_norm_dil"][0]), "kdil": twice(a["k_norm_dil"][0]),
        "ada_b": cols(a["ada_b_2"]), "conv": cols(a["gdn_conv_w_2"]),
    }
    row = {"qmla": a["q_norm_mla"][0], "kmla": a["k_norm_mla"][0], "b_rg": a["b_router_group"][0],
           "b_re": a["b_router_expert"][0], "a_log": a["gdn_a_log_2"][0], "dt_bias": a["gdn_dt_bias_2"][0]}
    arrays = {
        "consts": table,
        "xT": np.ascontiguousarray(a["x"][0].T),
        "cols": np.ascontiguousarray(np.concatenate([column[name] for name in COLS], 1)),
        "rows": np.ascontiguousarray(np.concatenate([row[name] for name in ROWS])),
        "positions": np.ascontiguousarray(np.concatenate([a["positions"].reshape(NT, P).T,
                                                          a["positions_2"].reshape(NT, P).T], 1)),
    }
    for name in ("w_in", "w_ukv", "w_o_mla", "w_o_dil", "w_out", "w_router_group", "w_router_expert", "w_gate",
                 "w_up", "w_down", "attn_w_in_2", "attn_w_out_2", "gdn_w_in_2", "gdn_w_out_2"):
        arrays[name] = a[name][0]
    for name in ("ada_w_2", "ffn_w_in_2", "ffn_w_out_2"):
        arrays[name] = a[name]
    nc = bacc.Bacc("TRN2", target_bir_lowering=False, num_devices=1)
    io = {n: nc.dram_tensor(n, v.shape, mybir.dt.from_np(v.dtype), kind="ExternalInput").ap()
          for n, v in arrays.items()}
    out = nc.dram_tensor("outT", [D, S], F32, kind="ExternalOutput").ap()
    build(nc, io, at, out)
    got = run_bass_kernel_spmd(nc, [arrays], core_ids=[0]).results[0]["outT"]
    return np.ascontiguousarray(got.T).reshape(1, S, D)
```
